# Optimizing a Trainium2 kernel written in Bass

```python
import math
import jax
import jax.numpy as jnp
from jax import lax
import numpy as np
import jax, jax.numpy as jnp

D_MODEL = 1024
BATCH = 1
SEQ = 512
DEPTH = 1

CHUNK = 64
EPS = 1e-6
NEG_INF = -1e30
ATT_HEADS = 8
ATT_HEAD_DIM = 64
ATT_WIDTH = ATT_HEADS * ATT_HEAD_DIM
LEFT_CHUNKS = 8
BAND_CHUNKS = LEFT_CHUNKS + 1
BAND = BAND_CHUNKS * CHUNK
REL_MAX = 128
REL_BUCKETS = (CHUNK - 1) + REL_MAX + 1
SSM_WIDTH = D_MODEL - ATT_WIDTH
SSM_GROUP = 16
SSM_GROUPS = SSM_WIDTH // SSM_GROUP
SSM_STATE = 64
MIX_WIDTH = ATT_WIDTH + SSM_WIDTH
IN_WIDTH = 3 * ATT_WIDTH + SSM_WIDTH
MEM_LEN = 256
MEM_HEADS = 4
MEM_HEAD_DIM = D_MODEL // MEM_HEADS
PEER_HEADS = 8
PEER_KEYS = 128
PEER_EXPERTS = PEER_KEYS * PEER_KEYS
PEER_TOPK = 16
PEER_QDIM = 256
PEER_BLOCK = 128


def _rmsnorm(x, g):
    xf = x.astype(jnp.float32)
    y = xf * lax.rsqrt(jnp.mean(xf * xf, axis=-1, keepdims=True) + EPS)
    return (y * g.astype(jnp.float32)).astype(x.dtype)

def _band_bias(rel_bias):
    qi = jnp.arange(CHUNK)
    kj = jnp.arange(BAND)
    dist = LEFT_CHUNKS * CHUNK + qi[:, None] - kj[None, :]
    bucket = jnp.clip(dist, -(CHUNK - 1), REL_MAX) + (CHUNK - 1)
    return rel_bias[:, bucket]

def _chunked_attention(q, k, v, rel_bias):
    bsz, seq = q.shape[0], q.shape[1]
    nc = seq // CHUNK
    shp = (bsz, nc, CHUNK, ATT_HEADS, ATT_HEAD_DIM)
    qc = q.reshape(shp)
    pad = ((0, 0), (LEFT_CHUNKS, 0), (0, 0), (0, 0), (0, 0))
    kp = jnp.pad(k.reshape(shp), pad)
    vp = jnp.pad(v.reshape(shp), pad)
    idx = jnp.arange(nc)[:, None] + jnp.arange(BAND_CHUNKS)[None, :]
    band_shp = (bsz, nc, BAND, ATT_HEADS, ATT_HEAD_DIM)
    kb = kp[:, idx].reshape(band_shp)
    vb = vp[:, idx].reshape(band_shp)
    s = jnp.einsum('bnqhd,bnkhd->bhnqk', qc, kb).astype(jnp.float32) * (ATT_HEAD_DIM ** -0.5)
    s = s + _band_bias(rel_bias).astype(jnp.float32)[None, :, None]
    key_chunk = jnp.arange(nc)[:, None] - LEFT_CHUNKS + (jnp.arange(BAND) // CHUNK)[None, :]
    s = jnp.where((key_chunk >= 0)[None, None, :, None, :], s, NEG_INF)
    p = jax.nn.softmax(s, axis=-1).astype(v.dtype)
    o = jnp.einsum('bhnqk,bnkhd->bnqhd', p, vb)
    return o.reshape(bsz, seq, ATT_WIDTH)

def _complex_affine_combine(c1, c2):
    a1r, a1i, b1r, b1i = c1
    a2r, a2i, b2r, b2i = c2
    ar = a2r * a1r - a2i * a1i
    ai = a2r * a1i + a2i * a1r
    br = a2r * b1r - a2i * b1i + b2r
    bi = a2r * b1i + a2i * b1r + b2i
    return (ar, ai, br, bi)

def _s5_mixer(u, lam_re, lam_im, log_step, b_re, b_im, c_re, c_im, d_skip, w_glu, b_glu):
    bsz, seq = u.shape[0], u.shape[1]
    uf = u.astype(jnp.float32).reshape(bsz, seq, SSM_GROUPS, SSM_GROUP)
    step = jnp.exp(log_step.astype(jnp.float32))[:, None]
    lr = lam_re.astype(jnp.float32)
    li = lam_im.astype(jnp.float32)
    mag = jnp.exp(lr * step)
    ar = mag * jnp.cos(li * step)
    ai = mag * jnp.sin(li * step)
    zr = ar - 1.0
    den = lr * lr + li * li
    fr = (zr * lr + ai * li) / den
    fi = (ai * lr - zr * li) / den
    br = b_re.astype(jnp.float32)
    bi = b_im.astype(jnp.float32)
    bbr = fr[..., None] * br - fi[..., None] * bi
    bbi = fr[..., None] * bi + fi[..., None] * br
    bu_r = jnp.einsum('blgc,gpc->blgp', uf, bbr)
    bu_i = jnp.einsum('blgc,gpc->blgp', uf, bbi)
    a_r = jnp.broadcast_to(ar, bu_r.shape)
    a_i = jnp.broadcast_to(ai, bu_i.shape)
    _, _, xr, xi = lax.associative_scan(_complex_affine_combine, (a_r, a_i, bu_r, bu_i), axis=1)
    y = (jnp.einsum('blgp,gcp->blgc', xr, c_re.astype(jnp.float32))
         - jnp.einsum('blgp,gcp->blgc', xi, c_im.astype(jnp.float32))
         + d_skip.astype(jnp.float32) * uf)
    y = jax.nn.gelu(y.reshape(bsz, seq, SSM_WIDTH), approximate=False)
    y = y * jax.nn.sigmoid(y @ w_glu.astype(jnp.float32) + b_glu.astype(jnp.float32))
    return y.astype(u.dtype)

def _memory_attention(hn, memn, w_q, w_k, w_v, q_g, k_g, w_o):
    bsz, seq = hn.shape[0], hn.shape[1]
    m = memn.shape[1]
    q = _rmsnorm((hn @ w_q).reshape(bsz, seq, MEM_HEADS, MEM_HEAD_DIM), q_g)
    k = _rmsnorm((memn @ w_k).reshape(bsz, m, MEM_HEADS, MEM_HEAD_DIM), k_g)
    v = (memn @ w_v).reshape(bsz, m, MEM_HEADS, MEM_HEAD_DIM)
    s = jnp.einsum('blhd,bmhd->bhlm', q, k).astype(jnp.float32) * (MEM_HEAD_DIM ** -0.5)
    p = jax.nn.softmax(s, axis=-1).astype(v.dtype)
    o = jnp.einsum('bhlm,bmhd->blhd', p, v).reshape(bsz, seq, D_MODEL)
    return o @ w_o

def _peer_ffn(hn, w_q, sub_keys, u_tab, v_tab):
    bsz, seq, d = hn.shape
    tokens = hn.reshape(-1, PEER_BLOCK, d)

    def block(xb):
        q = (xb @ w_q).reshape(PEER_BLOCK, PEER_HEADS, 2, PEER_QDIM // 2)
        s = jnp.einsum('thsd,hsnd->thsn', q, sub_keys).astype(jnp.float32)
        sv, si = lax.top_k(s, PEER_TOPK)
        cand = (sv[:, :, 0, :, None] + sv[:, :, 1, None, :]).reshape(PEER_BLOCK, PEER_HEADS, -1)
        cidx = (si[:, :, 0, :, None] * PEER_KEYS + si[:, :, 1, None, :]).reshape(PEER_BLOCK, PEER_HEADS, -1)
        top, pos = lax.top_k(cand, PEER_TOPK)
        e = jnp.take_along_axis(cidx, pos, axis=-1)
        g = jax.nn.softmax(top, axis=-1)
        act = jax.nn.gelu(jnp.einsum('thkd,td->thk', u_tab[e], xb), approximate=False)
        w = (g * act).astype(xb.dtype)
        return jnp.einsum('thk,thkd->td', w, v_tab[e])

    return lax.map(block, tokens).reshape(bsz, seq, d)

def first_inputs(seed: int = 0) -> dict:
    key = jax.random.key(seed)
    ks = iter(jax.random.split(key, 40))

    def nrm(shape, scale):
        return scale * jax.random.normal(next(ks), shape, jnp.float32)

    def gain(n):
        return 1.0 + nrm((DEPTH, n), 0.02)

    x = nrm((BATCH, SEQ, D_MODEL), 1.0)
    mem = nrm((BATCH, MEM_LEN, D_MODEL), 1.0)
    norm_mix_g = gain(D_MODEL)
    w_in = nrm((DEPTH, D_MODEL, IN_WIDTH), D_MODEL ** -0.5)
    att_q_g = gain(ATT_HEAD_DIM)
    att_k_g = gain(ATT_HEAD_DIM)
    rel_bias = nrm((DEPTH, ATT_HEADS, REL_BUCKETS), 0.5)
    ssm_lam_re = -0.5 + nrm((DEPTH, SSM_GROUPS, SSM_STATE), 0.01)
    ssm_lam_im = math.pi * jnp.arange(SSM_STATE, dtype=jnp.float32) + nrm((DEPTH, SSM_GROUPS, SSM_STATE), 0.01)
    ssm_log_step = jax.random.uniform(next(ks), (DEPTH, SSM_GROUPS), jnp.float32, math.log(1e-3), math.log(1e-1))
    ssm_b_re = nrm((DEPTH, SSM_GROUPS, SSM_STATE, SSM_GROUP), (2 * SSM_GROUP) ** -0.5)
    ssm_b_im = nrm((DEPTH, SSM_GROUPS, SSM_STATE, SSM_GROUP), (2 * SSM_GROUP) ** -0.5)
    ssm_c_re = nrm((DEPTH, SSM_GROUPS, SSM_GROUP, SSM_STATE), (2 * SSM_STATE) ** -0.5)
    ssm_c_im = nrm((DEPTH, SSM_GROUPS, SSM_GROUP, SSM_STATE), (2 * SSM_STATE) ** -0.5)
    ssm_d = nrm((DEPTH, SSM_GROUPS, SSM_GROUP), 1.0)
    ssm_w_glu = nrm((DEPTH, SSM_WIDTH, SSM_WIDTH), SSM_WIDTH ** -0.5)
    ssm_b_glu = nrm((DEPTH, SSM_WIDTH), 0.01)
    att_out_g = gain(ATT_WIDTH)
    ssm_out_g = gain(SSM_WIDTH)
    w_out = nrm((DEPTH, MIX_WIDTH, D_MODEL), MIX_WIDTH ** -0.5)
    norm_mem_g = gain(D_MODEL)
    norm_memkv_g = gain(D_MODEL)
    w_mem_q = nrm((DEPTH, D_MODEL, D_MODEL), D_MODEL ** -0.5)
    w_mem_k = nrm((DEPTH, D_MODEL, D_MODEL), D_MODEL ** -0.5)
    w_mem_v = nrm((DEPTH, D_MODEL, D_MODEL), D_MODEL ** -0.5)
    mem_q_g = gain(MEM_HEAD_DIM)
    mem_k_g = gain(MEM_HEAD_DIM)
    w_mem_o = nrm((DEPTH, D_MODEL, D_MODEL), D_MODEL ** -0.5)
    norm_peer_g = gain(D_MODEL)
    w_peer_q = nrm((DEPTH, D_MODEL, PEER_HEADS * PEER_QDIM), D_MODEL ** -0.5)
    peer_keys = nrm((DEPTH, PEER_HEADS, 2, PEER_KEYS, PEER_QDIM // 2), (PEER_QDIM // 2) ** -0.5)
    peer_u = nrm((DEPTH, PEER_EXPERTS, D_MODEL), D_MODEL ** -0.5)
    peer_v = nrm((DEPTH, PEER_EXPERTS, D_MODEL), PEER_HEADS ** -0.5)
    return {'x': x, 'mem': mem, 'norm_mix_g': norm_mix_g, 'w_in': w_in,
            'att_q_g': att_q_g, 'att_k_g': att_k_g, 'rel_bias': rel_bias,
            'ssm_lam_re': ssm_lam_re, 'ssm_lam_im': ssm_lam_im, 'ssm_log_step': ssm_log_step,
            'ssm_b_re': ssm_b_re, 'ssm_b_im': ssm_b_im, 'ssm_c_re': ssm_c_re, 'ssm_c_im': ssm_c_im,
            'ssm_d': ssm_d, 'ssm_w_glu': ssm_w_glu, 'ssm_b_glu': ssm_b_glu,
            'att_out_g': att_out_g, 'ssm_out_g': ssm_out_g, 'w_out': w_out,
            'norm_mem_g': norm_mem_g, 'norm_memkv_g': norm_memkv_g,
            'w_mem_q': w_mem_q, 'w_mem_k': w_mem_k, 'w_mem_v': w_mem_v,
            'mem_q_g': mem_q_g, 'mem_k_g': mem_k_g, 'w_mem_o': w_mem_o,
            'norm_peer_g': norm_peer_g, 'w_peer_q': w_peer_q, 'peer_keys': peer_keys,
            'peer_u': peer_u, 'peer_v': peer_v}

def first_block(x, mem, norm_mix_g, w_in, att_q_g, att_k_g, rel_bias,
              ssm_lam_re, ssm_lam_im, ssm_log_step, ssm_b_re, ssm_b_im, ssm_c_re, ssm_c_im,
              ssm_d, ssm_w_glu, ssm_b_glu, att_out_g, ssm_out_g, w_out,
              norm_mem_g, norm_memkv_g, w_mem_q, w_mem_k, w_mem_v, mem_q_g, mem_k_g, w_mem_o,
              norm_peer_g, w_peer_q, peer_keys, peer_u, peer_v):
    bsz, seq = x.shape[0], x.shape[1]
    h = x
    for l in range(DEPTH):
        proj = _rmsnorm(h, norm_mix_g[l]) @ w_in[l]
        q = proj[..., :ATT_WIDTH].reshape(bsz, seq, ATT_HEADS, ATT_HEAD_DIM)
        k = proj[..., ATT_WIDTH:2 * ATT_WIDTH].reshape(bsz, seq, ATT_HEADS, ATT_HEAD_DIM)
        v = proj[..., 2 * ATT_WIDTH:3 * ATT_WIDTH].reshape(bsz, seq, ATT_HEADS, ATT_HEAD_DIM)
        u = proj[..., 3 * ATT_WIDTH:]
        att = _chunked_attention(_rmsnorm(q, att_q_g[l]), _rmsnorm(k, att_k_g[l]), v, rel_bias[l])
        ssm = _s5_mixer(u, ssm_lam_re[l], ssm_lam_im[l], ssm_log_step[l], ssm_b_re[l], ssm_b_im[l],
                        ssm_c_re[l], ssm_c_im[l], ssm_d[l], ssm_w_glu[l], ssm_b_glu[l])
        mixed = jnp.concatenate([_rmsnorm(att, att_out_g[l]), _rmsnorm(ssm, ssm_out_g[l])], axis=-1)
        h = h + mixed @ w_out[l]
        h = h + _memory_attention(_rmsnorm(h, norm_mem_g[l]), _rmsnorm(mem, norm_memkv_g[l]),
                                  w_mem_q[l], w_mem_k[l], w_mem_v[l], mem_q_g[l], mem_k_g[l], w_mem_o[l])
        h = h + _peer_ffn(_rmsnorm(h, norm_peer_g[l]), w_peer_q[l], peer_keys[l], peer_u[l], peer_v[l])
    return h


DEPTH_2 = 2

SSD_HEAD_DIM = 64
SSD_INNER = D_MODEL
SSD_HEADS = SSD_INNER // SSD_HEAD_DIM
SSD_GROUPS = 2
SSD_STATE = 128
SSD_CONV = 4
SSD_CHUNK = 128
SSD_XBC = SSD_INNER + 2 * SSD_GROUPS * SSD_STATE
MLA_HEADS = D_MODEL // 128
MLA_NOPE = 128
MLA_ROPE = 64
MLA_V = 128
MLA_Q_LORA = D_MODEL // 2
MLA_KV_LORA = D_MODEL // 4
MLA_QBLOCK = 128
ROPE_THETA = 10000.0
GDN_HEAD_K = 128
GDN_HEAD_V = 128
GDN_V_HEADS = D_MODEL // GDN_HEAD_V
GDN_QK_HEADS = GDN_V_HEADS // 2
GDN_CONV = 4
GDN_CHUNK = 64
GDN_QK = GDN_QK_HEADS * GDN_HEAD_K
GDN_VW = GDN_V_HEADS * GDN_HEAD_V
GDN_QKV = 2 * GDN_QK + GDN_VW
N_BRANCH = 3
D_FF = 4 * D_MODEL
IN_SIZES = (SSD_INNER, SSD_XBC, SSD_HEADS, MLA_Q_LORA, MLA_KV_LORA, MLA_ROPE,
            GDN_QKV, GDN_VW, GDN_V_HEADS, GDN_V_HEADS, N_BRANCH * D_MODEL)
N_IN = (SSD_INNER + SSD_XBC + SSD_HEADS + MLA_Q_LORA + MLA_KV_LORA + MLA_ROPE
        + GDN_QKV + GDN_VW + 2 * GDN_V_HEADS + N_BRANCH * D_MODEL)


def rmsnorm(x, g):
    xf = x.astype(jnp.float32)
    y = xf * lax.rsqrt(jnp.mean(xf * xf, axis=-1, keepdims=True) + EPS)
    return (y * g.astype(jnp.float32)).astype(x.dtype)

def l2norm(x):
    xf = x.astype(jnp.float32)
    return xf * lax.rsqrt(jnp.sum(xf * xf, axis=-1, keepdims=True) + EPS)

def causal_dwconv(x, w):
    K, C = w.shape
    return lax.conv_general_dilated(
        x, w[:, None, :].astype(x.dtype), window_strides=(1,), padding=[(K - 1, 0)],
        dimension_numbers=('NWC', 'WIO', 'NWC'), feature_group_count=C)

def rope_tables(positions):
    inv = ROPE_THETA ** (-jnp.arange(0, MLA_ROPE, 2, dtype=jnp.float32) / MLA_ROPE)
    ang = positions.astype(jnp.float32)[..., None] * inv
    return jnp.cos(ang), jnp.sin(ang)

def apply_rope(t, cos, sin):
    half = t.shape[-1] // 2
    tf = t.astype(jnp.float32)
    t1, t2 = tf[..., :half], tf[..., half:]
    return jnp.concatenate([t1 * cos - t2 * sin, t2 * cos + t1 * sin], axis=-1).astype(t.dtype)

def ssd_chunked(X, dA, Bm, Cm):
    b, s, g, e, p = X.shape
    n = Bm.shape[-1]
    Q = SSD_CHUNK
    c = s // Q
    X = X.reshape(b, c, Q, g, e, p)
    Bc = Bm.reshape(b, c, Q, g, n)
    Cc = Cm.reshape(b, c, Q, g, n)
    A = jnp.transpose(dA.reshape(b, c, Q, g, e), (0, 3, 4, 1, 2))
    A_cum = jnp.cumsum(A, axis=-1)
    tril = jnp.tril(jnp.ones((Q, Q), dtype=bool))
    L = jnp.exp(jnp.where(tril, A_cum[..., :, None] - A_cum[..., None, :], -jnp.inf))
    CB = jnp.einsum('bclgn,bcsgn->bcgls', Cc, Bc)
    y_diag = jnp.einsum('bcgls,bgecls,bcsgep->bclgep', CB, L, X)
    decay_states = jnp.exp(A_cum[..., -1:] - A_cum)
    states = jnp.einsum('bclgn,bgecl,bclgep->bcgepn', Bc, decay_states, X)
    chunk_decay = jnp.exp(A_cum[..., -1])

    def step(h, inp):
        st, dec = inp
        return h * dec[..., None, None] + st, h

    _, h_prev = lax.scan(step, jnp.zeros_like(states[:, 0]),
                         (jnp.moveaxis(states, 1, 0), jnp.moveaxis(chunk_decay, -1, 0)))
    h_prev = jnp.moveaxis(h_prev, 0, 1)
    y_off = jnp.einsum('bclgn,bcgepn,bgecl->bclgep', Cc, h_prev, jnp.exp(A_cum))
    return (y_diag + y_off).reshape(b, s, g, e, p)

def ssd_mixer(z, xbc, dt_raw, conv_w, conv_b, dt_bias, a_log, d_skip, norm_g):
    Bsz, S, _ = z.shape
    G, E, P, N = SSD_GROUPS, SSD_HEADS // SSD_GROUPS, SSD_HEAD_DIM, SSD_STATE
    xbc = jax.nn.silu(causal_dwconv(xbc, conv_w) + conv_b.astype(xbc.dtype))
    xs, bm, cm = jnp.split(xbc, [SSD_INNER, SSD_INNER + G * N], axis=-1)
    xs = xs.astype(jnp.float32).reshape(Bsz, S, G, E, P)
    bm = bm.astype(jnp.float32).reshape(Bsz, S, G, N)
    cm = cm.astype(jnp.float32).reshape(Bsz, S, G, N)
    dt = jax.nn.softplus(dt_raw.astype(jnp.float32) + dt_bias.astype(jnp.float32)).reshape(Bsz, S, G, E)
    a = -jnp.exp(a_log.astype(jnp.float32)).reshape(G, E)
    y = ssd_chunked(xs * dt[..., None], dt * a, bm, cm)
    y = y + d_skip.astype(jnp.float32).reshape(G, E)[:, :, None] * xs
    y = y.reshape(Bsz, S, SSD_INNER) * jax.nn.silu(z.astype(jnp.float32))
    y = rmsnorm(y.reshape(Bsz, S, G, SSD_INNER // G), norm_g.reshape(G, SSD_INNER // G))
    return y.reshape(Bsz, S, SSD_INNER).astype(z.dtype)

def mla_mixer(cq, ckv, k_rope, cos, sin, q_norm_g, w_uq, kv_norm_g, w_ukv):
    Bsz, S, _ = cq.shape
    H = MLA_HEADS
    q = (rmsnorm(cq, q_norm_g) @ w_uq).reshape(Bsz, S, H, MLA_NOPE + MLA_ROPE)
    q_nope, q_pe = jnp.split(q, [MLA_NOPE], axis=-1)
    q_pe = apply_rope(q_pe, cos[:, :, None, :], sin[:, :, None, :])
    kv = (rmsnorm(ckv, kv_norm_g) @ w_ukv).reshape(Bsz, S, H, MLA_NOPE + MLA_V)
    k_nope, v = jnp.split(kv, [MLA_NOPE], axis=-1)
    k_pe = apply_rope(k_rope, cos, sin)
    nblk = S // MLA_QBLOCK
    scale = (MLA_NOPE + MLA_ROPE) ** -0.5
    kpos = jnp.arange(S)

    def to_blocks(t):
        return jnp.moveaxis(t.reshape((Bsz, nblk, MLA_QBLOCK) + t.shape[2:]), 1, 0)

    def attend(args):
        qn, qp, blk = args
        sc = (jnp.einsum('bqhd,bkhd->bhqk', qn, k_nope, preferred_element_type=jnp.float32)
              + jnp.einsum('bqhr,bkr->bhqk', qp, k_pe, preferred_element_type=jnp.float32))
        qpos = blk * MLA_QBLOCK + jnp.arange(MLA_QBLOCK)
        sc = jnp.where(kpos[None, :] <= qpos[:, None], sc * scale, -jnp.inf)
        pr = jax.nn.softmax(sc, axis=-1)
        return jnp.einsum('bhqk,bkhd->bqhd', pr.astype(v.dtype), v)

    o = lax.map(attend, (to_blocks(q_nope), to_blocks(q_pe), jnp.arange(nblk)))
    return jnp.moveaxis(o, 0, 1).reshape(Bsz, S, H * MLA_V)

def gated_delta_chunked(q, k, v, g, beta):
    Bsz, S, H, DK = k.shape
    DV = v.shape[-1]
    L = GDN_CHUNK
    C = S // L

    def chunks(t):
        return jnp.moveaxis(t.reshape((Bsz, C, L, H) + t.shape[3:]), 3, 1)

    q = chunks(q * (DK ** -0.5))
    k = chunks(k)
    v = chunks(v)
    g = jnp.cumsum(chunks(g), axis=-1)
    beta = chunks(beta)
    incl = jnp.tril(jnp.ones((L, L), dtype=bool))
    strict = jnp.tril(jnp.ones((L, L), dtype=bool), -1)
    decay = jnp.exp(jnp.where(incl, g[..., :, None] - g[..., None, :], -jnp.inf))
    kb = k * beta[..., None]
    a_mat = jnp.where(strict, jnp.einsum('bhcld,bhcmd->bhclm', kb, k) * decay, 0.0)
    rhs = jnp.concatenate([v * beta[..., None], kb * jnp.exp(g)[..., None]], axis=-1)
    sol = lax.linalg.triangular_solve(a_mat + jnp.eye(L, dtype=jnp.float32), rhs,
                                      left_side=True, lower=True)
    u, w = jnp.split(sol, [DV], axis=-1)
    qk = jnp.where(incl, jnp.einsum('bhcld,bhcmd->bhclm', q, k) * decay, 0.0)

    def step(state, inp):
        qc, kc, uc, wc, gc, ac = inp
        v_new = uc - jnp.einsum('bhld,bhdv->bhlv', wc, state)
        o = (jnp.einsum('bhld,bhdv->bhlv', qc * jnp.exp(gc)[..., None], state)
             + jnp.einsum('bhlm,bhmv->bhlv', ac, v_new))
        g_last = gc[..., -1:]
        state = (state * jnp.exp(g_last)[..., None]
                 + jnp.einsum('bhld,bhlv->bhdv', kc * jnp.exp(g_last - gc)[..., None], v_new))
        return state, o

    xs = tuple(jnp.moveaxis(t, 2, 0) for t in (q, k, u, w, g, qk))
    _, o = lax.scan(step, jnp.zeros((Bsz, H, DK, DV), jnp.float32), xs)
    return jnp.transpose(o, (1, 0, 3, 2, 4)).reshape(Bsz, S, H, DV)

def gdn_mixer(qkv, z, b_raw, a_raw, conv_w, dt_bias, a_log, norm_g):
    Bsz, S, _ = qkv.shape
    qkv = jax.nn.silu(causal_dwconv(qkv, conv_w))
    q, k, v = jnp.split(qkv, [GDN_QK, 2 * GDN_QK], axis=-1)
    rep = GDN_V_HEADS // GDN_QK_HEADS
    q = jnp.repeat(l2norm(q.reshape(Bsz, S, GDN_QK_HEADS, GDN_HEAD_K)), rep, axis=2)
    k = jnp.repeat(l2norm(k.reshape(Bsz, S, GDN_QK_HEADS, GDN_HEAD_K)), rep, axis=2)
    v = v.reshape(Bsz, S, GDN_V_HEADS, GDN_HEAD_V).astype(jnp.float32)
    beta = jax.nn.sigmoid(b_raw.astype(jnp.float32))
    g = -jnp.exp(a_log.astype(jnp.float32)) * jax.nn.softplus(a_raw.astype(jnp.float32) + dt_bias.astype(jnp.float32))
    o = gated_delta_chunked(q, k, v, g, beta)
    o = rmsnorm(o, norm_g) * jax.nn.silu(z.astype(jnp.float32).reshape(Bsz, S, GDN_V_HEADS, GDN_HEAD_V))
    return o.reshape(Bsz, S, GDN_VW).astype(z.dtype)

def hybrid_layer(x, cos, sin, norm1_g, w_in, ssd_conv_w, ssd_conv_b, ssd_dt_bias, ssd_a_log, ssd_d,
                 ssd_norm_g, mla_q_norm_g, mla_w_uq, mla_kv_norm_g, mla_w_ukv, gdn_conv_w, gdn_dt_bias,
                 gdn_a_log, gdn_norm_g, w_ssd_out, w_mla_out, w_gdn_out, w_out, norm2_g, w_up, w_down):
    xn = rmsnorm(x, norm1_g)
    proj = xn @ w_in
    split_at = [int(i) for i in np.cumsum(IN_SIZES)[:-1]]
    (ssd_z, ssd_xbc, ssd_dt, mla_cq, mla_ckv, mla_kr, gdn_qkv, gdn_z, gdn_b, gdn_a,
     gate_logits) = jnp.split(proj, split_at, axis=-1)
    y_ssd = ssd_mixer(ssd_z, ssd_xbc, ssd_dt, ssd_conv_w, ssd_conv_b, ssd_dt_bias, ssd_a_log, ssd_d, ssd_norm_g)
    y_mla = mla_mixer(mla_cq, mla_ckv, mla_kr, cos, sin, mla_q_norm_g, mla_w_uq, mla_kv_norm_g, mla_w_ukv)
    y_gdn = gdn_mixer(gdn_qkv, gdn_z, gdn_b, gdn_a, gdn_conv_w, gdn_dt_bias, gdn_a_log, gdn_norm_g)
    gates = jax.nn.sigmoid(gate_logits.astype(jnp.float32)).astype(x.dtype)
    g_ssd, g_mla, g_gdn = jnp.split(gates, N_BRANCH, axis=-1)
    mixed = g_ssd * (y_ssd @ w_ssd_out) + g_mla * (y_mla @ w_mla_out) + g_gdn * (y_gdn @ w_gdn_out)
    h = x + mixed @ w_out
    f = jnp.square(jax.nn.relu(rmsnorm(h, norm2_g) @ w_up)) @ w_down
    return h + f

def second_inputs(seed: int = 0) -> dict:
    key = jax.random.key(seed)
    ks = iter(jax.random.split(key, 40))

    def nrm(shape, scale):
        return jax.random.normal(next(ks), shape, jnp.float32) * scale

    def gain(shape):
        return 1.0 + nrm(shape, 0.02)

    def dt_bias_init(shape):
        dt = jnp.exp(jax.random.uniform(next(ks), shape, jnp.float32, math.log(1e-3), math.log(1e-1)))
        return dt + jnp.log(-jnp.expm1(-dt))

    def a_log_init(shape):
        return jnp.log(jax.random.uniform(next(ks), shape, jnp.float32, 1.0, 16.0))

    x = jax.random.normal(next(ks), (BATCH, SEQ, D_MODEL), jnp.float32)
    offset = jax.random.randint(next(ks), (BATCH, 1), 0, 1024, dtype=jnp.int32)
    positions = offset + jnp.arange(SEQ, dtype=jnp.int32)[None, :]
    return {
        'x': x,
        'positions': positions,
        'norm1_g': gain((DEPTH_2, D_MODEL)),
        'w_in': nrm((DEPTH_2, D_MODEL, N_IN), D_MODEL ** -0.5),
        'ssd_conv_w': nrm((DEPTH_2, SSD_CONV, SSD_XBC), SSD_CONV ** -0.5),
        'ssd_conv_b': nrm((DEPTH_2, SSD_XBC), 0.01),
        'ssd_dt_bias': dt_bias_init((DEPTH_2, SSD_HEADS)),
        'ssd_a_log': a_log_init((DEPTH_2, SSD_HEADS)),
        'ssd_d': gain((DEPTH_2, SSD_HEADS)),
        'ssd_norm_g': gain((DEPTH_2, SSD_INNER)),
        'mla_q_norm_g': gain((DEPTH_2, MLA_Q_LORA)),
        'mla_w_uq': nrm((DEPTH_2, MLA_Q_LORA, MLA_HEADS * (MLA_NOPE + MLA_ROPE)), MLA_Q_LORA ** -0.5),
        'mla_kv_norm_g': gain((DEPTH_2, MLA_KV_LORA)),
        'mla_w_ukv': nrm((DEPTH_2, MLA_KV_LORA, MLA_HEADS * (MLA_NOPE + MLA_V)), MLA_KV_LORA ** -0.5),
        'gdn_conv_w': nrm((DEPTH_2, GDN_CONV, GDN_QKV), GDN_CONV ** -0.5),
        'gdn_dt_bias': dt_bias_init((DEPTH_2, GDN_V_HEADS)),
        'gdn_a_log': a_log_init((DEPTH_2, GDN_V_HEADS)),
        'gdn_norm_g': gain((DEPTH_2, GDN_HEAD_V)),
        'w_ssd_out': nrm((DEPTH_2, SSD_INNER, D_MODEL), SSD_INNER ** -0.5),
        'w_mla_out': nrm((DEPTH_2, MLA_HEADS * MLA_V, D_MODEL), (MLA_HEADS * MLA_V) ** -0.5),
        'w_gdn_out': nrm((DEPTH_2, GDN_VW, D_MODEL), GDN_VW ** -0.5),
        'w_out': nrm((DEPTH_2, D_MODEL, D_MODEL), D_MODEL ** -0.5),
        'norm2_g': gain((DEPTH_2, D_MODEL)),
        'w_up': nrm((DEPTH_2, D_MODEL, D_FF), D_MODEL ** -0.5),
        'w_down': nrm((DEPTH_2, D_FF, D_MODEL), D_FF ** -0.5),
        'final_norm_g': gain((D_MODEL,)),
    }

def second_block(x, positions, norm1_g, w_in, ssd_conv_w, ssd_conv_b, ssd_dt_bias, ssd_a_log, ssd_d,
              ssd_norm_g, mla_q_norm_g, mla_w_uq, mla_kv_norm_g, mla_w_ukv, gdn_conv_w, gdn_dt_bias,
              gdn_a_log, gdn_norm_g, w_ssd_out, w_mla_out, w_gdn_out, w_out, norm2_g, w_up, w_down,
              final_norm_g):
    cos, sin = rope_tables(positions)
    for l in range(DEPTH_2):
        x = hybrid_layer(x, cos, sin, norm1_g[l], w_in[l], ssd_conv_w[l], ssd_conv_b[l], ssd_dt_bias[l],
                         ssd_a_log[l], ssd_d[l], ssd_norm_g[l], mla_q_norm_g[l], mla_w_uq[l],
                         mla_kv_norm_g[l], mla_w_ukv[l], gdn_conv_w[l], gdn_dt_bias[l], gdn_a_log[l],
                         gdn_norm_g[l], w_ssd_out[l], w_mla_out[l], w_gdn_out[l], w_out[l], norm2_g[l],
                         w_up[l], w_down[l])
    return rmsnorm(x, final_norm_g)


def setup_inputs(seed=0):
    out = dict(first_inputs(seed))
    for name, value in second_inputs(seed + 1).items():
        if name != "x":
            out[name + "_2"] = value
    return out


def reference(
    x, mem, norm_mix_g, w_in, att_q_g, att_k_g, rel_bias, ssm_lam_re, ssm_lam_im, ssm_log_step,
    ssm_b_re, ssm_b_im, ssm_c_re, ssm_c_im, ssm_d, ssm_w_glu, ssm_b_glu, att_out_g, ssm_out_g,
    w_out, norm_mem_g, norm_memkv_g, w_mem_q, w_mem_k, w_mem_v, mem_q_g, mem_k_g, w_mem_o,
    norm_peer_g, w_peer_q, peer_keys, peer_u, peer_v, positions_2, norm1_g_2, w_in_2,
    ssd_conv_w_2, ssd_conv_b_2, ssd_dt_bias_2, ssd_a_log_2, ssd_d_2, ssd_norm_g_2,
    mla_q_norm_g_2, mla_w_uq_2, mla_kv_norm_g_2, mla_w_ukv_2, gdn_conv_w_2, gdn_dt_bias_2,
    gdn_a_log_2, gdn_norm_g_2, w_ssd_out_2, w_mla_out_2, w_gdn_out_2, w_out_2, norm2_g_2,
    w_up_2, w_down_2, final_norm_g_2,
):
    x = first_block(
        x, mem, norm_mix_g, w_in, att_q_g, att_k_g, rel_bias, ssm_lam_re, ssm_lam_im,
        ssm_log_step, ssm_b_re, ssm_b_im, ssm_c_re, ssm_c_im, ssm_d, ssm_w_glu, ssm_b_glu,
        att_out_g, ssm_out_g, w_out, norm_mem_g, norm_memkv_g, w_mem_q, w_mem_k, w_mem_v,
        mem_q_g, mem_k_g, w_mem_o, norm_peer_g, w_peer_q, peer_keys, peer_u, peer_v,
    )
    return second_block(
        x, positions_2, norm1_g_2, w_in_2, ssd_conv_w_2, ssd_conv_b_2, ssd_dt_bias_2,
        ssd_a_log_2, ssd_d_2, ssd_norm_g_2, mla_q_norm_g_2, mla_w_uq_2, mla_kv_norm_g_2,
        mla_w_ukv_2, gdn_conv_w_2, gdn_dt_bias_2, gdn_a_log_2, gdn_norm_g_2, w_ssd_out_2,
        w_mla_out_2, w_gdn_out_2, w_out_2, norm2_g_2, w_up_2, w_down_2, final_norm_g_2,
    )


_drawn_inputs = setup_inputs


def setup_inputs(seed=0):
    import zlib

    import numpy as np

    out = dict(_drawn_inputs(seed))
    spreads = {}
    factors = {'att_q_g': 2.762,
     'ssm_lam_re': 33.251,
     'ssm_b_glu': 6.856,
     'norm_mem_g': 8.0,
     'norm_memkv_g': 7.022,
     'mem_q_g': 8.0,
     'mem_k_g': 8.0,
     'norm1_g_2': 3.117,
     'ssd_conv_b_2': 8.0,
     'ssd_d_2': 64.0,
     'ssd_norm_g_2': 23.997,
     'mla_q_norm_g_2': 8.0,
     'mla_kv_norm_g_2': 8.0,
     'gdn_norm_g_2': 8.0,
     'norm2_g_2': 2.867,
     'final_norm_g_2': 7.945}
    for name, (base, spread) in spreads.items():
        noise = np.random.default_rng([zlib.crc32(name.encode()), seed]).standard_normal(out[name].shape)
        drawn = base * np.exp(spread * noise) if base else spread * noise
        out[name] = jnp.asarray(drawn.astype(out[name].dtype))
    for name, factor in factors.items():
        out[name] = (out[name] * factor).astype(out[name].dtype)
    return out
```

```python
import math
from contextlib import ExitStack, contextmanager

import concourse.bass as bass
from concourse import mybir

F32 = mybir.dt.float32
F32R = mybir.dt.float32r
I32 = mybir.dt.int32
U32 = mybir.dt.uint32
ALU = mybir.AluOpType
ACT = mybir.ActivationFunctionType
AX = mybir.AxisListType

P = 128
T = 512
TT = T // P
D = 1024
DC = D // P
EPS = 1e-6
NEG = -1e30
SLOTS = 4
LAYERS = 2

TWO_PI = 2.0 * math.pi
PI_HIGH = 6.28125
PI_LOW = TWO_PI - PI_HIGH


@contextmanager
def stage(nc, names):
    with ExitStack() as held:
        sems = [held.enter_context(nc.semaphore(n)) for n in names.split()]
        with nc.Block() as block:
            yield (block, *sems)
        for s in sems:
            nc.gpsimd.sem_clear(s)
        nc.all_engine_barrier()


class Chain:

    def __init__(self, eng, sem):
        self.eng, self.sem, self.n = eng, sem, 0

    def __call__(self, ins):
        ins.then_inc(self.sem, 1)
        self.n += 1
        self.eng.wait_ge(self.sem, self.n)


def over(eng, n, body):
    body(0, True)
    if n > 1:
        with eng.Fori(1, n) as i:
            body(i, False)


def row(w, i):
    return w[bass.ds(i, 1)].rearrange("o p n -> p (o n)")


def linear(nc, name, w, at, tiles, x, kc, ring, banks, evac, write, pieces=1, n=T, post=None):
    u_n = min(SLOTS, tiles * pieces)
    steps = tiles * pieces // u_n
    per = u_n // pieces
    loaded_names = " ".join(f"{name}_w{u}_loaded" for u in range(u_n))
    with stage(nc, f"{name}_piece_done {name}_tile_written {name}_finished {loaded_names}") as (
            block, piece_done, tile_written, finished, *loaded):

        @block.sync
        def _(sp):
            def step(i, first):
                for u in range(u_n):
                    if not first:
                        sp.wait_ge(piece_done, (i - 1) * u_n + u + 1)
                    sp.dma_start(ring[:, u, 0:kc * P], row(w, at + i * u_n + u)).then_inc(loaded[u], 16)
            over(sp, steps, step)

        @block.tensor
        def _(pe):
            def step(i, first):
                for u in range(u_n):
                    pe.wait_ge(loaded[u], 16 * (i + 1))
                    t, piece = divmod(u, pieces)
                    if piece == 0 and not first:
                        pe.wait_ge(tile_written, (i - 1) * per + t + 1)
                    for c in range(kc):
                        last = nc.tensor.matmul(banks[t], ring[:, u, c * P:(c + 1) * P], x(piece * kc + c),
                                                start=(piece == 0 and c == 0),
                                                stop=(piece == pieces - 1 and c == kc - 1))
                    last.then_inc(piece_done, 1)
            over(pe, steps, step)

        def out(eng):
            def step(i, first):
                for t in range(per):
                    eng.wait_ge(piece_done, i * u_n + (t + 1) * pieces)
                    write(nc, i * per + t, banks[t]).then_inc(tile_written, 1)
            over(eng, steps, step)

        (block.scalar if evac == "scalar" else block.vector)(out)

        if post is not None:
            @block.vector
            def _(dve):
                def step(i, first):
                    for t in range(per):
                        dve.wait_ge(tile_written, i * per + t + 1)
                        post(nc, i * per + t).then_inc(finished, 1)
                over(dve, steps, step)


def linear_tokens(nc, name, w, at, x, kc, ring, banks, rows, out):
    weights = ring[:, :, :].rearrange("p s n -> p (s n)")[:, 0:kc * 512]
    with stage(nc, f"{name}_loaded {name}_done") as (block, loaded, done):

        @block.sync
        def _(sp):
            sp.dma_start(weights, row(w, at)).then_inc(loaded, 16)

        @block.tensor
        def _(pe):
            pe.wait_ge(loaded, 16)
            for t in range(rows):
                for c in range(kc):
                    last = nc.tensor.matmul(banks[t], x(c)[:, t * P:(t + 1) * P], weights[:, c * 512:(c + 1) * 512],
                                            start=(c == 0), stop=(c == kc - 1))
                last.then_inc(done, 1)

        @block.scalar
        def _(act):
            for t in range(rows):
                act.wait_ge(done, t + 1)
                nc.scalar.copy(out(t), banks[t])


def rmsnorm(nc, name, x, y, chunks, group, ones, width, gain, scratch, rstd, banks, n=T, eps=EPS, mean=True):
    groups = chunks // group
    with stage(nc, f"{name}_squared {name}_summed {name}_ready {name}_rooted {name}_inverse {name}_scaled") as (
            block, squared, summed, ready, rooted, inverse, scaled):

        @block.scalar
        def _(act):
            for c in range(chunks):
                nc.scalar.activation(scratch(c), x(c), ACT.Square).then_inc(squared, 1)
            for g in range(groups):
                act.wait_ge(ready, g + 1)
                nc.scalar.activation(rstd[g % 2], rstd[g % 2], ACT.Sqrt).then_inc(rooted, 1)

        @block.tensor
        def _(pe):
            for g in range(groups):
                pe.wait_ge(squared, (g + 1) * group)
                if g >= 4:
                    pe.wait_ge(ready, g - 3)
                for k in range(group):
                    last = nc.tensor.matmul(banks[g % 4], ones, scratch(g * group + k), start=(k == 0), stop=(k == group - 1))
                last.then_inc(summed, 1)

        @block.vector
        def _(dve):
            for g in range(groups):
                dve.wait_ge(summed, g + 1)
                nc.vector.tensor_scalar(rstd[g % 2], banks[g % 4], 1.0 / width if mean else 1.0, eps,
                                        ALU.mult, ALU.add).then_inc(ready, 1)
                dve.wait_ge(rooted, g + 1)
                nc.vector.reciprocal(rstd[g % 2], rstd[g % 2]).then_inc(inverse, 1)
                dve.wait_ge(inverse, g + 1)
                for k in range(group):
                    c = g * group + k
                    if gain is None:
                        nc.vector.tensor_tensor(y(c), x(c), rstd[g % 2], ALU.mult).then_inc(scaled, 1)
                    else:
                        nc.vector.scalar_tensor_tensor(y(c), x(c), gain(c), rstd[g % 2], ALU.mult, ALU.mult)\
                            .then_inc(scaled, 1)


def attention(nc, name, heads, scores, keys, scale, bias, values, depth, place, out, banks, sc, pr, pt, stats, ident):
    jobs = [(h, q) for h in range(heads) for q in range(TT)]
    with stage(nc, f"{name}_scored {name}_masked {name}_max {name}_exp {name}_inv {name}_probs {name}_turned "
                   f"{name}_copied {name}_mixed {name}_stored") as (
            block, scored, masked, maxed, exped, inverted, normed, turned, copied, mixed, stored):

        @block.tensor
        def _(pe):
            def turn(j):
                h, q = jobs[j]
                pe.wait_ge(normed, j + 1)
                if j >= 2:
                    pe.wait_ge(copied, j - 1)
                for k in range(keys(q)):
                    last = nc.tensor.transpose(banks[2 + j % 2][:, k * P:(k + 1) * P], pr[:, j % 2, k * P:(k + 1) * P], ident)
                last.then_inc(turned, 1)
                if q == TT - 1:
                    pe.wait_ge(copied, j + 1)
                    if h >= 2:
                        pe.wait_ge(stored, h - 1)
                    for k in range(keys(q)):
                        first_q = min(x for x in range(TT) if keys(x) > k) * P
                        last = nc.tensor.matmul(banks[4 + h % 2][place(h), first_q:T], values(h, k), pt[:, h % 2, k, first_q:T],
                                                start=(k == 0), stop=(k == keys(q) - 1))
                    last.then_inc(mixed, 1)

            for j, (h, q) in enumerate(jobs):
                if j >= 2:
                    pe.wait_ge(masked, j - 1)
                pairs = scores(h, q)
                for n, (a, b) in enumerate(pairs):
                    last = nc.tensor.matmul(banks[j % 2][:, 0:keys(q) * P], a, b, start=(n == 0), stop=(n == len(pairs) - 1))
                last.then_inc(scored, 1)
                if j:
                    turn(j - 1)
            turn(len(jobs) - 1)

        @block.vector
        def _(dve):
            def normalize(j):
                h, q = jobs[j]
                w = keys(q) * P
                dve.wait_ge(exped, j + 1)
                nc.vector.reciprocal(stats[:, 4 + j % 2:5 + j % 2], stats[:, 2 + j % 2:3 + j % 2]).then_inc(inverted, 1)
                dve.wait_ge(inverted, j + 1)
                nc.vector.tensor_scalar(pr[:, j % 2, 0:w], pr[:, j % 2, 0:w], stats[:, 4 + j % 2:5 + j % 2], None,
                                        ALU.mult).then_inc(normed, 1)

            for j, (h, q) in enumerate(jobs):
                w = keys(q) * P
                dve.wait_ge(scored, j + 1)
                b = bias(h, q)
                if b is None:
                    nc.vector.tensor_scalar(sc[:, j % 2, 0:w], banks[j % 2][:, 0:w], scale, None, ALU.mult).then_inc(masked, 1)
                else:
                    nc.vector.scalar_tensor_tensor(sc[:, j % 2, 0:w], banks[j % 2][:, 0:w], scale, b, ALU.mult, ALU.add)\
                        .then_inc(masked, 1)
                dve.wait_ge(masked, j + 1)
                nc.vector.tensor_reduce(stats[:, j % 2:j % 2 + 1], sc[:, j % 2, 0:w], AX.X, ALU.max, negate=True)\
                    .then_inc(maxed, 1)
                if j:
                    normalize(j - 1)
            normalize(len(jobs) - 1)

        @block.scalar
        def _(act):
            def copy(j):
                h, q = jobs[j]
                act.wait_ge(turned, j + 1)
                if h >= 2 and q == 0:
                    act.wait_ge(mixed, h - 1)
                w = keys(q) * P
                nc.scalar.copy(pt[:, h % 2, 0:keys(q), q * P:(q + 1) * P],
                               banks[2 + j % 2][:, 0:w].rearrange("p (k n) -> p k n", n=P)).then_inc(copied, 1)
                if q == TT - 1:
                    act.wait_ge(mixed, h + 1)
                    nc.scalar.copy(out(h), banks[4 + h % 2][place(h), :]).then_inc(stored, 1)

            for j, (h, q) in enumerate(jobs):
                w = keys(q) * P
                act.wait_ge(maxed, j + 1)
                if j >= 2:
                    act.wait_ge(turned, j - 1)
                nc.scalar.activation(pr[:, j % 2, 0:w], sc[:, j % 2, 0:w], ACT.Exp, bias=stats[:, j % 2:j % 2 + 1],
                                     accum_out=stats[:, 2 + j % 2:3 + j % 2]).then_inc(exped, 1)
                if j:
                    copy(j - 1)
            copy(len(jobs) - 1)


def sine(nc, link, angle, turns, turns_int, s, c):
    v = nc.vector
    link(v.tensor_scalar(turns, angle, 1.0 / TWO_PI, None, ALU.mult))
    link(v.tensor_copy(turns_int, turns))
    link(v.tensor_copy(turns, turns_int))
    link(v.scalar_tensor_tensor(s, turns, -PI_HIGH, angle, ALU.mult, ALU.add))
    link(v.scalar_tensor_tensor(s, turns, -PI_LOW, s, ALU.mult, ALU.add))
    link(v.tensor_scalar(s, s, 0.125, None, ALU.mult))
    return v.tensor_scalar(c, s, math.pi / 2, None, ALU.add)


def double_angle(nc, link, s, c, tmp, times=3):
    v = nc.vector
    for _ in range(times):
        link(v.tensor_tensor(tmp, s, c, ALU.mult))
        link(v.tensor_tensor(c, s, s, ALU.mult))
        link(v.tensor_scalar(c, c, -2.0, 1.0, ALU.mult, ALU.add))
        link(v.tensor_scalar(s, tmp, 2.0, None, ALU.mult))


def bc(ap, n):
    return ap.unsqueeze(2).to_broadcast([ap.shape[0], ap.shape[1], n])



HEADS1, HD1 = 8, 64
SSM_TILES = 16
MEM = 256
VEC1 = dict(mix_g=(0, 8), att_q_g=(8, 1), att_k_g=(9, 1), lam_re=(10, 16), lam_im=(26, 16), log_step=(42, 16),
            ssm_d=(58, 4), b_glu=(62, 4), mixed_g=(66, 8), mem_g=(74, 8), memkv_g=(82, 8), mem_q_g=(90, 2),
            mem_k_g=(92, 2), peer_g=(94, 8))
VEC1_N = 102


def first_block(nc, dram, sb, psum, hT, xnT, scratch, ring, rstd, ones, halves, ident, upto, start):
    banks = [psum[:, b, :] for b in range(8)]
    with ExitStack() as held:
        vec = held.enter_context(nc.sbuf_tensor("vec1", [P, VEC1_N], F32))

        def col(name, k=0):
            return vec[:, VEC1[name][0] + k:VEC1[name][0] + k + 1]

        def cols(name):
            return vec[:, VEC1[name][0]:VEC1[name][0] + VEC1[name][1]]

        with stage(nc, "inputs_loaded") as (block, loaded):
            @block.sync
            def _(sp):
                sp.dma_start(hT[:].rearrange("p c n -> p (c n)"), dram["xT"]).then_inc(loaded, 16)
                sp.dma_start(vec[:], dram["vec1"]).then_inc(loaded, 16)
                sp.wait_ge(loaded, 32)

        def norm_x(name, gain):
            rmsnorm(nc, name, lambda c: hT[:, c, :], lambda c: xnT[:, c, :], DC, DC, ones, D,
                    lambda c: col(gain, c), lambda c: scratch[:, c, :], rstd, banks)

        def xn(c):
            return xnT[:, c, :]

        def mix():
            norm_x("norm_mix", "mix_g")
            with ExitStack() as phase:
                qT = phase.enter_context(nc.sbuf_tensor("qT", [P, 4, T], F32))
                kT = phase.enter_context(nc.sbuf_tensor("kT", [P, 4, T], F32))
                uT = phase.enter_context(nc.sbuf_tensor("uT", [P, 4, T], F32))
                quk = [qT, kT, uT]
                vS = phase.enter_context(nc.sbuf_tensor("vS", [P, TT, 512], F32))
                mixT = phase.enter_context(nc.sbuf_tensor("mixT", [P, 8, T], F32))
                for n, dst in enumerate(quk):
                    linear(nc, f"w_in{n}", dram["w_in"], 4 * n, 4, xn, DC, ring, banks, "scalar",
                           lambda nc, f, ps, dst=dst: nc.scalar.copy(dst[:, bass.ds(f, 1), :].squeeze(1), ps))
                linear_tokens(nc, "w_v", dram["w_in_v"], 0, xn, DC, ring, banks, TT, lambda t: vS[:, t, :])
                for name, t_, g in (("norm_q", qT, "att_q_g"), ("norm_k", kT, "att_k_g")):
                    rmsnorm(nc, name, lambda c, t_=t_: t_[:, c, :], lambda c, t_=t_: t_[:, c, :], 4, 1, halves, HD1,
                            lambda c, g=g: col(g), lambda c: scratch[:, c, :], rstd, banks)
                with ExitStack() as att:
                    bias = att.enter_context(nc.sbuf_tensor("bias", [P, HEADS1, 512], F32))
                    sc = att.enter_context(nc.sbuf_tensor("sc", [P, 2, 512], F32))
                    pr = att.enter_context(nc.sbuf_tensor("pr", [P, 2, 512], F32))
                    pt = att.enter_context(nc.sbuf_tensor("pt", [P, 2, 4, 512], F32))
                    stats = att.enter_context(nc.sbuf_tensor("stats", [P, 8], F32))
                    with stage(nc, "bias_loaded bias_masked") as (block, loaded, masked):
                        @block.sync
                        def _(sp):
                            sp.dma_start(bias[:].rearrange("p h n -> p (h n)"), dram["bias"]).then_inc(loaded, 16)

                        @block.vector
                        def _(dve):
                            dve.wait_ge(loaded, 16)
                            nc.vector.memset(bias[0:64, :, 448:512], NEG).then_inc(masked, 1)

                    def half(h):
                        return slice(64 * (h % 2), 64 * (h % 2) + 64)
                    attention(nc, "band", HEADS1,
                              lambda h, q: [(qT[half(h), h // 2, q * P:(q + 1) * P], kT[half(h), h // 2, 0:(q + 1) * P])],
                              lambda q: q + 1, HD1 ** -0.5, lambda h, q: bias[:, h, 384 - 128 * q:512],
                              lambda h, k: vS[:, k, h * HD1:(h + 1) * HD1], HD1, half,
                              lambda h: mixT[half(h), h // 2, :], banks, sc, pr, pt, stats, ident)
                rmsnorm(nc, "norm_att", lambda c: mixT[:, c, :], lambda c: mixT[:, c, :], 4, 4, ones, 512,
                        lambda c: col("mixed_g", c), lambda c: scratch[:, c, :], rstd, banks)
                state_space(nc, dram, col, cols, uT, mixT, ring, banks, psum, scratch)
                rmsnorm(nc, "norm_ssm", lambda c: mixT[:, 4 + c, :], lambda c: mixT[:, 4 + c, :], 4, 4, ones, 512,
                        lambda c: col("mixed_g", 4 + c), lambda c: scratch[:, c, :], rstd, banks)
                linear(nc, "w_out", dram["w_out"], 0, 8, lambda c: mixT[:, c, :], DC, ring, banks, "vector",
                       lambda nc, f, ps: add_to(nc, hT, f, ps))

        if start is None:
            mix()
        if upto == "h1":
            return

        def memory():
            norm_x("norm_mem", "mem_g")
            with ExitStack() as phase:
                memT = phase.enter_context(nc.sbuf_tensor("memT", [P, 8, MEM], F32))
                mqT = phase.enter_context(nc.sbuf_tensor("mqT", [P, 8, T], F32))
                mkT = phase.enter_context(nc.sbuf_tensor("mkT", [P, 8, MEM], F32))
                mv = phase.enter_context(nc.sbuf_tensor("mv", [P, 2, D], F32))
                moT = phase.enter_context(nc.sbuf_tensor("moT", [P, 8, T], F32))
                with stage(nc, "memory_loaded") as (block, loaded):
                    @block.sync
                    def _(sp):
                        sp.dma_start(memT[:].rearrange("p c n -> p (c n)"), dram["memT"]).then_inc(loaded, 16)
                        sp.wait_ge(loaded, 16)

                def short(c):
                    return scratch[:, c, 0:MEM]
                rmsnorm(nc, "norm_memkv", lambda c: memT[:, c, :], lambda c: memT[:, c, :], 8, 8, ones, D,
                        lambda c: col("memkv_g", c), short, [r[:, 0:MEM] for r in rstd], [b[:, 0:MEM] for b in banks])
                linear(nc, "w_mem_q", dram["w_mem_q"], 0, 8, xn, DC, ring, banks, "scalar",
                       lambda nc, f, ps: nc.scalar.copy(mqT[:, bass.ds(f, 1), :].squeeze(1), ps))
                linear(nc, "w_mem_k", dram["w_mem_k"], 0, 8, lambda c: memT[:, c, :], DC, ring, [b[:, 0:MEM] for b in banks],
                       "scalar", lambda nc, f, ps: nc.scalar.copy(mkT[:, bass.ds(f, 1), :].squeeze(1), ps))
                for n in range(2):
                    linear_tokens(nc, f"w_mem_v{n}", dram["w_mem_v"], n, lambda c: memT[:, c, :], DC, ring, banks, 2,
                                  lambda t, n=n: mv[:, t, n * 512:(n + 1) * 512])
                rmsnorm(nc, "norm_mq", lambda c: mqT[:, c, :], lambda c: mqT[:, c, :], 8, 2, ones, 256,
                        lambda c: col("mem_q_g", c % 2), lambda c: scratch[:, c, :], rstd, banks)
                rmsnorm(nc, "norm_mk", lambda c: mkT[:, c, :], lambda c: mkT[:, c, :], 8, 2, ones, 256,
                        lambda c: col("mem_k_g", c % 2), short, [r[:, 0:MEM] for r in rstd], [b[:, 0:MEM] for b in banks])
                with ExitStack() as att:
                    sc = att.enter_context(nc.sbuf_tensor("mem_sc", [P, 2, 512], F32))
                    pr = att.enter_context(nc.sbuf_tensor("mem_pr", [P, 2, 512], F32))
                    pt = att.enter_context(nc.sbuf_tensor("mem_pt", [P, 2, 4, 512], F32))
                    stats = att.enter_context(nc.sbuf_tensor("mem_stats", [P, 8], F32))
                    attention(nc, "memory", 8,
                              lambda h, q: [(mqT[:, 2 * (h // 2) + c, q * P:(q + 1) * P], mkT[:, 2 * (h // 2) + c, :]) for c in range(2)],
                              lambda q: 2, 256 ** -0.5, lambda h, q: None,
                              lambda h, k: mv[:, k, h * P:(h + 1) * P], P, lambda h: slice(0, P),
                              lambda h: moT[:, h, :], banks, sc, pr, pt, stats, ident)
                linear(nc, "w_mem_o", dram["w_mem_o"], 0, 8, lambda c: moT[:, c, :], DC, ring, banks, "vector",
                       lambda nc, f, ps: add_to(nc, hT, f, ps))

        if start in (None, 'h1'):
            memory()
        if upto == "h2":
            return
        if start in (None, "h1", "h2"):
            norm_x("norm_peer", "peer_g")
            experts(nc, dram, hT, xnT, scratch, ring, banks, ident)
        if upto == "h3":
            return


def add_to(nc, hT, f, ps):
    tile = hT[:, bass.ds(f, 1), :].squeeze(1)
    return nc.vector.tensor_tensor(tile, tile, ps, ALU.add)


def state_space(nc, dram, col, cols, uT, mixT, ring, banks, psum, scratch):
    with ExitStack() as held:
        def sb(name, shape, dt=F32):
            return held.enter_context(nc.sbuf_tensor(name, shape, dt))
        N = SSM_TILES
        par = sb("ssm_par", [P, 16, N])
        step, lre, mag, sn, cs, tmp, turns, fr, fi, den, zr_, th, aim = (par[:, i, :] for i in range(13))
        turns_int = sb("turns_int", [P, N], I32)
        power = sb("power", [P, 9, 2, N])
        Er = sb("Er", [P, N, T])
        Ei = sb("Ei", [P, N, T])
        cre = sb("cre", [P, N, 32])
        cim = sb("cim", [P, N, 32])
        c1 = sb("c1", [P, N, 32])
        c2 = sb("c2", [P, N, 32])
        big = sb("rot_tmp", [P, N // 4, 256])
        bre = sb("bre", [P, 4, 128])
        bim = sb("bim", [P, 4, 128])
        with stage(nc, "c_loaded step_done angles_ready exps_done sines_done dve_step") as (
                block, loaded, step_done, angles, exps, sines, dve_step):

            @block.sync
            def _(sp):
                sp.dma_start(cre[:].rearrange("p a b -> p (a b)"), dram["c_re"]).then_inc(loaded, 16)
                sp.dma_start(cim[:].rearrange("p a b -> p (a b)"), dram["c_im"]).then_inc(loaded, 16)
                sp.dma_start(bre[:].rearrange("p a b -> p (a b)"), dram["b_re"]).then_inc(loaded, 16)
                sp.dma_start(bim[:].rearrange("p a b -> p (a b)"), dram["b_im"]).then_inc(loaded, 16)

            @block.scalar
            def _(act):
                nc.scalar.activation(step, cols("log_step"), ACT.Exp).then_inc(step_done, 1)
                act.wait_ge(angles, 1)
                nc.scalar.activation(mag, lre, ACT.Exp).then_inc(exps, 1)
                act.wait_ge(angles, 2)
                nc.scalar.activation(sn, sn, ACT.Sin).then_inc(sines, 1)
                nc.scalar.activation(cs, cs, ACT.Sin).then_inc(sines, 1)

            @block.vector
            def _(dve):
                v = nc.vector
                link = Chain(dve, dve_step)
                dve.wait_ge(step_done, 1)
                link(v.tensor_tensor(th, cols("lam_im"), step, ALU.mult))
                v.tensor_tensor(lre, cols("lam_re"), step, ALU.mult).then_inc(angles, 1)
                sine(nc, link, th, turns, turns_int[:], sn, cs).then_inc(angles, 1)
                dve.wait_ge(exps, 1)
                dve.wait_ge(sines, 2)
                double_angle(nc, link, sn, cs, tmp)
                link(v.tensor_tensor(zr_, mag, cs, ALU.mult))
                link(v.tensor_scalar(zr_, zr_, -1.0, None, ALU.add))
                link(v.tensor_tensor(aim, mag, sn, ALU.mult))
                link(v.tensor_tensor(den, cols("lam_re"), cols("lam_re"), ALU.mult))
                link(v.tensor_tensor(tmp, cols("lam_im"), cols("lam_im"), ALU.mult))
                link(v.tensor_tensor(den, den, tmp, ALU.add))
                link(v.reciprocal(den, den))
                link(v.tensor_tensor(fr, zr_, cols("lam_re"), ALU.mult))
                link(v.tensor_tensor(tmp, aim, cols("lam_im"), ALU.mult))
                link(v.tensor_tensor(fr, fr, tmp, ALU.add))
                link(v.tensor_tensor(fr, fr, den, ALU.mult))
                link(v.tensor_tensor(fi, aim, cols("lam_re"), ALU.mult))
                link(v.tensor_tensor(tmp, zr_, cols("lam_im"), ALU.mult))
                link(v.tensor_tensor(fi, fi, tmp, ALU.subtract))
                link(v.tensor_tensor(fi, fi, den, ALU.mult))
                dve.wait_ge(loaded, 64)
                link(v.tensor_tensor(c1[:], cre[:], bc(fr, 32), ALU.mult))
                link(v.tensor_tensor(c2[:], cim[:], bc(fi, 32), ALU.mult))
                link(v.tensor_tensor(c1[:], c1[:], c2[:], ALU.subtract))
                link(v.tensor_tensor(cre[:], cre[:], bc(fi, 32), ALU.mult))
                link(v.tensor_tensor(cim[:], cim[:], bc(fr, 32), ALU.mult))
                link(v.tensor_tensor(c2[:], cre[:], cim[:], ALU.add))
                link(v.tensor_scalar(c2[:], c2[:], -1.0, None, ALU.mult))
                link(v.tensor_scalar(cre[:], c1[:], -1.0, None, ALU.mult))
                link(v.tensor_copy(power[:, 0, 0, :], cs))
                link(v.tensor_copy(power[:, 0, 1, :], sn))
                for k in range(8):
                    c_, s_, c2_, s2_ = power[:, k, 0, :], power[:, k, 1, :], power[:, k + 1, 0, :], power[:, k + 1, 1, :]
                    link(v.tensor_tensor(tmp, s_, s_, ALU.mult))
                    link(v.tensor_tensor(c2_, c_, c_, ALU.mult))
                    link(v.tensor_tensor(c2_, c2_, tmp, ALU.subtract))
                    link(v.scalar_tensor_tensor(s2_, s_, 2.0, c_, ALU.mult, ALU.mult))
                link(v.memset(Er[:, :, 0:1], 1.0))
                link(v.memset(Ei[:, :, 0:1], 0.0))
                for k in range(9):
                    n = 1 << k
                    for t0 in range(0, N, 4):
                        ts_ = slice(t0, t0 + 4)
                        c_, s_ = bc(power[:, k, 0, ts_], n), bc(power[:, k, 1, ts_], n)
                        link(v.tensor_tensor(big[:, :, 0:n], Ei[:, ts_, 0:n], s_, ALU.mult))
                        link(v.tensor_tensor(Er[:, ts_, n:2 * n], Er[:, ts_, 0:n], c_, ALU.mult))
                        link(v.tensor_tensor(Er[:, ts_, n:2 * n], Er[:, ts_, n:2 * n], big[:, :, 0:n], ALU.subtract))
                        link(v.tensor_tensor(big[:, :, 0:n], Er[:, ts_, 0:n], s_, ALU.mult))
                        link(v.tensor_tensor(Ei[:, ts_, n:2 * n], Ei[:, ts_, 0:n], c_, ALU.mult))
                        link(v.tensor_tensor(Ei[:, ts_, n:2 * n], Ei[:, ts_, n:2 * n], big[:, :, 0:n], ALU.add))

        w = scratch
        with stage(nc, "b_ready turned_in scanned products y_ready y_summed y_activated dve_step pool_step") as (
                block, b_ready, rotated, scanned, products, y_ready, summed, activated, dve_step, pool_step):

            @block.tensor
            def _(pe):
                def project(i):
                    g, k = divmod(i, 4)
                    s = slice(32 * k, 32 * k + 32)
                    if i >= 1:
                        pe.wait_ge(rotated, i)
                    nc.tensor.matmul(banks[0], bre[s, g, :], uT[s, g, :], start=True, stop=True)
                    nc.tensor.matmul(banks[1], bim[s, g, :], uT[s, g, :], start=True, stop=True).then_inc(b_ready, 1)
                project(0)
                for i in range(N):
                    g, k = divmod(i, 4)
                    if i + 1 < N:
                        project(i + 1)
                    pe.wait_ge(products, i + 1)
                    for n, c in enumerate((c1, cre, c2, c2)):
                        last = nc.tensor.matmul(banks[4 + g][32 * k:32 * k + 32, :], c[:, i, :], w[:, 4 + n, :],
                                                start=(n == 0), stop=(n == 3), skip_group_check=True)
                    last.then_inc(y_ready, 1)

            @block.vector
            def _(dve):
                v = nc.vector
                link = Chain(dve, dve_step)
                for i in range(N):
                    dve.wait_ge(b_ready, i + 1)
                    link(v.tensor_tensor(w[:, 0, :], banks[0], Er[:, i, :], ALU.mult))
                    link(v.tensor_tensor(w[:, 1, :], banks[1], Ei[:, i, :], ALU.mult))
                    link(v.tensor_tensor(w[:, 0, :], w[:, 0, :], w[:, 1, :], ALU.add))
                    link(v.tensor_tensor(w[:, 1, :], banks[1], Er[:, i, :], ALU.mult))
                    if i:
                        dve.wait_ge(products, i)
                    v.tensor_tensor(w[:, 2, :], banks[0], Ei[:, i, :], ALU.mult).then_inc(rotated, 1)
                    dve.wait_ge(rotated, i + 1)
                    link(v.tensor_tensor(w[:, 1, :], w[:, 1, :], w[:, 2, :], ALU.subtract))
                    m = mag[:, i:i + 1].to_broadcast([P, T])
                    link(v.tensor_tensor_scan(w[:, 2, :], m, w[:, 0, :], 0.0, ALU.mult, ALU.add))
                    v.tensor_tensor_scan(w[:, 3, :], m, w[:, 1, :], 0.0, ALU.mult, ALU.add).then_inc(scanned, 1)
                for g in range(4):
                    dve.wait_ge(y_ready, 4 * g + 4)
                    v.scalar_tensor_tensor(uT[:, g, :], uT[:, g, :], col("ssm_d", g), banks[4 + g], ALU.mult, ALU.add)\
                        .then_inc(summed, 1)

            @block.gpsimd
            def _(pool):
                for i in range(N):
                    pool.wait_ge(scanned, i + 1)
                    if i:
                        pool.wait_ge(y_ready, i)
                    nc.gpsimd.tensor_tensor(w[:, 4, :], w[:, 2, :], Er[:, i, :], ALU.mult)
                    nc.gpsimd.tensor_tensor(w[:, 5, :], w[:, 3, :], Ei[:, i, :], ALU.mult)
                    nc.gpsimd.tensor_tensor(w[:, 6, :], w[:, 3, :], Er[:, i, :], ALU.mult)
                    nc.gpsimd.tensor_tensor(w[:, 7, :], w[:, 2, :], Ei[:, i, :], ALU.mult).then_inc(products, 1)

            @block.scalar
            def _(act):
                for g in range(4):
                    act.wait_ge(summed, g + 1)
                    nc.scalar.activation(uT[:, g, :], uT[:, g, :], ACT.Gelu).then_inc(activated, 1)

        bglu = cols("b_glu")
        with stage(nc, "glu_loaded glu_done gate_ready gated") as (block, loaded, done, gate, gated):
            glu = ring[:, :, :].rearrange("p s n -> p (s n)")

            @block.sync
            def _(sp):
                for f in range(4):
                    sp.dma_start(glu[:, f * 512:(f + 1) * 512], row(dram["w_glu"], f)).then_inc(loaded, 16)

            @block.tensor
            def _(pe):
                pe.wait_ge(loaded, 64)
                for f in range(4):
                    for c in range(4):
                        last = nc.tensor.matmul(banks[f], glu[:, f * 512 + c * P:f * 512 + (c + 1) * P], uT[:, c, :],
                                                start=(c == 0), stop=(c == 3))
                    last.then_inc(done, 1)

            @block.scalar
            def _(act):
                for f in range(4):
                    act.wait_ge(done, f + 1)
                    nc.scalar.activation(scratch[:, f, :], banks[f], ACT.Sigmoid, bias=bglu[:, f:f + 1]).then_inc(gate, 1)

            @block.vector
            def _(dve):
                for f in range(4):
                    dve.wait_ge(gate, f + 1)
                    nc.vector.tensor_tensor(mixT[:, 4 + f, :], uT[:, f, :], scratch[:, f, :], ALU.mult).then_inc(gated, 1)



PH, PK, TOP = 8, 128, 16
GROUP = 4
LOWEST = -3e38


def experts(nc, dram, hT, xnT, scratch, ring, banks, ident):
    with ExitStack() as held:
        first = held.enter_context(nc.sbuf_tensor("firstT", [P, T], F32))
        second = held.enter_context(nc.sbuf_tensor("secondT", [P, T], F32))
        gateT = held.enter_context(nc.sbuf_tensor("gateT", [P, T], F32))
        iota = held.enter_context(nc.sbuf_tensor("iota", [P, PK], F32))
        with stage(nc, "iota_ready") as (block, ready):
            @block.gpsimd
            def _(pool):
                nc.gpsimd.iota(iota[:], pattern=[[1, PK]], base=0, channel_multiplier=0,
                               allow_small_or_imprecise_dtypes=True).then_inc(ready, 1)
        choose_experts(nc, dram, xnT, ring, banks, ident, first, second, gateT, iota)
        build_gates(nc, dram, scratch, ring, banks, first, second, gateT, iota)
    stream_experts(nc, dram, hT, xnT, scratch, ring, banks)


def choose_experts(nc, dram, xnT, ring, banks, ident, first, second, gateT, iota):
    with ExitStack() as held:
        def sb(name, shape, dt=F32):
            return held.enter_context(nc.sbuf_tensor(name, shape, dt))
        qT = sb("peer_qT", [P, 2 * PH, T])
        keys = sb("peer_keys_sb", [P, 2 * PH, PK])
        qs = sb("q_tile", [P, 2 * PH, P])
        s1 = sb("key_scores", [P, 2 * PH, PK])
        s2 = sb("key_scores_rest", [P, 2 * PH, PK])
        sv = sb("key_top", [P, 2 * PH, TOP])
        si = sb("key_index", [P, 2 * PH, TOP], U32)
        sif = sb("key_index_f", [P, 2 * PH, TOP])
        top = sb("pair_top", [P, PH, TOP])
        pos = sb("pair_index", [P, PH, TOP], U32)
        ab = sb("pair_ab", [P, 2, PH * TOP], U32)
        abf = sb("pair_ab_f", [P, 2, PH * TOP])
        tab = sb("to_turn", [P, 3, PH * TOP])
        sums = sb("gate_sums", [P, PH])
        linear(nc, "w_peer_q", dram["w_peer_q"], 0, 2 * PH, lambda c: xnT[:, c, :], DC, ring, banks, "scalar",
               lambda nc, f, ps: nc.scalar.copy(qT[:, bass.ds(f, 1), :].squeeze(1), ps))
        with stage(nc, "keys_loaded") as (block, loaded):
            @block.sync
            def _(sp):
                sp.dma_start(keys[:].rearrange("p h n -> p (h n)"), dram["peer_keys"]).then_inc(loaded, 16)
                sp.wait_ge(loaded, 16)
        with nc.Fori(0, TT) as t:
            with stage(nc, "q_copied keys_scored scores_stored") as (block, copied, scored, kept):
                @block.scalar
                def _(act):
                    nc.scalar.copy(qs[:], qT[:, :, bass.ds(t * P, P)]).then_inc(copied, 1)
                    for b in range(4):
                        act.wait_ge(scored, b + 1)
                        nc.scalar.copy(s1[:, 4 * b:4 * b + 4, :], banks[b].rearrange("p (h n) -> p h n", n=PK)).then_inc(kept, 1)

                @block.tensor
                def _(pe):
                    pe.wait_ge(copied, 1)
                    for b in range(4):
                        for k in range(4):
                            last = nc.tensor.matmul(banks[b][:, k * PK:(k + 1) * PK], qs[:, 4 * b + k, :], keys[:, 4 * b + k, :],
                                                    start=True, stop=True)
                        last.then_inc(scored, 1)

            with stage(nc, "dve_step logits_ready exps_done gates_ready turned") as (
                    block, dve_step, logits, exps, gates, turned):
                @block.vector
                def _(dve):
                    v = nc.vector
                    link = Chain(dve, dve_step)

                    def top16(n, values, rest, best, index):
                        for k in range(n):
                            last = v.max(best[:, k, 0:8], values[:, k, :])
                        link(last)
                        for k in range(n):
                            v.max_index(index[:, k, 0:8], best[:, k, 0:8], values[:, k, :])
                            last = v.match_replace(rest[:, k, :], best[:, k, 0:8], values[:, k, :], LOWEST)
                        link(last)
                        for k in range(n):
                            last = v.max(best[:, k, 8:16], rest[:, k, :])
                        link(last)
                        for k in range(n):
                            last = v.max_index(index[:, k, 8:16], best[:, k, 8:16], rest[:, k, :])
                        link(last)

                    top16(2 * PH, s1, s2, sv, si)
                    link(v.tensor_copy(sif[:], si[:]))
                    cand = s1[:].rearrange("p (h two) n -> p h (two n)", two=2)
                    rest = s2[:].rearrange("p (h two) n -> p h (two n)", two=2)
                    by_side = sv[:].rearrange("p (h two) a -> p h two a", two=2)
                    for h in range(PH):
                        last = v.tensor_tensor(cand[:, h, :].rearrange("p (a b) -> p a b", b=TOP),
                                               bc(by_side[:, h, 0, :], TOP),
                                               by_side[:, h, 1:2, :].to_broadcast([P, TOP, TOP]), ALU.add)
                    link(last)
                    top16(PH, cand, rest, top, pos)
                    flat = pos[:].rearrange("p h k -> p (h k)")
                    link(v.tensor_scalar(ab[:, 0, :], flat, 4, None, ALU.logical_shift_right))
                    link(v.tensor_scalar(ab[:, 1, :], flat, 15, None, ALU.bitwise_and))
                    link(v.tensor_copy(abf[:], ab[:]))
                    tops = top[:]
                    gate = tab[:, 2, :].rearrange("p (h k) -> p h k", k=TOP)
                    v.tensor_tensor(gate, tops, top[:, :, 0:1].to_broadcast([P, PH, TOP]), ALU.subtract).then_inc(logits, 1)
                    for side in range(2):
                        eq = s1[:].rearrange("p h n -> p (h n)").rearrange("p (x a) -> p x a", a=TOP)
                        link(v.tensor_tensor(eq, bc(abf[:, side, :], TOP),
                                             iota[:, 0:TOP].unsqueeze(1).to_broadcast([P, PH * TOP, TOP]), ALU.is_equal))
                        for h in range(PH):
                            e = eq[:, h * TOP:(h + 1) * TOP, :]
                            last = v.tensor_tensor(e, e, sif[:, 2 * h + side, :].unsqueeze(1).to_broadcast([P, TOP, TOP]), ALU.mult)
                        link(last)
                        link(v.tensor_reduce(tab[:, side, :], eq, AX.X, ALU.add))
                    dve.wait_ge(exps, 1)
                    link(v.tensor_reduce(sums[:], gate, AX.X, ALU.add))
                    link(v.reciprocal(sums[:], sums[:]))
                    v.tensor_tensor(gate, gate, bc(sums[:], TOP), ALU.mult).then_inc(gates, 1)

                @block.scalar
                def _(act):
                    act.wait_ge(logits, 1)
                    nc.scalar.activation(tab[:, 2, :], tab[:, 2, :], ACT.Exp).then_inc(exps, 1)
                    for n, dst in enumerate((first, second, gateT)):
                        act.wait_ge(turned, n + 1)
                        last = nc.scalar.copy(dst[:, bass.ds(t * P, P)], banks[n][:, 0:P])
                    last.then_inc(exps, 1)

                @block.tensor
                def _(pe):
                    pe.wait_ge(gates, 1)
                    for n in range(3):
                        nc.tensor.transpose(banks[n][:, 0:P], tab[:, n, :], ident).then_inc(turned, 1)


ONEHOT = 16


def build_gates(nc, dram, scratch, ring, banks, first, second, gateT, iota):
    a_ = scratch[:].rearrange("p c n -> p (c n)").rearrange("p (b t i) -> p b t i", b=2, i=PK)
    b_ = ring[:].rearrange("p c n -> p (c n)").rearrange("p (b t i) -> p b t i", b=2, i=PK)
    iota_b = iota[:].unsqueeze(1).to_broadcast([P, ONEHOT, PK])
    per_block = P // ONEHOT
    with ExitStack() as held:
        G = held.enter_context(nc.sbuf_tensor("gate_block", [P, 2, PK, P], F32))
        with stage(nc, "first_onehot second_onehot gated block_used tokens_done copied stored_0 stored_1") as (
                block, first_hot, second_hot, gated, used, tokens_done, copied, stored_0, stored_1):
            stored = [stored_0, stored_1]

            @block.vector
            def _(dve):
                for tb in range(TT):
                    def pair(i, tb=tb):
                        for u in range(2):
                            n = tb * per_block + 2 * i + u
                            at = bass.ds(n * ONEHOT, ONEHOT)
                            if tb or not isinstance(i, int):
                                dve.wait_ge(used, n - 1)
                            nc.vector.tensor_tensor(a_[:, u], bc(first[:, at], PK), iota_b, ALU.is_equal).then_inc(first_hot, 1)
                            nc.vector.tensor_tensor(b_[:, u], bc(second[:, at], PK), iota_b, ALU.is_equal).then_inc(second_hot, 1)
                    pair(0)
                    with dve.Fori(1, per_block // 2) as i:
                        pair(i)

            @block.gpsimd
            def _(pool):
                for tb in range(TT):
                    with pool.Fori(0, per_block // 2) as i:
                        for u in range(2):
                            n = tb * per_block + 2 * i + u
                            pool.wait_ge(first_hot, n + 1)
                            nc.gpsimd.tensor_tensor(a_[:, u], a_[:, u], bc(gateT[:, bass.ds(n * ONEHOT, ONEHOT)], PK),
                                                    ALU.mult).then_inc(gated, 1)

            @block.tensor
            def _(pe):
                for tb in range(TT):
                    def pair(i, tb=tb):
                        for u in range(2):
                            n = tb * per_block + 2 * i + u
                            pe.wait_ge(second_hot, n + 1)
                            pe.wait_ge(gated, n + 1)
                            for k in range(ONEHOT):
                                bank = u * 4 + k // 4
                                if k % 4 == 0 and (tb or not isinstance(i, int)):
                                    pe.wait_ge(copied, 4 * n + k // 4 - 7)
                                last = nc.tensor.matmul(banks[bank][:, (k % 4) * P:(k % 4 + 1) * P], b_[:, u, k, :], a_[:, u, k, :],
                                                        start=True, stop=True)
                                if k % 4 == 3 and k < ONEHOT - 1:
                                    last.then_inc(tokens_done, 1)
                            last.then_inc(used, 1)
                    pair(0)
                    with pe.Fori(1, per_block // 2) as i:
                        pair(i)

            @block.scalar
            def _(act):
                for tb in range(TT):
                    if tb >= 2:
                        act.wait_ge(stored[tb % 2], 64)
                    with act.Fori(0, per_block // 2) as i:
                        for u in range(2):
                            n = tb * per_block + 2 * i + u
                            for q in range(4):
                                if q < 3:
                                    act.wait_ge(tokens_done, 3 * n + q + 1)
                                else:
                                    act.wait_ge(used, n + 1)
                                nc.scalar.copy(G[:, tb % 2, :, bass.ds((2 * i + u) * ONEHOT + 4 * q, 4)],
                                               banks[u * 4 + q].rearrange("p (t i) -> p i t", i=PK)).then_inc(copied, 1)

            @block.sync
            def _(sp):
                for tb in range(TT):
                    sp.wait_ge(copied, 4 * per_block * (tb + 1))
                    for part in range(4):
                        r = slice(32 * part, 32 * part + 32)
                        sp.dma_start(dram["gates"][r, :, tb * P:(tb + 1) * P].rearrange("i j t -> j i t"),
                                     G[:, tb % 2, r, :]).then_inc(stored[tb % 2], 16)
                sp.wait_ge(stored_0, 128)
                sp.wait_ge(stored_1, 128)


def split(nc, name, chunks, x, high, low):
    with stage(nc, f"{name}_high {name}_low") as (block, highs, lows):
        @block.scalar
        def _(act):
            for c in range(chunks):
                nc.scalar.copy(high(c), x(c)).then_inc(highs, 1)

        @block.vector
        def _(dve):
            for c in range(chunks):
                dve.wait_ge(highs, c + 1)
                nc.vector.tensor_tensor(low(c), x(c), high(c).bitcast(F32), ALU.subtract).then_inc(lows, 1)


def product(nc, out, w_high, w_low, x_high, x_low, start, stop):
    nc.tensor.matmul(out, w_high, x_high, start=start, stop=False)
    nc.tensor.matmul(out, w_high, x_low, start=False, stop=False)
    return nc.tensor.matmul(out, w_low, x_high, start=False, stop=stop)


def stream_experts(nc, dram, hT, xnT, scratch, ring, banks):
    groups = PK // GROUP
    with ExitStack() as held:
        def sb(name, shape, dt=F32):
            return held.enter_context(nc.sbuf_tensor(name, shape, dt))
        xH = sb("xn_high", [P, DC, T], F32R)
        xL = sb("xn_low", [P, DC, T], F32R)
        uH = sb("in_high", [P, 2, D], F32R)
        uL = sb("in_low", [P, 2, D], F32R)
        vH = sb("out_high", [P, GROUP, D], F32R)
        vL = sb("out_low", [P, GROUP, D], F32R)
        aH = sb("act_high", [P, 2 * GROUP, T], F32R)
        aL = sb("act_low", [P, 2 * GROUP, T], F32R)
        split(nc, "xn", DC, lambda c: xnT[:, c, :], lambda c: xH[:, c, :], lambda c: xL[:, c, :])
        G = xnT[:, 0:GROUP, :]
        A = xnT[:, GROUP:2 * GROUP, :]
        U = ring
        V = scratch[:].rearrange("p (s two) n -> p s (two n)", two=2)
        names = [f"{k}{u}_loaded" for k in ("in", "out", "gate") for u in range(GROUP)]
        with stage(nc, "in_high_ready in_low_ready out_high_ready out_low_ready dots_done activated gated "
                       "act_high_ready act_low_ready summed added " + " ".join(names)) as (
                block, in_high, in_low, out_high, out_low, dots, activated, gated, act_high, act_low, summed, added, *loads):
            u_in, v_in, g_in = loads[0:4], loads[4:8], loads[8:12]

            def pairs(eng, body):
                body(0, 0)
                body(1, 1)
                with eng.Fori(1, groups // 2) as k:
                    body(2 * k, 0)
                    body(2 * k + 1, 1)

            def is_first(g):
                return isinstance(g, int) and g == 0

            @block.sync
            def _(sp):
                def load_out(g):
                    for u in range(GROUP):
                        if not is_first(g):
                            sp.wait_ge(out_low, GROUP * (g - 1) + u + 1)
                        sp.dma_start(V[:, u, :], row(dram["peer_v"], g * GROUP + u)).then_inc(v_in[u], 16)

                def body(g, half):
                    for u in range(GROUP):
                        if not is_first(g):
                            sp.wait_ge(in_low, GROUP * (g - 1) + u + 1)
                        sp.dma_start(U[:, u, :], row(dram["peer_u"], g * GROUP + u)).then_inc(u_in[u], 16)
                        if not is_first(g):
                            sp.wait_ge(gated, GROUP * (g - 1) + u + 1)
                        sp.dma_start(G[:, u, :], row(dram["gates"], g * GROUP + u)).then_inc(g_in[u], 16)
                    if is_first(g):
                        return
                    load_out(g - 1)
                pairs(sp, body)
                load_out(groups - 1)

            @block.scalar
            def _(act):
                def split_in(n, g, u, first):
                    act.wait_ge(u_in[u], 16 * (g + 1))
                    if not first:
                        act.wait_ge(dots, n - 1)
                    nc.scalar.copy(uH[:, u % 2, :], U[:, u, :]).then_inc(in_high, 1)

                def split_out(g, u):
                    act.wait_ge(v_in[u], 16 * (g + 1))
                    if not is_first(g):
                        act.wait_ge(summed, DC * g)
                    nc.scalar.copy(vH[:, u, :], V[:, u, :]).then_inc(out_high, 1)

                def body(g, half, last=False):
                    for u in range(GROUP):
                        n = g * GROUP + u
                        if not is_first(g):
                            split_out(g - 1, u)
                        act.wait_ge(dots, n + 1)
                        if not is_first(g):
                            act.wait_ge(act_low, n - GROUP + 1)
                        nc.scalar.activation(A[:, u, :], banks[u % 2], ACT.Gelu).then_inc(activated, 1)
                        if not (last and u >= 2):
                            split_in(n + 2, g + (u + 2) // GROUP, (u + 2) % GROUP, False)
                split_in(0, 0, 0, True)
                split_in(1, 0, 1, True)
                body(0, 0)
                body(1, 1)
                with act.Fori(1, groups // 2 - 1) as k:
                    body(2 * k, 0)
                    body(2 * k + 1, 1)
                body(groups - 2, 0)
                body(groups - 1, 1, last=True)
                for u in range(GROUP):
                    split_out(groups - 1, u)

            @block.gpsimd
            def _(pool):
                def split_in(n, u):
                    pool.wait_ge(in_high, n + 1)
                    nc.gpsimd.tensor_tensor(uL[:, u % 2, :], U[:, u, :], uH[:, u % 2, :].bitcast(F32), ALU.subtract)\
                        .then_inc(in_low, 1)

                def split_out(g, u):
                    pool.wait_ge(out_high, g * GROUP + u + 1)
                    nc.gpsimd.tensor_tensor(vL[:, u, :], V[:, u, :], vH[:, u, :].bitcast(F32), ALU.subtract)\
                        .then_inc(out_low, 1)

                def body(g, half, last=False):
                    for u in range(GROUP):
                        if not is_first(g):
                            split_out(g - 1, u)
                        if not (last and u >= 2):
                            split_in(g * GROUP + u + 2, (u + 2) % GROUP)
                split_in(0, 0)
                split_in(1, 1)
                body(0, 0)
                body(1, 1)
                with pool.Fori(1, groups // 2 - 1) as k:
                    body(2 * k, 0)
                    body(2 * k + 1, 1)
                body(groups - 2, 0)
                body(groups - 1, 1, last=True)
                for u in range(GROUP):
                    split_out(groups - 1, u)

            @block.tensor
            def _(pe):
                def dot(g, half):
                    for u in range(GROUP):
                        n = g * GROUP + u
                        pe.wait_ge(in_low, n + 1)
                        if u >= 2 or not is_first(g):
                            pe.wait_ge(activated, n - 1)
                        for c in range(DC):
                            w = slice(c * P, (c + 1) * P)
                            last = product(nc, banks[u % 2], uH[:, u % 2, w], uL[:, u % 2, w], xH[:, c, :], xL[:, c, :],
                                           c == 0, c == DC - 1)
                        last.then_inc(dots, 1)

                def combine(g, half):
                    for d in range(DC):
                        if d == 0:
                            pe.wait_ge(act_low, GROUP * (g + 1))
                            pe.wait_ge(out_low, GROUP * (g + 1))
                        if d >= 4 or not is_first(g):
                            pe.wait_ge(added, g * DC + d - 3)
                        for u in range(GROUP):
                            w = slice(d * P, (d + 1) * P)
                            s = half * GROUP + u
                            last = product(nc, banks[2 + d % 4], vH[:, u, w], vL[:, u, w], aH[:, s, :], aL[:, s, :],
                                           u == 0, u == GROUP - 1)
                        last.then_inc(summed, 1)

                dot(0, 0)
                dot(1, 1)
                combine(0, 0)
                with pe.Fori(1, groups // 2) as k:
                    dot(2 * k, 0)
                    combine(2 * k - 1, 1)
                    dot(2 * k + 1, 1)
                    combine(2 * k, 0)
                combine(groups - 1, 1)

            @block.vector
            def _(dve):
                def weigh(g, half):
                    for u in range(GROUP):
                        n = g * GROUP + u
                        s = half * GROUP + u
                        dve.wait_ge(activated, n + 1)
                        dve.wait_ge(g_in[u], 16 * (g + 1))
                        nc.vector.tensor_tensor(A[:, u, :], A[:, u, :], G[:, u, :], ALU.mult).then_inc(gated, 1)
                        if not isinstance(g, int):
                            dve.wait_ge(summed, DC * (g - 1))
                        dve.wait_ge(gated, n + 1)
                        nc.vector.tensor_copy(aH[:, s, :], A[:, u, :]).then_inc(act_high, 1)
                        dve.wait_ge(act_high, n + 1)
                        nc.vector.tensor_tensor(aL[:, s, :], A[:, u, :], aH[:, s, :].bitcast(F32), ALU.subtract).then_inc(act_low, 1)

                def add(g, half):
                    for d in range(DC):
                        dve.wait_ge(summed, g * DC + d + 1)
                        if not is_first(g):
                            dve.wait_ge(added, g * DC + d + 1 - DC)
                        nc.vector.tensor_tensor(hT[:, d, :], hT[:, d, :], banks[2 + d % 4], ALU.add).then_inc(added, 1)

                weigh(0, 0)
                weigh(1, 1)
                add(0, 0)
                with dve.Fori(1, groups // 2) as k:
                    weigh(2 * k, 0)
                    add(2 * k - 1, 1)
                    weigh(2 * k + 1, 1)
                    add(2 * k, 0)
                add(groups - 1, 1)



CONST = dict(neg128=(0, 128), neg64=(128, 128), strict64=(256, 128), level=(384, 768), causal=(1152, 512), inv_freq=(1664, 1))
CONST_N = 1665
VEC2 = dict(norm1=(0, 8), conv_ssd=(8, 48), conv_ssd_b=(56, 12), small_b=(68, 1), a_log=(69, 1), ssd_d=(70, 8),
            ssd_g=(78, 8), mla_q_g=(86, 4), mla_kv_g=(90, 2), conv_gdn=(92, 64), gdn_g=(156, 1), norm2=(157, 8))
VEC2_N = 165
DT_ROWS, BETA_ROWS, A_ROWS = 0, 32, 64
SSD_HEADS, GDN_HEADS = 16, 8
GDN_SCALE = 128 ** -0.5


def rope_tables(nc, dram, const, cosT, sinT, scratch):
    turns_int = scratch[:, 3, :].bitcast(I32)
    pos = scratch[:, 0, :].bitcast(I32)
    ang, turns, tmp = scratch[:, 1, :], scratch[:, 2, :], scratch[:, 4, :]
    with stage(nc, "positions_loaded reduced sines_done dve_step") as (block, loaded, reduced, sines, dve_step):
        @block.sync
        def _(sp):
            sp.dma_start(const[:], dram["consts"]).then_inc(loaded, 16)
            sp.dma_start(pos, dram["positions"]).then_inc(loaded, 16)

        @block.vector
        def _(dve):
            link = Chain(dve, dve_step)
            dve.wait_ge(loaded, 32)
            link(nc.vector.tensor_copy(ang, pos))
            link(nc.vector.tensor_scalar(ang, ang, const[:, CONST["inv_freq"][0]:CONST["inv_freq"][0] + 1], None, ALU.mult))
            sine(nc, link, ang, turns, turns_int, sinT, cosT).then_inc(reduced, 1)
            dve.wait_ge(sines, 2)
            double_angle(nc, link, sinT, cosT, tmp)

        @block.scalar
        def _(act):
            act.wait_ge(reduced, 1)
            nc.scalar.activation(sinT, sinT, ACT.Sin).then_inc(sines, 1)
            nc.scalar.activation(cosT, cosT, ACT.Sin).then_inc(sines, 1)


def causal_conv(nc, name, xp, chunks, weight, bias, acc):
    with stage(nc, f"{name}_tap {name}_summed {name}_activated") as (block, tap, summed, activated):
        @block.vector
        def _(dve):
            n = 0
            for c in range(chunks):
                a = acc[c % 2]
                if c >= 2:
                    dve.wait_ge(activated, c - 1)
                if bias is None:
                    nc.vector.tensor_scalar(a, xp[:, c, 3:3 + T], weight(c, 3), None, ALU.mult).then_inc(tap, 1)
                else:
                    nc.vector.tensor_scalar(a, xp[:, c, 3:3 + T], weight(c, 3), bias(c), ALU.mult, ALU.add).then_inc(tap, 1)
                for k in (2, 1, 0):
                    n += 1
                    dve.wait_ge(tap, n)
                    last = nc.vector.scalar_tensor_tensor(a, xp[:, c, k:k + T], weight(c, k), a, ALU.mult, ALU.add)
                    last.then_inc(tap if k else summed, 1)

        @block.scalar
        def _(act):
            for c in range(chunks):
                act.wait_ge(summed, c + 1)
                nc.scalar.activation(xp[:, c, 0:T], acc[c % 2], ACT.Silu).then_inc(activated, 1)


def second_block(nc, dram, psum, hT, xnT, scratch, ring, rstd, ones, ident, upto=None):
    banks = [psum[:, b, :] for b in range(8)]
    with ExitStack() as held:
        def sb(name, shape, dt=F32):
            return held.enter_context(nc.sbuf_tensor(name, shape, dt))
        const = sb("consts_sb", [P, CONST_N])
        cosT = sb("cosT", [P, T])
        sinT = sb("sinT", [P, T])
        vec = sb("vec2", [P, VEC2_N])
        small = sb("small", [P, T])
        cum = sb("cum", [P, T])
        smallN = sb("smallN", [P, TT, P])
        cumN = sb("cumN", [P, TT, P])
        rope_tables(nc, dram, const, cosT[:], sinT[:], scratch)

        def col(name, k=0):
            return vec[:, VEC2[name][0] + k:VEC2[name][0] + k + 1]

        def cst(name, k=0, n=None):
            a, w = CONST[name]
            return const[:, a + k:a + (k + n if n else w)]

        def xn(c):
            return xnT[:, c, :]

        def into(dst, chunk0=0, func=None):
            def write(nc, f, ps):
                tile = dst[:, bass.ds(f + chunk0, 1), 0:T].squeeze(1)
                return nc.scalar.copy(tile, ps) if func is None else nc.scalar.activation(tile, ps, func)
            return write

        with nc.Fori(0, LAYERS if upto == "final" else 1) as layer:
            with stage(nc, "vec_loaded") as (block, loaded):
                @block.sync
                def _(sp):
                    sp.dma_start(vec[:], row(dram["vec2"], layer)).then_inc(loaded, 16)
                    sp.wait_ge(loaded, 16)
            rmsnorm(nc, "norm1", lambda c: hT[:, c, :], xn, DC, DC, ones, D, lambda c: col("norm1", c),
                    lambda c: scratch[:, c, :], rstd, banks)
            narrow_rows(nc, dram, layer, xn, small, cum, smallN, cumN, col, ones, ring, banks, ident, scratch)

            with ExitStack() as mix:
                yT = mix.enter_context(nc.sbuf_tensor("branch_y", [P, 8, T], F32))

                def branch_out(name, n, mixT, add):
                    linear(nc, f"{name}_gate", dram["w_gate"], layer * 24 + 8 * n, 8, xn, DC, ring, banks, "scalar",
                           into(scratch, func=ACT.Sigmoid))

                    def write(nc, f, ps):
                        gate = scratch[:, bass.ds(f, 1), :].squeeze(1)
                        return nc.vector.tensor_tensor(gate if add else mixT[:, bass.ds(f, 1), :].squeeze(1), gate, ps, ALU.mult)
                    linear(nc, f"{name}_out", dram[f"w_{name}_out"], layer * 8, 8, lambda c: yT[:, c, :], DC, ring, banks,
                           "vector", write)
                    if add:
                        with stage(nc, f"{name}_added") as (block, added):
                            @block.vector
                            def _(dve):
                                for c in range(4):
                                    nc.vector.tensor_tensor(mixT[:, c, :], mixT[:, c, :], scratch[:, c, :], ALU.add)

                            @block.gpsimd
                            def _(pool):
                                for c in range(4, 8):
                                    nc.gpsimd.tensor_tensor(mixT[:, c, :], mixT[:, c, :], scratch[:, c, :], ALU.add)

                delta_rule(nc, dram, layer, xn, yT, small, cum, smallN, cumN, col, cst, ones, ring, banks, ident, scratch, rstd, into)
                if upto == "yg0":
                    return copy_out(nc, yT, hT)
                mixT = mix.enter_context(nc.sbuf_tensor("mixed", [P, 8, T], F32))
                branch_out("gdn", 2, mixT, False)
                latent_attention(nc, dram, layer, xn, yT, col, cst, ones, ring, banks, ident, scratch, rstd, into, cosT, sinT)
                if upto == "ym0":
                    return copy_out(nc, yT, hT)
                branch_out("mla", 1, mixT, True)
                duality(nc, dram, layer, xn, yT, small, cum, smallN, cumN, col, cst, ones, ring, banks, ident, scratch, rstd, into)
                if upto == "ys0":
                    return copy_out(nc, yT, hT)
                branch_out("ssd", 0, mixT, True)
                linear(nc, "w_mix", dram["w_mix"], layer * 8, 8, lambda c: mixT[:, c, :], DC, ring, banks, "vector",
                       lambda nc, f, ps: add_to(nc, hT, f, ps))
            rmsnorm(nc, "norm2", lambda c: hT[:, c, :], xn, DC, DC, ones, D, lambda c: col("norm2", c),
                    lambda c: scratch[:, c, :], rstd, banks)
            with ExitStack() as mlp:
                up = mlp.enter_context(nc.sbuf_tensor("up", [P, 32, T], F32))
                linear(nc, "w_up", dram["w_up"], layer * 32, 32, xn, DC, ring, banks, "scalar", into(up, func=ACT.Relu),
                       post=lambda nc, f: nc.vector.tensor_tensor(up[:, bass.ds(f, 1), :].squeeze(1), up[:, bass.ds(f, 1), :].squeeze(1),
                                                                  up[:, bass.ds(f, 1), :].squeeze(1), ALU.mult))
                linear(nc, "w_down", dram["w_down"], layer * 32, 8, lambda c: up[:, c, :], DC, ring, banks, "vector",
                       lambda nc, f, ps: add_to(nc, hT, f, ps), pieces=4)


def copy_out(nc, src, dst):
    with stage(nc, "copied_out") as (block, s):
        @block.vector
        def _(dve):
            nc.vector.tensor_copy(dst[:], src[:])


def narrow_rows(nc, dram, layer, xn, small, cum, smallN, cumN, col, ones, ring, banks, ident, scratch):
    x, neg_abs, e, rate = scratch[:, 0, :], scratch[:, 1, :], scratch[:, 2, :], scratch[:, 3, 0:1]
    with stage(nc, "w_loaded projected shifted magnitude logs rates beta_ready dve_step rows_ready turned copied") as (
            block, loaded, projected, shifted, magnitude, logs, rates, beta, dve_step, rows_ready, turned, copied):
        @block.sync
        def _(sp):
            sp.dma_start(ring[:, 0, :], row(dram["w_narrow"], layer)).then_inc(loaded, 16)

        @block.tensor
        def _(pe):
            pe.wait_ge(loaded, 16)
            for c in range(DC):
                last = nc.tensor.matmul(banks[0], ring[:, 0, c * P:(c + 1) * P], xn(c), start=(c == 0), stop=(c == DC - 1))
            last.then_inc(projected, 1)
            pe.wait_ge(rows_ready, 1)
            for n, src in enumerate((small, cum)):
                for t in range(TT):
                    last = nc.tensor.transpose(banks[2 + n][:, t * P:(t + 1) * P], src[:, t * P:(t + 1) * P], ident)
                last.then_inc(turned, 1)

        @block.scalar
        def _(act):
            act.wait_ge(shifted, 1)
            nc.scalar.activation(small[32:64, :], x[32:64, :], ACT.Sigmoid).then_inc(beta, 1)
            act.wait_ge(shifted, 2)
            nc.scalar.activation(e, neg_abs, ACT.Exp).then_inc(magnitude, 1)
            nc.scalar.activation(rate, col("a_log"), ACT.Exp).then_inc(rates, 1)
            act.wait_ge(magnitude, 1)
            nc.scalar.activation(e, e, ACT.Ln, bias=1.0).then_inc(logs, 1)
            for n, dst in enumerate((smallN, cumN)):
                act.wait_ge(turned, n + 1)
                nc.scalar.copy(dst[:].rearrange("p a b -> p (a b)"), banks[2 + n]).then_inc(copied, 1)

        @block.vector
        def _(dve):
            v = nc.vector
            link = Chain(dve, dve_step)
            dve.wait_ge(projected, 1)
            v.tensor_scalar(x, banks[0], col("small_b"), None, ALU.add).then_inc(shifted, 1)
            dve.wait_ge(shifted, 1)
            link(v.tensor_scalar(neg_abs, x, -1.0, None, ALU.mult))
            v.tensor_tensor(neg_abs, x, neg_abs, ALU.min).then_inc(shifted, 1)
            link(v.memset(cum[:], 0.0))
            dve.wait_ge(rates, 1)
            dve.wait_ge(logs, 1)
            dve.wait_ge(beta, 1)
            link(v.scalar_tensor_tensor(x, x, 0.0, e, ALU.max, ALU.add))
            v.tensor_copy(small[0:32, :], x[0:32, :])
            v.tensor_copy(small[64:128, :], x[64:128, :])
            link(v.tensor_scalar(e, x, rate, -1.0, ALU.mult, ALU.mult))
            for t in range(TT):
                s = slice(t * P, (t + 1) * P)
                v.tensor_tensor_scan(cum[0:32, s], ones[0:32, :], e[0:32, s], 0.0, ALU.mult, ALU.add)
            for t in range(2 * TT):
                s = slice(t * 64, (t + 1) * 64)
                last = v.tensor_tensor_scan(cum[64:96, s], ones[64:96, 0:64], e[64:96, s], 0.0, ALU.mult, ALU.add)
            last.then_inc(rows_ready, 1)


def spread_row(nc, bank, src, base, h, ident):
    rows = slice(base, base + 32)
    return nc.tensor.matmul(bank, ident[rows, base + h:base + h + 1].to_broadcast([32, P]), src[rows, :], start=True, stop=True)


def wide(ap):
    return ap.unsqueeze(1).to_broadcast([ap.shape[0], TT, P])


def tiles4(bank):
    return bank.rearrange("p (t n) -> p t n", n=P)


def duality(nc, dram, layer, xn, yT, small, cum, smallN, cumN, col, cst, ones, ring, banks, ident, scratch, rstd, into):
    with ExitStack() as held:
        def sb(name, shape, dt=F32):
            return held.enter_context(nc.sbuf_tensor(name, shape, dt))
        xp = sb("ssd_xbc", [P, 12, T + 3])
        with stage(nc, "ssd_zeroed") as (block, zeroed):
            @block.vector
            def _(dve):
                nc.vector.memset(xp[:, :, 0:3], 0.0)
        linear(nc, "ssd_xbc_in", dram["w_ssd_xbc"], layer * 12, 12, xn, DC, ring, banks, "scalar",
               lambda nc, f, ps: nc.scalar.copy(xp[:, bass.ds(f, 1), 3:T + 3].squeeze(1), ps))
        causal_conv(nc, "ssd_conv", xp, 12, lambda c, k: col("conv_ssd", 4 * c + k), lambda c: col("conv_ssd_b", c),
                    [scratch[:, 0, :], scratch[:, 1, :]])
        xdt = sb("ssd_xdt", [P, TT, D])
        xdd = sb("ssd_xdd", [P, 3, D])
        Bn = sb("ssd_Bn", [P, 2, TT, P])
        CBT = sb("ssd_CBT", [P, 2, TT, P])
        H = sb("ssd_H", [P, 3, D])
        last_cum = sb("ssd_last", [P, SSD_HEADS, TT])
        state_decay = sb("ssd_state_decay", [P, SSD_HEADS, TT])
        decay_end = sb("ssd_decay_end", [P, TT, SSD_HEADS])
        with stage(nc, "turned scaled b_turned b_copied cb_done cb_copied row_spread last_copied exps dve_step ends_ready") as (
                block, turned, scaled, b_turned, b_copied, cb_done, cb_copied, spread, last_copied, exps, dve_step, ends):
            @block.tensor
            def _(pe):
                for j in range(8):
                    t, half = divmod(j, 2)
                    if j >= 2:
                        pe.wait_ge(scaled, j - 1)
                    for k in range(4):
                        last = nc.tensor.transpose(banks[j % 2][:, k * P:(k + 1) * P], xp[:, 4 * half + k, t * P:(t + 1) * P], ident)
                    last.then_inc(turned, 1)
                for g in range(2):
                    for t in range(TT):
                        last = nc.tensor.transpose(banks[2 + g][:, t * P:(t + 1) * P], xp[:, 8 + g, t * P:(t + 1) * P], ident)
                    last.then_inc(b_turned, 1)
                    for t in range(TT):
                        s = slice(t * P, (t + 1) * P)
                        last = nc.tensor.matmul(banks[4 + g][:, s], xp[:, 8 + g, s], xp[:, 10 + g, s], start=True, stop=True)
                    last.then_inc(cb_done, 1)
                for h in range(SSD_HEADS):
                    if h >= 2:
                        pe.wait_ge(last_copied, h - 1)
                    spread_row(nc, banks[6 + h % 2], cum, DT_ROWS, h, ident).then_inc(spread, 1)

            @block.scalar
            def _(act):
                for g in range(2):
                    act.wait_ge(b_turned, g + 1)
                    nc.scalar.copy(Bn[:, g], tiles4(banks[2 + g])).then_inc(b_copied, 1)
                    act.wait_ge(cb_done, g + 1)
                    nc.scalar.copy(CBT[:, g], tiles4(banks[4 + g])).then_inc(cb_copied, 1)
                for h in range(SSD_HEADS):
                    act.wait_ge(spread, h + 1)
                    nc.scalar.copy(last_cum[:, h, :], tiles4(banks[6 + h % 2])[:, :, P - 1:P].squeeze(2)).then_inc(last_copied, 1)
                act.wait_ge(last_copied, SSD_HEADS)
                nc.scalar.activation(state_decay[:], last_cum[:], ACT.Exp).then_inc(exps, 1)
                act.wait_ge(ends, 1)
                nc.scalar.activation(decay_end[:], decay_end[:], ACT.Exp).then_inc(exps, 1)

            @block.vector
            def _(dve):
                v = nc.vector
                link = Chain(dve, dve_step)
                for j in range(8):
                    t, half = divmod(j, 2)
                    dve.wait_ge(turned, j + 1)
                    v.tensor_tensor(xdt[:, t, 512 * half:512 * half + 512].rearrange("p (h d) -> p h d", d=64),
                                    banks[j % 2].rearrange("p (h d) -> p h d", d=64),
                                    bc(smallN[:, t, 8 * half:8 * half + 8], 64), ALU.mult).then_inc(scaled, 1)
                dve.wait_ge(last_copied, SSD_HEADS)
                v.tensor_tensor(decay_end[:], last_cum[:].rearrange("p h t -> p t h"), cumN[:, :, 0:SSD_HEADS], ALU.subtract)\
                    .then_inc(ends, 1)
                dve.wait_ge(exps, 2)
                dve.wait_ge(scaled, 8)
                for t in range(3):
                    link(v.tensor_tensor(xdd[:, t, :].rearrange("p (h d) -> p h d", d=64),
                                         xdt[:, t, :].rearrange("p (h d) -> p h d", d=64), bc(decay_end[:, t, :], 64), ALU.mult))
        with stage(nc, "states_done dve_step") as (block, done, dve_step):
            @block.tensor
            def _(pe):
                for t in range(3):
                    for g in range(2):
                        nc.tensor.matmul(banks[2 * t + g], Bn[:, g, t, :], xdd[:, t, 512 * g:512 * g + 512],
                                         start=True, stop=True).then_inc(done, 1)

            @block.vector
            def _(dve):
                v = nc.vector
                link = Chain(dve, dve_step)
                for t in range(3):
                    for g in range(2):
                        dve.wait_ge(done, 2 * t + g + 1)
                        s = slice(512 * g, 512 * g + 512)
                        if t == 0:
                            link(v.tensor_copy(H[:, 0, s], banks[g]))
                        else:
                            link(v.tensor_tensor(H[:, t, s].rearrange("p (h d) -> p h d", d=64),
                                                 H[:, t - 1, s].rearrange("p (h d) -> p h d", d=64),
                                                 bc(state_decay[:, 8 * g:8 * g + 8, t], 64), ALU.mult))
                            link(v.tensor_tensor(H[:, t, s], H[:, t, s], banks[2 * t + g], ALU.add))
        L = sb("ssd_L", [P, 2, T])
        CE = sb("ssd_CE", [P, 2, T])
        with stage(nc, "row_spread differences masked exps weighted c_scaled y_done y_stored") as (
                block, spread, differences, masked, exps, weighted, c_scaled, y_done, y_stored):
            @block.tensor
            def _(pe):
                def row_of(h):
                    if h >= 2:
                        pe.wait_ge(exps, 2 * (h - 1))
                    spread_row(nc, banks[h % 2], cum, DT_ROWS, h, ident).then_inc(spread, 1)
                row_of(0)
                for h in range(SSD_HEADS):
                    if h + 1 < SSD_HEADS:
                        row_of(h + 1)
                    out = banks[2 + (h // 2) % 2][64 * (h % 2):64 * (h % 2) + 64, :]
                    pe.wait_ge(weighted, h + 1)
                    pe.wait_ge(c_scaled, h + 1)
                    if h % 2 == 0 and h >= 4:
                        pe.wait_ge(y_stored, h // 2 - 1)
                    for t in range(TT):
                        s = slice(t * P, (t + 1) * P)
                        last = nc.tensor.matmul(out[:, s], xdt[:, t, 64 * h:64 * h + 64], L[:, h % 2, s], start=True, stop=(t == 0))
                        if t:
                            last = nc.tensor.matmul(out[:, s], H[:, t - 1, 64 * h:64 * h + 64], CE[:, h % 2, s], start=False, stop=True)
                    last.then_inc(y_done, 1)

            @block.vector
            def _(dve):
                v = nc.vector

                def finish(c):
                    dve.wait_ge(y_done, 2 * c + 2)
                    v.scalar_tensor_tensor(yT[:, c, :], xp[:, c, 0:T], col("ssd_d", c), banks[2 + c % 2], ALU.mult, ALU.add)\
                        .then_inc(y_stored, 1)

                def differ(h):
                    dve.wait_ge(spread, h + 1)
                    if h >= 2:
                        dve.wait_ge(y_done, h - 1)
                    v.tensor_tensor(tiles4(L[:, h % 2]), tiles4(banks[h % 2]), cumN[:, :, h:h + 1].to_broadcast([P, TT, P]),
                                    ALU.subtract).then_inc(differences, 1)
                    dve.wait_ge(differences, h + 1)
                    v.tensor_tensor(tiles4(L[:, h % 2]), tiles4(L[:, h % 2]), wide(cst("neg128")), ALU.add).then_inc(masked, 1)

                differ(0)
                for h in range(SSD_HEADS):
                    if h + 1 < SSD_HEADS:
                        differ(h + 1)
                    dve.wait_ge(exps, 2 * h + 2)
                    v.tensor_tensor(tiles4(L[:, h % 2]), tiles4(L[:, h % 2]), CBT[:, h // 8], ALU.mult).then_inc(weighted, 1)
                    if h % 2 == 1 and h >= 3:
                        finish(h // 2 - 1)
                finish(7)

            @block.scalar
            def _(act):
                for h in range(SSD_HEADS):
                    act.wait_ge(differences, h + 1)
                    if h >= 2:
                        act.wait_ge(y_done, h - 1)
                    nc.scalar.activation(CE[:, h % 2, :], banks[h % 2], ACT.Exp).then_inc(exps, 1)
                    act.wait_ge(masked, h + 1)
                    nc.scalar.activation(L[:, h % 2, :], L[:, h % 2, :], ACT.Exp).then_inc(exps, 1)

            @block.gpsimd
            def _(pool):
                for h in range(SSD_HEADS):
                    pool.wait_ge(exps, 2 * h + 1)
                    nc.gpsimd.tensor_tensor(CE[:, h % 2, :], CE[:, h % 2, :], xp[:, 10 + h // 8, 0:T], ALU.mult).then_inc(c_scaled, 1)
    gate_and_norm(nc, "ssd", dram["w_ssd_z"], layer, xn, yT, True, 4, 512, lambda c: col("ssd_g", c), ones, ring, banks, scratch, rstd, into)


def gate_and_norm(nc, name, w_z, layer, xn, yT, gate_first, group, width, gain, ones, ring, banks, scratch, rstd, into):
    def norm():
        rmsnorm(nc, f"{name}_norm", lambda c: yT[:, c, :], lambda c: yT[:, c, :], 8, group, ones, width, gain,
                lambda c: scratch[:, c, :], rstd, banks)
    if not gate_first:
        norm()
    linear(nc, f"{name}_z", w_z, layer * 8, 8, xn, DC, ring, banks, "scalar", into(scratch, func=ACT.Silu),
           post=lambda nc, f: nc.vector.tensor_tensor(yT[:, bass.ds(f, 1), :].squeeze(1), yT[:, bass.ds(f, 1), :].squeeze(1),
                                                      scratch[:, bass.ds(f, 1), :].squeeze(1), ALU.mult))
    if gate_first:
        norm()


def latent_attention(nc, dram, layer, xn, yT, col, cst, ones, ring, banks, ident, scratch, rstd, into, cosT, sinT):
    with ExitStack() as held:
        def sb(name, shape, dt=F32):
            return held.enter_context(nc.sbuf_tensor(name, shape, dt))
        q = sb("mla_q", [P, 12, T])
        kn = sb("mla_k", [P, 8, T])
        vals = sb("mla_v", [P, TT, D])
        c8 = sb("mla_c", [P, 8, T])
        linear(nc, "mla_in", dram["w_mla_in"], layer * 8, 8, xn, DC, ring, banks, "scalar", into(c8))
        rmsnorm(nc, "mla_norm_q", lambda c: c8[:, c, :], lambda c: c8[:, c, :], 4, 4, ones, 512, lambda c: col("mla_q_g", c),
                lambda c: scratch[:, c, :], rstd, banks)
        rmsnorm(nc, "mla_norm_kv", lambda c: c8[:, 4 + c, :], lambda c: c8[:, 4 + c, :], 2, 2, ones, 256, lambda c: col("mla_kv_g", c),
                lambda c: scratch[:, c, :], rstd, banks)
        linear(nc, "mla_uq", dram["w_mla_uq"], layer * 12, 12, lambda c: c8[:, c, :], 4, ring, banks, "scalar", into(q))
        linear(nc, "mla_uk", dram["w_mla_uk"], layer * 8, 8, lambda c: c8[:, 4 + c, :], 2, ring, banks, "scalar", into(kn))
        for n in range(2):
            linear_tokens(nc, f"mla_uv{n}", dram["w_mla_uv"], layer * 2 + n, lambda c: c8[:, 4 + c, :], 2, ring, banks, TT,
                          lambda t, n=n: vals[:, t, n * 512:(n + 1) * 512])
        with stage(nc, "rotate_step rotate_step_pool pool_done") as (block, step, pool_step, pool_done):
            def rotate(eng, ops, sem, a, b, t0, t1):
                link = Chain(eng, sem)
                for x, y in zip(a, b):
                    link(ops.tensor_tensor(t0, x, sinT[:], ALU.mult))
                    link(ops.tensor_tensor(t1, y, sinT[:], ALU.mult))
                    link(ops.tensor_tensor(x, x, cosT[:], ALU.mult))
                    link(ops.tensor_tensor(x, x, t1, ALU.subtract))
                    link(ops.tensor_tensor(y, y, cosT[:], ALU.mult))
                    link(ops.tensor_tensor(y, y, t0, ALU.add))

            @block.vector
            def _(dve):
                rotate(dve, nc.vector, step, [q[:, 8, :], q[:, 9, :]], [q[:, 10, :], q[:, 11, :]], scratch[:, 0, :], scratch[:, 1, :])

            @block.gpsimd
            def _(pool):
                rotate(pool, nc.gpsimd, pool_step, [c8[:, 6, :]], [c8[:, 7, :]], scratch[:, 2, :], scratch[:, 3, :])
        sc = scratch[:, 4:6, :]
        pr = scratch[:, 6:8, :]
        pt = ring[:].rearrange("p s n -> p (s n)").rearrange("p (b k n) -> p b k n", b=2, k=4)
        stats = sb("mla_stats", [P, 8])

        def scores(h, qt):
            r = slice(32 * (h % 4), 32 * (h % 4) + 32)
            qs, ks = slice(qt * P, (qt + 1) * P), slice(0, (qt + 1) * P)
            return [(q[:, h, qs], kn[:, h, ks]), (q[r, 8 + h // 4, qs], c8[r, 6, ks]), (q[r, 10 + h // 4, qs], c8[r, 7, ks])]
        attention(nc, "latent", 8, scores, lambda qt: qt + 1, 192 ** -0.5, lambda h, qt: cst("causal", 384 - P * qt, P * (qt + 1)),
                  lambda h, k: vals[:, k, h * P:(h + 1) * P], P, lambda h: slice(0, P), lambda h: yT[:, h, :],
                  banks, sc, pr, pt, stats, ident)


def delta_rule(nc, dram, layer, xn, yT, small, cum, smallN, cumN, col, cst, ones, ring, banks, ident, scratch, rstd, into):
    B4 = 4
    with ExitStack() as held:
        def sb(name, shape, dt=F32):
            return held.enter_context(nc.sbuf_tensor(name, shape, dt))
        xp = sb("gdn_qkv", [P, 16, T + 3])
        with stage(nc, "gdn_zeroed") as (block, zeroed):
            @block.vector
            def _(dve):
                nc.vector.memset(xp[:, :, 0:3], 0.0)
        linear(nc, "gdn_qkv_in", dram["w_gdn_qkv"], layer * 16, 16, xn, DC, ring, banks, "scalar",
               lambda nc, f, ps: nc.scalar.copy(xp[:, bass.ds(f, 1), 3:T + 3].squeeze(1), ps))
        causal_conv(nc, "gdn_conv", xp, 16, lambda c, k: col("conv_gdn", 4 * c + k), None, [scratch[:, 0, :], scratch[:, 1, :]])
        rmsnorm(nc, "gdn_l2", lambda c: xp[:, c, 0:T], lambda c: xp[:, c, 0:T], 8, 1, ones, 1.0, None,
                lambda c: scratch[:, c, :], rstd, banks, mean=False)
        acT = sb("gdn_acT", [P, B4, TT, P])
        qg = sb("gdn_qg", [P, B4, T])
        kd = sb("gdn_kd", [P, B4, TT, P])
        uN = yT[:].rearrange("p c (t n) -> p c t n", n=P)[:, 0:4]
        wT = yT[:, 4:8, :]
        AT = scratch[:].rearrange("p c (t n) -> p c t n", n=P)[:, 0:4]
        Tn = scratch[:].rearrange("p c (t n) -> p c t n", n=P)[:, 4:8]
        Tt = sb("gdn_Tt", [P, B4, TT, P])
        vb = sb("gdn_vb", [P, B4, TT, P])
        kb = sb("gdn_kb", [P, B4, TT, P])
        ring4 = ring[:].rearrange("p s (a t n) -> p s a t n", t=TT, n=P)
        Dm = [ring4[:, 0, 0], ring4[:, 0, 1]]
        eg = [ring4[:, 1, 0], ring4[:, 1, 1]]
        am = [ring4[:, 2, 0], ring4[:, 2, 1]]
        Wb = [ring4[:, 3, 0], ring4[:, 3, 1]]
        S = sb("gdn_S", [P, B4, P])
        Sd = sb("gdn_Sd", [P, B4, P])
        vn = sb("gdn_vn", [P, B4, P])
        g_last = sb("gdn_last", [P, B4, 8])
        g_end = sb("gdn_end", [P, B4, TT])
        kbs = sb("gdn_kbs", [P, TT, B4])

        for hb in range(2):
            heads = [4 * hb + x for x in range(B4)]
            g0 = A_ROWS + 4 * hb
            b0 = BETA_ROWS + 4 * hb
            with stage(nc, "products_done differ masked exps ends_done dve_step banks_used ends_exp") as (
                    block, products, differ, masked, exps, ends, dve_step, used, ends_exp):
                @block.tensor
                def _(pe):
                    for x, h in enumerate(heads):
                        b = 4 * (x % 2)
                        if x >= 2:
                            pe.wait_ge(used, x - 1)
                        q_, k_ = xp[:, h // 2, :], xp[:, 4 + h // 2, :]
                        spread_row(nc, banks[b], cum, A_ROWS, h, ident)
                        spread_row(nc, banks[b + 1], small, BETA_ROWS, h, ident)
                        for n, r in ((2, q_), (3, k_)):
                            for t in range(TT):
                                s = slice(t * P, (t + 1) * P)
                                last = nc.tensor.matmul(banks[b + n][:, s], k_[:, s], r[:, s], start=True, stop=True)
                        last.then_inc(products, 1)

                @block.vector
                def _(dve):
                    v = nc.vector
                    link = Chain(dve, dve_step)
                    for x, h in enumerate(heads):
                        b = 4 * (x % 2)
                        dve.wait_ge(products, x + 1)
                        v.tensor_tensor(Dm[x % 2], tiles4(banks[b]), cumN[:, :, A_ROWS + h:A_ROWS + h + 1].to_broadcast([P, TT, P]),
                                        ALU.subtract).then_inc(differ, 1)
                        dve.wait_ge(differ, x + 1)
                        v.tensor_tensor(Dm[x % 2], Dm[x % 2], wide(cst("neg64")), ALU.add).then_inc(masked, 1)
                        v.tensor_copy(g_last[:, x, :], banks[b].rearrange("p (c n) -> p c n", n=64)[:, :, 63:64].squeeze(2))
                        t_ = tiles4(banks[b])
                        v.tensor_copy(g_end[0:64, x, :], t_[0:64, :, 63:64].squeeze(2))
                        link(v.tensor_copy(g_end[64:128, x, :], t_[64:128, :, 127:128].squeeze(2)))
                        v.tensor_tensor(g_end[:, x, :], g_end[:, x, :], cumN[:, :, A_ROWS + h:A_ROWS + h + 1].squeeze(2), ALU.subtract)\
                            .then_inc(ends, 1)
                        dve.wait_ge(exps, 2 * x + 2)
                        v.scalar_tensor_tensor(acT[:, x].rearrange("p t n -> p (t n)"), banks[b + 2], GDN_SCALE,
                                               Dm[x % 2].rearrange("p t n -> p (t n)"), ALU.mult, ALU.mult)
                        link(v.tensor_tensor(AT[:, x], tiles4(banks[b + 3]), Dm[x % 2], ALU.mult))
                        link(v.tensor_tensor(AT[:, x], AT[:, x], tiles4(banks[b + 1]), ALU.mult))
                        link(v.tensor_tensor(AT[:, x], AT[:, x], wide(cst("strict64")), ALU.mult))
                        v.scalar_tensor_tensor(qg[:, x, :], xp[:, h // 2, 0:T], GDN_SCALE, eg[x % 2].rearrange("p t n -> p (t n)"),
                                               ALU.mult, ALU.mult).then_inc(used, 1)
                    dve.wait_ge(ends_exp, 3)
                    v.tensor_tensor(kbs[:], kbs[:], smallN[:, :, b0:b0 + B4], ALU.mult)

                @block.scalar
                def _(act):
                    for x in range(B4):
                        act.wait_ge(ends, x + 1)
                        if x >= 2:
                            act.wait_ge(used, x - 1)
                        nc.scalar.activation(eg[x % 2], tiles4(banks[4 * (x % 2)]), ACT.Exp).then_inc(exps, 1)
                        act.wait_ge(masked, x + 1)
                        nc.scalar.activation(Dm[x % 2], Dm[x % 2], ACT.Exp).then_inc(exps, 1)
                    act.wait_ge(ends, B4)
                    nc.scalar.activation(g_end[:], g_end[:], ACT.Exp).then_inc(ends_exp, 1)
                    nc.scalar.activation(g_last[:], g_last[:], ACT.Exp).then_inc(ends_exp, 1)
                    nc.scalar.activation(kbs[:], cumN[:, :, g0:g0 + B4], ACT.Exp).then_inc(ends_exp, 1)

            with stage(nc, "turned scaled dve_step t_ready t_turned t_copied") as (
                    block, turned, scaled, dve_step, t_ready, t_turned, t_copied):
                @block.tensor
                def _(pe):
                    for x, h in enumerate(heads):
                        b = 2 * (x % 2)
                        if x >= 2:
                            pe.wait_ge(scaled, x - 1)
                        for n, c in enumerate((8 + h, 4 + h // 2)):
                            for t in range(TT):
                                s = slice(t * P, (t + 1) * P)
                                last = nc.tensor.transpose(banks[b + n][:, s], xp[:, c, s], ident)
                        last.then_inc(turned, 1)
                    for x in range(B4):
                        pe.wait_ge(t_ready, x + 1)
                        for t in range(TT):
                            last = nc.tensor.transpose(banks[4 + x][:, t * P:(t + 1) * P], Tt[:, x, t, :], ident)
                        last.then_inc(t_turned, 1)

                @block.vector
                def _(dve):
                    v = nc.vector
                    link = Chain(dve, dve_step)
                    for x, h in enumerate(heads):
                        b = 2 * (x % 2)
                        dve.wait_ge(turned, x + 1)
                        v.tensor_tensor(vb[:, x], tiles4(banks[b]), smallN[:, :, BETA_ROWS + h:BETA_ROWS + h + 1].to_broadcast([P, TT, P]), ALU.mult)
                        v.tensor_tensor(kb[:, x], tiles4(banks[b + 1]), kbs[:, :, x:x + 1].to_broadcast([P, TT, P]), ALU.mult)
                        v.tensor_tensor(kd[:, x], tiles4(banks[b + 1]), bc(g_end[:, x, :], P), ALU.mult).then_inc(scaled, 1)
                    for x in range(B4):
                        link(v.tensor_tensor(Tt[:, x], AT[:, x], wide(cst("level", 0, P)), ALU.mult))
                        v.tensor_tensor(Tt[:, x], wide(ident), Tt[:, x], ALU.subtract).then_inc(t_ready, 1)

                @block.scalar
                def _(act):
                    for x in range(B4):
                        act.wait_ge(t_turned, x + 1)
                        nc.scalar.copy(Tn[:, x], tiles4(banks[4 + x])).then_inc(t_copied, 1)

            jobs = [(k, x) for k in range(1, 6) for x in range(B4)]
            with stage(nc, "level_ready w_done w_copied v_done half_updated updated") as (
                    block, level_ready, w_done, w_copied, v_done, half_updated, updated):
                @block.gpsimd
                def _(pool):
                    for j, (k, x) in enumerate(jobs):
                        if j >= 2:
                            pool.wait_ge(w_done, j - 1)
                        nc.gpsimd.tensor_tensor(am[j % 2], AT[:, x], wide(cst("level", k * P, P)), ALU.mult).then_inc(level_ready, 1)

                @block.tensor
                def _(pe):
                    def w(j):
                        k, x = jobs[j]
                        pe.wait_ge(level_ready, j + 1)
                        if j >= 4:
                            pe.wait_ge(updated, j - 3)
                        if j >= 2:
                            pe.wait_ge(w_copied, j - 1)
                        for t in range(TT):
                            last = nc.tensor.matmul(banks[j % 2][:, t * P:(t + 1) * P], am[j % 2][:, t, :], Tn[:, x, t, :], start=True, stop=True)
                        last.then_inc(w_done, 1)

                    w(0)
                    for j, (k, x) in enumerate(jobs):
                        if j + 1 < len(jobs):
                            w(j + 1)
                        pe.wait_ge(w_copied, j + 1)
                        if j >= 2:
                            pe.wait_ge(updated, j - 1)
                        for t in range(TT):
                            s = slice(t * P, (t + 1) * P)
                            last = nc.tensor.matmul(banks[2 + j % 2][:, s], Wb[j % 2][:, t, :], Tt[:, x, t, :], start=True, stop=True)
                            if k < 5:
                                last = nc.tensor.matmul(banks[4 + j % 2][:, s], Tt[:, x, t, :], Wb[j % 2][:, t, :], start=True, stop=True)
                        last.then_inc(v_done, 1)

                @block.scalar
                def _(act):
                    for j in range(len(jobs)):
                        act.wait_ge(w_done, j + 1)
                        if j >= 2:
                            act.wait_ge(v_done, j - 1)
                        nc.scalar.copy(Wb[j % 2], tiles4(banks[j % 2])).then_inc(w_copied, 1)

                @block.vector
                def _(dve):
                    for j, (k, x) in enumerate(jobs):
                        dve.wait_ge(v_done, j + 1)
                        last = nc.vector.tensor_tensor(Tt[:, x], Tt[:, x], tiles4(banks[2 + j % 2]), ALU.subtract)
                        if k < 5:
                            last = nc.vector.tensor_tensor(Tn[:, x], Tn[:, x], tiles4(banks[4 + j % 2]), ALU.subtract)
                        last.then_inc(updated, 1)

            with stage(nc, "solved u_copied w_copied") as (block, solved, u_copied, w_copied):
                @block.tensor
                def _(pe):
                    for x in range(B4):
                        if x >= 2:
                            pe.wait_ge(u_copied, x - 1)
                            pe.wait_ge(w_copied, x - 1)
                        for t in range(TT):
                            s = slice(t * P, (t + 1) * P)
                            nc.tensor.matmul(banks[x % 2][:, s], Tt[:, x, t, :], vb[:, x, t, :], start=True, stop=True)
                            last = nc.tensor.matmul(banks[2 + x % 2][:, s], kb[:, x, t, :], Tt[:, x, t, :], start=True, stop=True)
                        last.then_inc(solved, 1)

                @block.scalar
                def _(act):
                    for x in range(B4):
                        act.wait_ge(solved, x + 1)
                        nc.scalar.copy(uN[:, x], tiles4(banks[x % 2])).then_inc(u_copied, 1)

                @block.vector
                def _(dve):
                    for x in range(B4):
                        dve.wait_ge(solved, x + 1)
                        nc.vector.tensor_copy(wT[:, x, :], banks[2 + x % 2]).then_inc(w_copied, 1)

            with stage(nc, "state_ready ws_done v_new_ready o_done ds_done o_copied decayed") as (
                    block, state_ready, ws_done, v_new, o_done, ds_done, o_copied, decayed):
                @block.tensor
                def _(pe):
                    for c in range(8):
                        t, half = divmod(c, 2)
                        r = slice(64 * half, 64 * half + 64)
                        s = slice(64 * c, 64 * c + 64)
                        pe.wait_ge(state_ready, c + 1)
                        for x in range(B4):
                            last = nc.tensor.matmul(banks[0][r, x * P:(x + 1) * P], wT[:, x, s], S[:, x, :], start=True, stop=True)
                        last.then_inc(ws_done, 1)
                        pe.wait_ge(v_new, c + 1)
                        if c >= 1:
                            pe.wait_ge(o_copied, c)
                        for x in range(B4):
                            o = banks[1][:, x * 64:(x + 1) * 64]
                            nc.tensor.matmul(o, S[:, x, :], qg[:, x, s], start=True, stop=False)
                            last = nc.tensor.matmul(o, vn[r, x, :], acT[r, x, t, 64 * half:64 * half + 64], start=False, stop=True)
                        last.then_inc(o_done, 1)
                        for x in range(B4):
                            last = nc.tensor.matmul(banks[2][:, x * P:(x + 1) * P], kd[r, x, t, :], vn[r, x, :], start=True, stop=True)
                        last.then_inc(ds_done, 1)

                @block.vector
                def _(dve):
                    v = nc.vector
                    v.memset(S[:], 0.0).then_inc(state_ready, 1)
                    dve.wait_ge(state_ready, 1)
                    for c in range(8):
                        t, half = divmod(c, 2)
                        r = slice(64 * half, 64 * half + 64)
                        dve.wait_ge(ws_done, c + 1)
                        v.tensor_tensor(vn[r], uN[r, :, t, :], banks[0][r, :].rearrange("p (x n) -> p x n", n=P), ALU.subtract)\
                            .then_inc(v_new, 1)
                        v.tensor_tensor(Sd[:], S[:], g_last[:, :, c:c + 1].to_broadcast([P, B4, P]), ALU.mult).then_inc(decayed, 1)
                        dve.wait_ge(decayed, c + 1)
                        dve.wait_ge(ds_done, c + 1)
                        v.tensor_tensor(S[:], Sd[:], banks[2].rearrange("p (x n) -> p x n", n=P), ALU.add).then_inc(state_ready, 1)
                        dve.wait_ge(state_ready, c + 2)

                @block.scalar
                def _(act):
                    for c in range(8):
                        act.wait_ge(o_done, c + 1)
                        nc.scalar.copy(xp[:, 8 + 4 * hb:12 + 4 * hb, 64 * c:64 * c + 64],
                                       banks[1][:, 0:256].rearrange("p (x n) -> p x n", n=64)).then_inc(o_copied, 1)
        rmsnorm(nc, "gdn_norm", lambda c: xp[:, 8 + c, 0:T], lambda c: yT[:, c, :], 8, 1, ones, P, lambda c: col("gdn_g"),
                lambda c: scratch[:, c, :], rstd, banks)
    linear(nc, "gdn_z", dram["w_gdn_z"], layer * 8, 8, xn, DC, ring, banks, "scalar", into(scratch, func=ACT.Silu),
           post=lambda nc, f: nc.vector.tensor_tensor(yT[:, bass.ds(f, 1), :].squeeze(1), yT[:, bass.ds(f, 1), :].squeeze(1),
                                                      scratch[:, bass.ds(f, 1), :].squeeze(1), ALU.mult))


def program(nc, dram, out, upto="final", start=None):
    with ExitStack() as held:
        def sb(name, shape, dt=F32):
            return held.enter_context(nc.sbuf_tensor(name, shape, dt))
        psum = held.enter_context(nc.psum_tensor("banks", [P, 8, 512], F32))
        hT = sb("hT", [P, DC, T])
        xnT = sb("xnT", [P, DC, T])
        scratch = sb("scratch", [P, 8, T])
        ring = sb("ring", [P, SLOTS, 8 * P])
        rs = sb("rstd", [P, 2, T])
        rstd = [rs[:, i, :] for i in range(2)]
        ones = sb("ones", [P, P])
        halves = sb("halves", [P, P])
        ident = sb("ident", [P, P])
        with stage(nc, "filled made") as (block, filled, made):
            @block.gpsimd
            def _(pool):
                nc.gpsimd.memset(ident[:], 0.0).then_inc(filled, 1)
                pool.wait_ge(filled, 1)
                nc.gpsimd.affine_select(out=ident[:], in_=ident[:], compare_op=ALU.not_equal, fill=1.0, base=0,
                                        pattern=[[-1, P]], channel_multiplier=1)

            @block.vector
            def _(dve):
                nc.vector.memset(ones[:], 1.0)
                nc.vector.memset(halves[:], 0.0).then_inc(made, 1)
                dve.wait_ge(made, 1)
                for k in range(2):
                    nc.vector.memset(halves[64 * k:64 * k + 64, 64 * k:64 * k + 64], 1.0)

        def finished():
            with stage(nc, "stored") as (block, stored):
                @block.sync
                def _(sp):
                    sp.dma_start(out, hT[:].rearrange("p c n -> p (c n)")).then_inc(stored, 16)
                    sp.wait_ge(stored, 16)

        if start in (None, "h1", "h2"):
            first_block(nc, dram, sb, psum, hT, xnT, scratch, ring, rstd, ones[:], halves[:], ident[:], upto, start)
        else:
            with stage(nc, "h_loaded") as (block, loaded):
                @block.sync
                def _(sp):
                    sp.dma_start(hT[:].rearrange("p c n -> p (c n)"), dram["xT"]).then_inc(loaded, 16)
                    sp.wait_ge(loaded, 16)
        if upto in ("h1", "h2", "h3"):
            return finished()
        second_block(nc, dram, psum, hT, xnT, scratch, ring, rstd, ones[:], ident[:], upto)
        if upto == "final":
            final_g = sb("final_g", [P, DC])
            banks = [psum[:, b, :] for b in range(8)]
            with stage(nc, "final_g_loaded") as (block, loaded):
                @block.sync
                def _(sp):
                    sp.dma_start(final_g[:], dram["final_g"]).then_inc(loaded, 16)
                    sp.wait_ge(loaded, 16)
            rmsnorm(nc, "final_norm", lambda c: hT[:, c, :], lambda c: hT[:, c, :], DC, DC, ones[:], D,
                    lambda c: final_g[:, c:c + 1], lambda c: scratch[:, c, :], rstd, banks)
        finished()



def _tiles(w):
    import numpy as np
    k, n = w.shape
    return np.ascontiguousarray(w.reshape(k // P, P, n // P, P).transpose(2, 1, 0, 3)).reshape(n // P, P, k)


def _strips(w, n=512):
    import numpy as np
    k, m = w.shape
    return np.ascontiguousarray(w.reshape(k // P, P, m // n, n).transpose(2, 1, 0, 3)).reshape(m // n, P, k // P * n)


def _cols(v):
    return v.reshape(-1, P).T


def _chunks(x):
    import numpy as np
    k, n = x.shape
    return np.ascontiguousarray(x.reshape(k // P, P, n).transpose(1, 0, 2)).reshape(P, -1)


def _layout_first(a):
    import numpy as np
    d = {}
    d["xT"] = _chunks(a["x"][0].T)
    d["memT"] = _chunks(a["mem"][0].T)
    w = a["w_in"][0]
    d["w_in"] = np.concatenate([_tiles(w[:, 0:1024]), _tiles(w[:, 1536:2048])])
    d["w_in_v"] = _strips(w[:, 1024:1536])
    dist = np.arange(P)[:, None] - (np.arange(512)[None, :] - 384)
    d["bias"] = np.ascontiguousarray(a["rel_bias"][0][:, np.clip(dist, -63, 128) + 63].transpose(1, 0, 2)).reshape(P, -1)
    c = {n: np.zeros((P, 16, 32), np.float32) for n in ("c_re", "c_im")}
    b = {n: np.zeros((P, 4, 128), np.float32) for n in ("b_re", "b_im")}
    for n in ("re", "im"):
        src_c, src_b = a["ssm_c_" + n][0], a["ssm_b_" + n][0]
        for g in range(32):
            i, k = divmod(g, 2)
            c["c_" + n][64 * k:64 * k + 64, i, 16 * k:16 * k + 16] = src_c[g].T
            p = 32 * (i % 4) + 16 * k
            b["b_" + n][p:p + 16, i // 4, 64 * k:64 * k + 64] = src_b[g].T
    for n, v in list(c.items()) + list(b.items()):
        d[n] = v.reshape(P, -1)
    d["w_glu"] = _tiles(a["ssm_w_glu"][0])
    d["w_out"] = _tiles(a["w_out"][0])
    for n in ("w_mem_q", "w_mem_k", "w_mem_o"):
        d[n] = _tiles(a[n][0])
    d["w_mem_v"] = _strips(a["w_mem_v"][0])
    d["w_peer_q"] = _tiles(a["w_peer_q"][0])
    d["peer_keys"] = np.ascontiguousarray(a["peer_keys"][0].reshape(16, P, P).transpose(2, 0, 1)).reshape(P, -1)
    d["peer_u"] = _tiles(a["peer_u"][0].T)
    d["peer_v"] = a["peer_v"][0].reshape(P, P, D)
    state = lambda v: v.reshape(16, P).T
    parts = dict(mix_g=_cols(a["norm_mix_g"][0]), att_q_g=_cols(np.tile(a["att_q_g"][0], 2)),
                 att_k_g=_cols(np.tile(a["att_k_g"][0], 2)), lam_re=state(a["ssm_lam_re"][0]),
                 lam_im=state(a["ssm_lam_im"][0]), log_step=state(np.repeat(a["ssm_log_step"][0], 64)),
                 ssm_d=_cols(a["ssm_d"][0].reshape(-1)), b_glu=_cols(a["ssm_b_glu"][0]),
                 mixed_g=np.concatenate([_cols(a["att_out_g"][0]), _cols(a["ssm_out_g"][0])], axis=1),
                 mem_g=_cols(a["norm_mem_g"][0]), memkv_g=_cols(a["norm_memkv_g"][0]), mem_q_g=_cols(a["mem_q_g"][0]),
                 mem_k_g=_cols(a["mem_k_g"][0]), peer_g=_cols(a["norm_peer_g"][0]))
    assert list(parts) == list(VEC1)
    d["vec1"] = np.concatenate([parts[n] for n in VEC1], axis=1)
    return d


def _layout_second(a):
    import numpy as np
    d = {}
    a = {n[:-2]: v for n, v in a.items() if n.endswith("_2")}
    both = lambda f: np.concatenate([f(l) for l in range(LAYERS)])
    at = np.cumsum([0, 1024, 1536, 16, 512, 256, 64, 2048, 1024, 8, 8, 3072])
    part = lambda l, n: a["w_in"][l][:, at[n]:at[n + 1]]
    d["w_ssd_z"] = both(lambda l: _tiles(part(l, 0)))
    d["w_ssd_xbc"] = both(lambda l: _tiles(part(l, 1)))
    d["w_gdn_qkv"] = both(lambda l: _tiles(part(l, 6)))
    d["w_gdn_z"] = both(lambda l: _tiles(part(l, 7)))
    d["w_gate"] = both(lambda l: _tiles(part(l, 10)))

    def narrow(l):
        w = np.zeros((D, P), np.float32)
        w[:, DT_ROWS:DT_ROWS + 16] = part(l, 2)
        w[:, BETA_ROWS:BETA_ROWS + 8] = part(l, 8)
        w[:, A_ROWS:A_ROWS + 8] = part(l, 9)
        return _tiles(w)
    d["w_narrow"] = both(narrow)

    def mla_in(l):
        kr = part(l, 5)
        return _tiles(np.concatenate([part(l, 3), part(l, 4), np.tile(kr[:, 0:32], (1, 4)), np.tile(kr[:, 32:64], (1, 4))], axis=1))
    d["w_mla_in"] = both(mla_in)

    def uq(l):
        w = a["mla_w_uq"][l].reshape(512, 8, 192)
        return _tiles(np.concatenate([w[:, :, n0:n1].reshape(512, -1) for n0, n1 in ((0, 128), (128, 160), (160, 192))], axis=1))
    d["w_mla_uq"] = both(uq)
    ukv = lambda l: a["mla_w_ukv"][l].reshape(256, 8, 256)
    d["w_mla_uk"] = both(lambda l: _tiles(ukv(l)[:, :, 0:128].reshape(256, -1)))
    d["w_mla_uv"] = both(lambda l: _strips(ukv(l)[:, :, 128:256].reshape(256, -1)))
    for n, src in (("w_ssd_out", "w_ssd_out"), ("w_mla_out", "w_mla_out"), ("w_gdn_out", "w_gdn_out"), ("w_mix", "w_out"),
                   ("w_up", "w_up")):
        d[n] = both(lambda l: _tiles(a[src][l]))
    d["w_down"] = both(lambda l: np.ascontiguousarray(
        _tiles(a["w_down"][l]).reshape(8, P, 4, 1024).transpose(0, 2, 1, 3)).reshape(32, P, 1024))
    d["positions"] = np.tile(a["positions"].reshape(1, T), (P, 1))

    m, l = np.arange(P)[:, None], np.arange(P)[None, :]
    neg = lambda keep: np.where(keep, 0.0, NEG)
    levels = [((m ^ l) >= 1 << k) & ((m ^ l) < 2 << k) & (l > m) for k in range(6)]
    inv = 10000.0 ** (-np.arange(0, 64, 2, dtype=np.float32) / np.float32(64))
    parts = dict(neg128=neg(l >= m), neg64=neg((l >= m) & (l // 64 == m // 64)), strict64=(l > m) & (l // 64 == m // 64),
                 level=np.concatenate(levels, axis=1), causal=np.concatenate([np.zeros((P, 384)), neg(l <= m)], axis=1),
                 inv_freq=np.tile(inv, 4)[:, None])
    assert list(parts) == list(CONST)
    d["consts"] = np.concatenate([np.asarray(v, np.float32) for v in parts.values()], axis=1)

    def vec(l):
        conv = lambda w: w.reshape(4, -1, P).transpose(2, 1, 0).reshape(P, -1)
        small = np.zeros((2, P, 1), np.float32)
        small[0, DT_ROWS:DT_ROWS + 16, 0], small[0, A_ROWS:A_ROWS + 8, 0] = a["ssd_dt_bias"][l], a["gdn_dt_bias"][l]
        small[1, DT_ROWS:DT_ROWS + 16, 0], small[1, A_ROWS:A_ROWS + 8, 0] = a["ssd_a_log"][l], a["gdn_a_log"][l]
        parts = dict(norm1=_cols(a["norm1_g"][l]), conv_ssd=conv(a["ssd_conv_w"][l]), conv_ssd_b=_cols(a["ssd_conv_b"][l]),
                     small_b=small[0], a_log=small[1], ssd_d=_cols(np.repeat(a["ssd_d"][l], 64)), ssd_g=_cols(a["ssd_norm_g"][l]),
                     mla_q_g=_cols(a["mla_q_norm_g"][l]), mla_kv_g=_cols(a["mla_kv_norm_g"][l]), conv_gdn=conv(a["gdn_conv_w"][l]),
                     gdn_g=_cols(a["gdn_norm_g"][l]), norm2=_cols(a["norm2_g"][l]))
        assert list(parts) == list(VEC2)
        return np.concatenate(list(parts.values()), axis=1)
    d["vec2"] = np.stack([vec(l) for l in range(LAYERS)])
    d["final_g"] = _cols(a["final_norm_g"])
    return d


def layout(a):
    import numpy as np
    a = {n: np.asarray(v) for n, v in a.items()}
    d = _layout_first(a)
    d.update(_layout_second(a))
    return {n: np.ascontiguousarray(v) for n, v in d.items()}


def kernel(**inputs):
    import numpy as np
    import concourse.bacc as bacc
    from concourse.bass_utils import run_bass_kernel_spmd

    nc = bacc.Bacc("TRN2", target_bir_lowering=False, num_devices=1)
    arrays = {f"in_{n}": v for n, v in layout(inputs).items()}
    dram = {n[3:]: nc.dram_tensor(n, v.shape, mybir.dt.from_np(v.dtype), kind="ExternalInput").ap()
            for n, v in arrays.items()}
    dram["gates"] = nc.dram_tensor("gates", (PK, PK, T), F32, kind="Internal").ap()
    out = nc.dram_tensor("out", (P, DC * T), F32, kind="ExternalOutput").ap()
    program(nc, dram, out)
    result = run_bass_kernel_spmd(nc, [arrays], core_ids=[0]).results[0]["out"]
    return np.ascontiguousarray(np.asarray(result).reshape(P, DC, T).transpose(2, 1, 0)).reshape(1, T, D)
```

```python
import math
from contextlib import ExitStack, contextmanager

import concourse.bass as bass
from concourse import mybir

F32 = mybir.dt.float32
F32R = mybir.dt.float32r
I32 = mybir.dt.int32
U32 = mybir.dt.uint32
ALU = mybir.AluOpType
ACT = mybir.ActivationFunctionType
AX = mybir.AxisListType

P = 128
T = 512
TT = T // P
D = 1024
DC = D // P
EPS = 1e-6
NEG = -1e30
SLOTS = 4
LAYERS = 2

TWO_PI = 2.0 * math.pi
PI_HIGH = 6.28125
PI_LOW = TWO_PI - PI_HIGH


@contextmanager
def stage(nc, names):
    with ExitStack() as held:
        sems = [held.enter_context(nc.semaphore(n)) for n in names.split()]
        with nc.Block() as block:
            yield (block, *sems)
        for s in sems:
            nc.gpsimd.sem_clear(s)
        nc.all_engine_barrier()


class Chain:

    def __init__(self, eng, sem):
        self.eng, self.sem, self.n = eng, sem, 0

    def __call__(self, ins):
        ins.then_inc(self.sem, 1)
        self.n += 1
        self.eng.wait_ge(self.sem, self.n)


def over(eng, n, body):
    body(0, True)
    if n > 1:
        with eng.Fori(1, n) as i:
            body(i, False)


def row(w, i):
    return w[bass.ds(i, 1)].rearrange("o p n -> p (o n)")


def product(nc, out, w_high, w_low, x_high, x_low, start, stop):
    nc.tensor.matmul(out, w_high, x_high, start=start, stop=False)
    nc.tensor.matmul(out, w_high, x_low, start=False, stop=False)
    return nc.tensor.matmul(out, w_low, x_high, start=False, stop=stop)


class Norm:
    NAMES = "squared summed ready rooted inverse scaled high low"

    def __init__(self, nc, x, y, chunks, group, ones, width, gain, scratch, rstd, banks, pair=None, mean=True):
        self.nc, self.x, self.chunks, self.group, self.ones, self.width, self.gain = nc, x, chunks, group, ones, width, gain
        self.scratch, self.rstd, self.banks, self.pair, self.mean = scratch, rstd, banks, pair, mean
        self.y = scratch if pair else y

    def take(self, sems):
        self.squared, self.summed, self.ready, self.rooted, self.inverse, self.scaled, self.high, self.low = sems

    def act(self, act):
        nc = self.nc
        for c in range(self.chunks):
            nc.scalar.activation(self.scratch(c), self.x(c), ACT.Square).then_inc(self.squared, 1)
        for g in range(self.chunks // self.group):
            act.wait_ge(self.ready, g + 1)
            nc.scalar.activation(self.rstd[g % 2], self.rstd[g % 2], ACT.Sqrt).then_inc(self.rooted, 1)
        if self.pair:
            for c in range(self.chunks):
                act.wait_ge(self.scaled, c + 1)
                nc.scalar.copy(self.pair[0](c), self.y(c)).then_inc(self.high, 1)

    def pe(self, pe):
        for g in range(self.chunks // self.group):
            pe.wait_ge(self.squared, (g + 1) * self.group)
            if g >= 4:
                pe.wait_ge(self.ready, g - 3)
            for k in range(self.group):
                last = self.nc.tensor.matmul(self.banks[g % 4], self.ones, self.scratch(g * self.group + k),
                                             start=(k == 0), stop=(k == self.group - 1))
            last.then_inc(self.summed, 1)

    def dve(self, dve):
        nc = self.nc
        for g in range(self.chunks // self.group):
            r = self.rstd[g % 2]
            dve.wait_ge(self.summed, g + 1)
            nc.vector.tensor_scalar(r, self.banks[g % 4], 1.0 / self.width if self.mean else 1.0, EPS, ALU.mult, ALU.add)\
                .then_inc(self.ready, 1)
            dve.wait_ge(self.rooted, g + 1)
            nc.vector.reciprocal(r, r).then_inc(self.inverse, 1)
            dve.wait_ge(self.inverse, g + 1)
            for k in range(self.group):
                c = g * self.group + k
                if self.gain is None:
                    nc.vector.tensor_tensor(self.y(c), self.x(c), r, ALU.mult).then_inc(self.scaled, 1)
                else:
                    nc.vector.scalar_tensor_tensor(self.y(c), self.x(c), self.gain(c), r, ALU.mult, ALU.mult)\
                        .then_inc(self.scaled, 1)

    def pool(self, pool):
        if self.pair:
            for c in range(self.chunks):
                pool.wait_ge(self.high, c + 1)
                self.nc.gpsimd.tensor_tensor(self.pair[1](c), self.y(c), self.pair[0](c).bitcast(F32), ALU.subtract)\
                    .then_inc(self.low, 1)


class Split:
    NAMES = "high low"

    def __init__(self, nc, x, chunks, pair):
        self.nc, self.x, self.chunks, self.pair = nc, x, chunks, pair

    def take(self, sems):
        self.high, self.low = sems

    def act(self, act):
        for c in range(self.chunks):
            self.nc.scalar.copy(self.pair[0](c), self.x(c)).then_inc(self.high, 1)

    def pe(self, pe):
        pass

    def dve(self, dve):
        for c in range(self.chunks):
            dve.wait_ge(self.high, c + 1)
            self.nc.vector.tensor_tensor(self.pair[1](c), self.x(c), self.pair[0](c).bitcast(F32), ALU.subtract)\
                .then_inc(self.low, 1)

    def pool(self, pool):
        pass


def alone(nc, name, work):
    with stage(nc, " ".join(f"{name}_{n}" for n in work.NAMES.split())) as (block, *sems):
        work.take(sems)
        block.scalar(work.act)
        block.tensor(work.pe)
        block.vector(work.dve)
        block.gpsimd(work.pool)


def walk(eng, tiles, body):
    m = max(1, (tiles - 2) // SLOTS)
    for f in range(min(SLOTS, tiles)):
        body(0, f)
    if m > 1:
        with eng.Fori(1, m) as i:
            for s in range(SLOTS):
                body(i, s)
    for f in range(SLOTS * m, tiles):
        body(f // SLOTS, f % SLOTS)


class Linear:

    def __init__(self, name, w, at, tiles, kc, x, steps, n=T, behind=None, fed=False):
        self.fed = fed
        self.name, self.w, self.at, self.tiles, self.kc, self.x, self.steps, self.n, self.behind = \
            name, w, at, tiles, kc, x, steps, n, behind


def linears(nc, name, specs, ring, banks, pre=None, spill=None, fill=None):
    names = [f"{name}_w{u}_loaded" for u in range(SLOTS)] + [f"{name}_w_high", f"{name}_w_low", f"{name}_tile_done"]
    pre_names = [f"{name}_{n}" for n in pre.NAMES.split()] if pre else []
    step_names = [f"{sp.name}_step{k}" for sp in specs for k in range(len(sp.steps))]
    extra = [f"{name}_moved"]
    with ExitStack() as held:
        wH = held.enter_context(nc.sbuf_tensor(f"{name}_high_part", [P, 2, D], F32R))
        wL = held.enter_context(nc.sbuf_tensor(f"{name}_low_part", [P, 2, D], F32R))
        _linears(nc, names, pre_names, step_names, extra, specs, ring, wH, wL, banks, pre, spill, fill)


def _linears(nc, names, pre_names, step_names, extra, specs, ring, wH, wL, banks, pre, spill, fill):
    with stage(nc, " ".join(names + pre_names + step_names + extra)) as (block, *sems):
        moved = sems.pop()
        loaded, (w_high, w_low, tile_done) = sems[0:SLOTS], sems[SLOTS:SLOTS + 3]
        sems = sems[SLOTS + 3:]
        if pre:
            pre.take(sems[:len(pre_names)])
            sems = sems[len(pre_names):]
        g0 = 0
        for sp in specs:
            sp.g0 = g0
            g0 += sp.tiles
            sp.done, sems = sems[:len(sp.steps)], sems[len(sp.steps):]
            sp.bank_read = sp.done[max(k for k, st in enumerate(sp.steps) if st[1])]
        total = g0

        def spec_of(g):
            return next(sp for sp in specs if sp.g0 <= g < sp.g0 + sp.tiles)

        def first_four(sp, i, s):
            return isinstance(i, int) and sp.g0 + SLOTS * i + s < SLOTS

        @block.sync
        def _(eng):
            if spill:
                eng.dma_start(*spill).then_inc(moved, 16)
            for n, sp in enumerate(specs):
                if fill and n == 1:
                    eng.wait_ge(pre.low, pre.chunks)
                    eng.dma_start(*fill).then_inc(moved, 16)

                def load(i, s, sp=sp):
                    g = sp.g0 + SLOTS * i + s
                    if not first_four(sp, i, s):
                        eng.wait_ge(w_low, g - SLOTS + 1)
                    slot = (sp.g0 + s) % SLOTS
                    eng.dma_start(ring[:, slot, 0:sp.kc * P], row(sp.w, sp.at + SLOTS * i + s)).then_inc(loaded[slot], 16)
                walk(eng, sp.tiles, load)
            if spill or fill:
                eng.wait_ge(moved, 16)

        def split_high(eng, sp, i, s, behind=True):
            slot, g = (sp.g0 + s) % SLOTS, sp.g0 + SLOTS * i + s
            eng.wait_ge(loaded[slot], 16 * ((sp.g0 + s) // SLOTS + i + 1))
            if behind:
                eng.wait_ge(tile_done, g - 1)
            w = sp.kc * P
            nc.scalar.copy(wH[:, (sp.g0 + s) % 2, 0:w], ring[:, slot, 0:w]).then_inc(w_high, 1)

        def run_steps(eng, which, sp, i, s):
            f = SLOTS * i + s
            for k, (engine, reads, fn) in enumerate(sp.steps):
                if engine == which:
                    if k == 0:
                        eng.wait_ge(tile_done, sp.g0 + f + 1)
                    else:
                        eng.wait_ge(sp.done[k - 1], f + 1)
                    fn(f, banks[(sp.g0 + s) % SLOTS][:, 0:sp.n], s).then_inc(sp.done[k], 1)

        @block.scalar
        def _(eng):
            if pre:
                pre.act(eng)
            for g in range(min(2, total)):
                sp = spec_of(g)
                split_high(eng, sp, 0, g - sp.g0, behind=False)
            for sp in specs:
                def body(i, s, sp=sp):
                    nxt = SLOTS * i + s + 2 if isinstance(i, int) else None
                    if nxt is not None and nxt >= sp.tiles:
                        g = sp.g0 + nxt
                        if g < total:
                            to = spec_of(g)
                            split_high(eng, to, (g - to.g0) // SLOTS, (g - to.g0) % SLOTS)
                    elif nxt is not None:
                        split_high(eng, sp, nxt // SLOTS, nxt % SLOTS)
                    elif s < 2:
                        split_high(eng, sp, i, s + 2)
                    else:
                        split_high(eng, sp, i + 1, s - 2)
                    run_steps(eng, "act", sp, i, s)
                walk(eng, sp.tiles, body)

        @block.gpsimd
        def _(eng):
            if pre:
                pre.pool(eng)
            for sp in specs:
                def body(i, s, sp=sp):
                    g = sp.g0 + SLOTS * i + s
                    w, slot, half = sp.kc * P, (sp.g0 + s) % SLOTS, (sp.g0 + s) % 2
                    eng.wait_ge(w_high, g + 1)
                    nc.gpsimd.tensor_tensor(wL[:, half, 0:w], ring[:, slot, 0:w], wH[:, half, 0:w].bitcast(F32), ALU.subtract)\
                        .then_inc(w_low, 1)
                walk(eng, sp.tiles, body)

        @block.tensor
        def _(eng):
            if pre:
                pre.pe(eng)
            for n, sp in enumerate(specs):
                if sp.behind:
                    maker = next(x for x in specs if x.name == sp.behind)
                    eng.wait_ge(maker.done[-1], maker.tiles)

                def body(i, s, sp=sp, n=n):
                    g = sp.g0 + SLOTS * i + s
                    half = (sp.g0 + s) % 2
                    eng.wait_ge(w_low, g + 1)
                    if isinstance(i, int) and i == 0:
                        if g >= SLOTS:
                            before = spec_of(g - SLOTS)
                            eng.wait_ge(before.bank_read, g - SLOTS - before.g0 + 1)
                    else:
                        eng.wait_ge(sp.bank_read, SLOTS * (i - 1) + s + 1)
                    for c in range(sp.kc):
                        if sp.fed and isinstance(i, int) and i == 0 and s == 0:
                            eng.wait_ge(pre.low, c + 1)
                        w = slice(c * P, (c + 1) * P)
                        last = product(nc, banks[(sp.g0 + s) % SLOTS][:, 0:sp.n], wH[:, half, w], wL[:, half, w],
                                       sp.x[0](c), sp.x[1](c), c == 0, c == sp.kc - 1)
                    last.then_inc(tile_done, 1)
                walk(eng, sp.tiles, body)

        @block.vector
        def _(eng):
            if pre:
                pre.dve(eng)
            for sp in specs:
                walk(eng, sp.tiles, lambda i, s, sp=sp: run_steps(eng, "dve", sp, i, s))


def part(t, f):
    return t[:, bass.ds(f, 1), 0:T].squeeze(1)


def copy_to(nc, dst, n=T):
    return [("dve", True, lambda f, ps, s: nc.vector.tensor_copy(dst[:, bass.ds(f, 1), 0:n].squeeze(1), ps))]


def pair_to(nc, high, low):
    return [("act", True, lambda f, ps, s: nc.scalar.copy(part(high, f), ps)),
            ("dve", True, lambda f, ps, s: nc.vector.tensor_tensor(part(low, f), ps, part(high, f).bitcast(F32), ALU.subtract))]


def add_steps(nc, hT):
    return [("dve", True, lambda f, ps, s: nc.vector.tensor_tensor(part(hT, f), part(hT, f), ps, ALU.add))]


def chunks_of(t, base=0, n=T):
    return lambda c: t[:, base + c, 0:n]


def linear(nc, name, w, at, tiles, x, kc, ring, banks, evac, write, pieces=1, n=T, post=None):
    u_n = min(SLOTS, tiles * pieces)
    steps = tiles * pieces // u_n
    per = u_n // pieces
    loaded_names = " ".join(f"{name}_w{u}_loaded" for u in range(u_n))
    with stage(nc, f"{name}_piece_done {name}_tile_written {name}_finished {loaded_names}") as (
            block, piece_done, tile_written, finished, *loaded):

        @block.sync
        def _(sp):
            def step(i, first):
                for u in range(u_n):
                    if not first:
                        sp.wait_ge(piece_done, (i - 1) * u_n + u + 1)
                    sp.dma_start(ring[:, u, 0:kc * P], row(w, at + i * u_n + u)).then_inc(loaded[u], 16)
            over(sp, steps, step)

        @block.tensor
        def _(pe):
            def step(i, first):
                for u in range(u_n):
                    pe.wait_ge(loaded[u], 16 * (i + 1))
                    t, piece = divmod(u, pieces)
                    if piece == 0 and not first:
                        pe.wait_ge(tile_written, (i - 1) * per + t + 1)
                    for c in range(kc):
                        last = nc.tensor.matmul(banks[t], ring[:, u, c * P:(c + 1) * P], x(piece * kc + c),
                                                start=(piece == 0 and c == 0),
                                                stop=(piece == pieces - 1 and c == kc - 1))
                    last.then_inc(piece_done, 1)
            over(pe, steps, step)

        def out(eng):
            def step(i, first):
                for t in range(per):
                    eng.wait_ge(piece_done, i * u_n + (t + 1) * pieces)
                    write(nc, i * per + t, banks[t]).then_inc(tile_written, 1)
            over(eng, steps, step)

        (block.scalar if evac == "scalar" else block.vector)(out)

        if post is not None:
            @block.vector
            def _(dve):
                def step(i, first):
                    for t in range(per):
                        dve.wait_ge(tile_written, i * per + t + 1)
                        post(nc, i * per + t).then_inc(finished, 1)
                over(dve, steps, step)


def linear_tokens(nc, name, w, at, x, kc, ring, banks, rows, out):
    weights = ring[:, :, :].rearrange("p s n -> p (s n)")[:, 0:kc * 512]
    with stage(nc, f"{name}_loaded {name}_done") as (block, loaded, done):

        @block.sync
        def _(sp):
            sp.dma_start(weights, row(w, at)).then_inc(loaded, 16)

        @block.tensor
        def _(pe):
            pe.wait_ge(loaded, 16)
            for t in range(rows):
                for c in range(kc):
                    last = nc.tensor.matmul(banks[t], x(c)[:, t * P:(t + 1) * P], weights[:, c * 512:(c + 1) * 512],
                                            start=(c == 0), stop=(c == kc - 1))
                last.then_inc(done, 1)

        @block.scalar
        def _(act):
            for t in range(rows):
                act.wait_ge(done, t + 1)
                nc.scalar.copy(out(t), banks[t])


def rmsnorm(nc, name, x, y, chunks, group, ones, width, gain, scratch, rstd, banks, n=T, eps=EPS, mean=True):
    groups = chunks // group
    with stage(nc, f"{name}_squared {name}_summed {name}_ready {name}_rooted {name}_inverse {name}_scaled") as (
            block, squared, summed, ready, rooted, inverse, scaled):

        @block.scalar
        def _(act):
            for c in range(chunks):
                nc.scalar.activation(scratch(c), x(c), ACT.Square).then_inc(squared, 1)
            for g in range(groups):
                act.wait_ge(ready, g + 1)
                nc.scalar.activation(rstd[g % 2], rstd[g % 2], ACT.Sqrt).then_inc(rooted, 1)

        @block.tensor
        def _(pe):
            for g in range(groups):
                pe.wait_ge(squared, (g + 1) * group)
                if g >= 4:
                    pe.wait_ge(ready, g - 3)
                for k in range(group):
                    last = nc.tensor.matmul(banks[g % 4], ones, scratch(g * group + k), start=(k == 0), stop=(k == group - 1))
                last.then_inc(summed, 1)

        @block.vector
        def _(dve):
            for g in range(groups):
                dve.wait_ge(summed, g + 1)
                nc.vector.tensor_scalar(rstd[g % 2], banks[g % 4], 1.0 / width if mean else 1.0, eps,
                                        ALU.mult, ALU.add).then_inc(ready, 1)
                dve.wait_ge(rooted, g + 1)
                nc.vector.reciprocal(rstd[g % 2], rstd[g % 2]).then_inc(inverse, 1)
                dve.wait_ge(inverse, g + 1)
                for k in range(group):
                    c = g * group + k
                    if gain is None:
                        nc.vector.tensor_tensor(y(c), x(c), rstd[g % 2], ALU.mult).then_inc(scaled, 1)
                    else:
                        nc.vector.scalar_tensor_tensor(y(c), x(c), gain(c), rstd[g % 2], ALU.mult, ALU.mult)\
                            .then_inc(scaled, 1)


def attention(nc, name, heads, scores, keys, scale, bias, values, depth, place, out, banks, sc, pr, pt, stats, ident):
    jobs = [(h, q) for h in range(heads) for q in range(TT)]
    with stage(nc, f"{name}_scored {name}_masked {name}_max {name}_exp {name}_inv {name}_probs {name}_turned "
                   f"{name}_copied {name}_mixed {name}_stored") as (
            block, scored, masked, maxed, exped, inverted, normed, turned, copied, mixed, stored):

        @block.tensor
        def _(pe):
            def turn(j):
                h, q = jobs[j]
                pe.wait_ge(normed, j + 1)
                if j >= 2:
                    pe.wait_ge(copied, j - 1)
                for k in range(keys(q)):
                    last = nc.tensor.transpose(banks[2 + j % 2][:, k * P:(k + 1) * P], pr[:, j % 2, k * P:(k + 1) * P], ident)
                last.then_inc(turned, 1)
                if q == TT - 1:
                    pe.wait_ge(copied, j + 1)
                    if h >= 2:
                        pe.wait_ge(stored, h - 1)
                    for k in range(keys(q)):
                        first_q = min(x for x in range(TT) if keys(x) > k) * P
                        last = nc.tensor.matmul(banks[4 + h % 2][place(h), first_q:T], values(h, k), pt[:, h % 2, k, first_q:T],
                                                start=(k == 0), stop=(k == keys(q) - 1))
                    last.then_inc(mixed, 1)

            for j, (h, q) in enumerate(jobs):
                if j >= 2:
                    pe.wait_ge(masked, j - 1)
                pairs = scores(h, q)
                for n, (a, b) in enumerate(pairs):
                    last = nc.tensor.matmul(banks[j % 2][:, 0:keys(q) * P], a, b, start=(n == 0), stop=(n == len(pairs) - 1))
                last.then_inc(scored, 1)
                if j:
                    turn(j - 1)
            turn(len(jobs) - 1)

        @block.vector
        def _(dve):
            def normalize(j):
                h, q = jobs[j]
                w = keys(q) * P
                dve.wait_ge(exped, j + 1)
                nc.vector.reciprocal(stats[:, 4 + j % 2:5 + j % 2], stats[:, 2 + j % 2:3 + j % 2]).then_inc(inverted, 1)
                dve.wait_ge(inverted, j + 1)
                nc.vector.tensor_scalar(pr[:, j % 2, 0:w], pr[:, j % 2, 0:w], stats[:, 4 + j % 2:5 + j % 2], None,
                                        ALU.mult).then_inc(normed, 1)

            for j, (h, q) in enumerate(jobs):
                w = keys(q) * P
                dve.wait_ge(scored, j + 1)
                b = bias(h, q)
                if b is None:
                    nc.vector.tensor_scalar(sc[:, j % 2, 0:w], banks[j % 2][:, 0:w], scale, None, ALU.mult).then_inc(masked, 1)
                else:
                    nc.vector.scalar_tensor_tensor(sc[:, j % 2, 0:w], banks[j % 2][:, 0:w], scale, b, ALU.mult, ALU.add)\
                        .then_inc(masked, 1)
                dve.wait_ge(masked, j + 1)
                nc.vector.tensor_reduce(stats[:, j % 2:j % 2 + 1], sc[:, j % 2, 0:w], AX.X, ALU.max, negate=True)\
                    .then_inc(maxed, 1)
                if j:
                    normalize(j - 1)
            normalize(len(jobs) - 1)

        @block.scalar
        def _(act):
            def copy(j):
                h, q = jobs[j]
                act.wait_ge(turned, j + 1)
                if h >= 2 and q == 0:
                    act.wait_ge(mixed, h - 1)
                w = keys(q) * P
                nc.scalar.copy(pt[:, h % 2, 0:keys(q), q * P:(q + 1) * P],
                               banks[2 + j % 2][:, 0:w].rearrange("p (k n) -> p k n", n=P)).then_inc(copied, 1)
                if q == TT - 1:
                    act.wait_ge(mixed, h + 1)
                    nc.scalar.copy(out(h), banks[4 + h % 2][place(h), :]).then_inc(stored, 1)

            for j, (h, q) in enumerate(jobs):
                w = keys(q) * P
                act.wait_ge(maxed, j + 1)
                if j >= 2:
                    act.wait_ge(turned, j - 1)
                nc.scalar.activation(pr[:, j % 2, 0:w], sc[:, j % 2, 0:w], ACT.Exp, bias=stats[:, j % 2:j % 2 + 1],
                                     accum_out=stats[:, 2 + j % 2:3 + j % 2]).then_inc(exped, 1)
                if j:
                    copy(j - 1)
            copy(len(jobs) - 1)


def sine(nc, link, angle, turns, turns_int, s, c):
    v = nc.vector
    link(v.tensor_scalar(turns, angle, 1.0 / TWO_PI, None, ALU.mult))
    link(v.tensor_copy(turns_int, turns))
    link(v.tensor_copy(turns, turns_int))
    link(v.scalar_tensor_tensor(s, turns, -PI_HIGH, angle, ALU.mult, ALU.add))
    link(v.scalar_tensor_tensor(s, turns, -PI_LOW, s, ALU.mult, ALU.add))
    link(v.tensor_scalar(s, s, 0.125, None, ALU.mult))
    return v.tensor_scalar(c, s, math.pi / 2, None, ALU.add)


def double_angle(nc, link, s, c, tmp, times=3):
    v = nc.vector
    for _ in range(times):
        link(v.tensor_tensor(tmp, s, c, ALU.mult))
        link(v.tensor_tensor(c, s, s, ALU.mult))
        link(v.tensor_scalar(c, c, -2.0, 1.0, ALU.mult, ALU.add))
        link(v.tensor_scalar(s, tmp, 2.0, None, ALU.mult))


def bc(ap, n):
    return ap.unsqueeze(2).to_broadcast([ap.shape[0], ap.shape[1], n])



HEADS1, HD1 = 8, 64
SSM_TILES = 16
MEM = 256
VEC1 = dict(mix_g=(0, 8), att_q_g=(8, 1), att_k_g=(9, 1), lam_re=(10, 16), lam_im=(26, 16), log_step=(42, 16),
            ssm_d=(58, 4), b_glu=(62, 4), mixed_g=(66, 8), mem_g=(74, 8), memkv_g=(82, 8), mem_q_g=(90, 2),
            mem_k_g=(92, 2), peer_g=(94, 8))
VEC1_N = 102


def first_block(nc, dram, sb, psum, hT, xnT, scratch, ring, rstd, ones, halves, ident, upto, start):
    banks = [psum[:, b, :] for b in range(8)]
    with ExitStack() as held:
        vec = held.enter_context(nc.sbuf_tensor("vec1", [P, VEC1_N], F32))

        def col(name, k=0):
            return vec[:, VEC1[name][0] + k:VEC1[name][0] + k + 1]

        def cols(name):
            return vec[:, VEC1[name][0]:VEC1[name][0] + VEC1[name][1]]

        with stage(nc, "inputs_loaded") as (block, loaded):
            @block.sync
            def _(sp):
                sp.dma_start(hT[:].rearrange("p c n -> p (c n)"), dram["xT"]).then_inc(loaded, 16)
                sp.dma_start(vec[:], dram["vec1"]).then_inc(loaded, 16)
                sp.wait_ge(loaded, 32)

        def norm_x(name, gain):
            rmsnorm(nc, name, lambda c: hT[:, c, :], lambda c: xnT[:, c, :], DC, DC, ones, D,
                    lambda c: col(gain, c), lambda c: scratch[:, c, :], rstd, banks)

        def xn(c):
            return xnT[:, c, :]

        def mix():
            norm_x("norm_mix", "mix_g")
            with ExitStack() as phase:
                qT = phase.enter_context(nc.sbuf_tensor("qT", [P, 4, T], F32))
                kT = phase.enter_context(nc.sbuf_tensor("kT", [P, 4, T], F32))
                uT = phase.enter_context(nc.sbuf_tensor("uT", [P, 4, T], F32))
                quk = [qT, kT, uT]
                vS = phase.enter_context(nc.sbuf_tensor("vS", [P, TT, 512], F32))
                mixT = phase.enter_context(nc.sbuf_tensor("mixT", [P, 8, T], F32))
                for n, dst in enumerate(quk):
                    linear(nc, f"w_in{n}", dram["w_in"], 4 * n, 4, xn, DC, ring, banks, "scalar",
                           lambda nc, f, ps, dst=dst: nc.scalar.copy(dst[:, bass.ds(f, 1), :].squeeze(1), ps))
                linear_tokens(nc, "w_v", dram["w_in_v"], 0, xn, DC, ring, banks, TT, lambda t: vS[:, t, :])
                for name, t_, g in (("norm_q", qT, "att_q_g"), ("norm_k", kT, "att_k_g")):
                    rmsnorm(nc, name, lambda c, t_=t_: t_[:, c, :], lambda c, t_=t_: t_[:, c, :], 4, 1, halves, HD1,
                            lambda c, g=g: col(g), lambda c: scratch[:, c, :], rstd, banks)
                with ExitStack() as att:
                    bias = att.enter_context(nc.sbuf_tensor("bias", [P, HEADS1, 512], F32))
                    sc = att.enter_context(nc.sbuf_tensor("sc", [P, 2, 512], F32))
                    pr = att.enter_context(nc.sbuf_tensor("pr", [P, 2, 512], F32))
                    pt = att.enter_context(nc.sbuf_tensor("pt", [P, 2, 4, 512], F32))
                    stats = att.enter_context(nc.sbuf_tensor("stats", [P, 8], F32))
                    with stage(nc, "bias_loaded bias_masked") as (block, loaded, masked):
                        @block.sync
                        def _(sp):
                            sp.dma_start(bias[:].rearrange("p h n -> p (h n)"), dram["bias"]).then_inc(loaded, 16)

                        @block.vector
                        def _(dve):
                            dve.wait_ge(loaded, 16)
                            nc.vector.memset(bias[0:64, :, 448:512], NEG).then_inc(masked, 1)

                    def half(h):
                        return slice(64 * (h % 2), 64 * (h % 2) + 64)
                    attention(nc, "band", HEADS1,
                              lambda h, q: [(qT[half(h), h // 2, q * P:(q + 1) * P], kT[half(h), h // 2, 0:(q + 1) * P])],
                              lambda q: q + 1, HD1 ** -0.5, lambda h, q: bias[:, h, 384 - 128 * q:512],
                              lambda h, k: vS[:, k, h * HD1:(h + 1) * HD1], HD1, half,
                              lambda h: mixT[half(h), h // 2, :], banks, sc, pr, pt, stats, ident)
                rmsnorm(nc, "norm_att", lambda c: mixT[:, c, :], lambda c: mixT[:, c, :], 4, 4, ones, 512,
                        lambda c: col("mixed_g", c), lambda c: scratch[:, c, :], rstd, banks)
                state_space(nc, dram, col, cols, uT, mixT, ring, banks, psum, scratch)
                rmsnorm(nc, "norm_ssm", lambda c: mixT[:, 4 + c, :], lambda c: mixT[:, 4 + c, :], 4, 4, ones, 512,
                        lambda c: col("mixed_g", 4 + c), lambda c: scratch[:, c, :], rstd, banks)
                linear(nc, "w_out", dram["w_out"], 0, 8, lambda c: mixT[:, c, :], DC, ring, banks, "vector",
                       lambda nc, f, ps: add_to(nc, hT, f, ps))

        if start is None:
            mix()
        if upto == "h1":
            return

        def memory():
            norm_x("norm_mem", "mem_g")
            with ExitStack() as phase:
                memT = phase.enter_context(nc.sbuf_tensor("memT", [P, 8, MEM], F32))
                mqT = phase.enter_context(nc.sbuf_tensor("mqT", [P, 8, T], F32))
                mkT = phase.enter_context(nc.sbuf_tensor("mkT", [P, 8, MEM], F32))
                mv = phase.enter_context(nc.sbuf_tensor("mv", [P, 2, D], F32))
                moT = phase.enter_context(nc.sbuf_tensor("moT", [P, 8, T], F32))
                with stage(nc, "memory_loaded") as (block, loaded):
                    @block.sync
                    def _(sp):
                        sp.dma_start(memT[:].rearrange("p c n -> p (c n)"), dram["memT"]).then_inc(loaded, 16)
                        sp.wait_ge(loaded, 16)

                def short(c):
                    return scratch[:, c, 0:MEM]
                rmsnorm(nc, "norm_memkv", lambda c: memT[:, c, :], lambda c: memT[:, c, :], 8, 8, ones, D,
                        lambda c: col("memkv_g", c), short, [r[:, 0:MEM] for r in rstd], [b[:, 0:MEM] for b in banks])
                linear(nc, "w_mem_q", dram["w_mem_q"], 0, 8, xn, DC, ring, banks, "scalar",
                       lambda nc, f, ps: nc.scalar.copy(mqT[:, bass.ds(f, 1), :].squeeze(1), ps))
                linear(nc, "w_mem_k", dram["w_mem_k"], 0, 8, lambda c: memT[:, c, :], DC, ring, [b[:, 0:MEM] for b in banks],
                       "scalar", lambda nc, f, ps: nc.scalar.copy(mkT[:, bass.ds(f, 1), :].squeeze(1), ps))
                for n in range(2):
                    linear_tokens(nc, f"w_mem_v{n}", dram["w_mem_v"], n, lambda c: memT[:, c, :], DC, ring, banks, 2,
                                  lambda t, n=n: mv[:, t, n * 512:(n + 1) * 512])
                rmsnorm(nc, "norm_mq", lambda c: mqT[:, c, :], lambda c: mqT[:, c, :], 8, 2, ones, 256,
                        lambda c: col("mem_q_g", c % 2), lambda c: scratch[:, c, :], rstd, banks)
                rmsnorm(nc, "norm_mk", lambda c: mkT[:, c, :], lambda c: mkT[:, c, :], 8, 2, ones, 256,
                        lambda c: col("mem_k_g", c % 2), short, [r[:, 0:MEM] for r in rstd], [b[:, 0:MEM] for b in banks])
                with ExitStack() as att:
                    sc = att.enter_context(nc.sbuf_tensor("mem_sc", [P, 2, 512], F32))
                    pr = att.enter_context(nc.sbuf_tensor("mem_pr", [P, 2, 512], F32))
                    pt = att.enter_context(nc.sbuf_tensor("mem_pt", [P, 2, 4, 512], F32))
                    stats = att.enter_context(nc.sbuf_tensor("mem_stats", [P, 8], F32))
                    attention(nc, "memory", 8,
                              lambda h, q: [(mqT[:, 2 * (h // 2) + c, q * P:(q + 1) * P], mkT[:, 2 * (h // 2) + c, :]) for c in range(2)],
                              lambda q: 2, 256 ** -0.5, lambda h, q: None,
                              lambda h, k: mv[:, k, h * P:(h + 1) * P], P, lambda h: slice(0, P),
                              lambda h: moT[:, h, :], banks, sc, pr, pt, stats, ident)
                linear(nc, "w_mem_o", dram["w_mem_o"], 0, 8, lambda c: moT[:, c, :], DC, ring, banks, "vector",
                       lambda nc, f, ps: add_to(nc, hT, f, ps))

        if start in (None, 'h1'):
            memory()
        if upto == "h2":
            return
        if start in (None, "h1", "h2"):
            norm_x("norm_peer", "peer_g")
            experts(nc, dram, hT, xnT, scratch, ring, banks, ident)
        if upto == "h3":
            return


def add_to(nc, hT, f, ps):
    tile = hT[:, bass.ds(f, 1), :].squeeze(1)
    return nc.vector.tensor_tensor(tile, tile, ps, ALU.add)


def state_space(nc, dram, col, cols, uT, mixT, ring, banks, psum, scratch):
    with ExitStack() as held:
        def sb(name, shape, dt=F32):
            return held.enter_context(nc.sbuf_tensor(name, shape, dt))
        N = SSM_TILES
        par = sb("ssm_par", [P, 16, N])
        step, lre, mag, sn, cs, tmp, turns, fr, fi, den, zr_, th, aim = (par[:, i, :] for i in range(13))
        turns_int = sb("turns_int", [P, N], I32)
        power = sb("power", [P, 9, 2, N])
        Er = sb("Er", [P, N, T])
        Ei = sb("Ei", [P, N, T])
        cre = sb("cre", [P, N, 32])
        cim = sb("cim", [P, N, 32])
        c1 = sb("c1", [P, N, 32])
        c2 = sb("c2", [P, N, 32])
        big = sb("rot_tmp", [P, N // 4, 256])
        bre = sb("bre", [P, 4, 128])
        bim = sb("bim", [P, 4, 128])
        with stage(nc, "c_loaded step_done angles_ready exps_done sines_done dve_step") as (
                block, loaded, step_done, angles, exps, sines, dve_step):

            @block.sync
            def _(sp):
                sp.dma_start(cre[:].rearrange("p a b -> p (a b)"), dram["c_re"]).then_inc(loaded, 16)
                sp.dma_start(cim[:].rearrange("p a b -> p (a b)"), dram["c_im"]).then_inc(loaded, 16)
                sp.dma_start(bre[:].rearrange("p a b -> p (a b)"), dram["b_re"]).then_inc(loaded, 16)
                sp.dma_start(bim[:].rearrange("p a b -> p (a b)"), dram["b_im"]).then_inc(loaded, 16)

            @block.scalar
            def _(act):
                nc.scalar.activation(step, cols("log_step"), ACT.Exp).then_inc(step_done, 1)
                act.wait_ge(angles, 1)
                nc.scalar.activation(mag, lre, ACT.Exp).then_inc(exps, 1)
                act.wait_ge(angles, 2)
                nc.scalar.activation(sn, sn, ACT.Sin).then_inc(sines, 1)
                nc.scalar.activation(cs, cs, ACT.Sin).then_inc(sines, 1)

            @block.vector
            def _(dve):
                v = nc.vector
                link = Chain(dve, dve_step)
                dve.wait_ge(step_done, 1)
                link(v.tensor_tensor(th, cols("lam_im"), step, ALU.mult))
                v.tensor_tensor(lre, cols("lam_re"), step, ALU.mult).then_inc(angles, 1)
                sine(nc, link, th, turns, turns_int[:], sn, cs).then_inc(angles, 1)
                dve.wait_ge(exps, 1)
                dve.wait_ge(sines, 2)
                double_angle(nc, link, sn, cs, tmp)
                link(v.tensor_tensor(zr_, mag, cs, ALU.mult))
                link(v.tensor_scalar(zr_, zr_, -1.0, None, ALU.add))
                link(v.tensor_tensor(aim, mag, sn, ALU.mult))
                link(v.tensor_tensor(den, cols("lam_re"), cols("lam_re"), ALU.mult))
                link(v.tensor_tensor(tmp, cols("lam_im"), cols("lam_im"), ALU.mult))
                link(v.tensor_tensor(den, den, tmp, ALU.add))
                link(v.reciprocal(den, den))
                link(v.tensor_tensor(fr, zr_, cols("lam_re"), ALU.mult))
                link(v.tensor_tensor(tmp, aim, cols("lam_im"), ALU.mult))
                link(v.tensor_tensor(fr, fr, tmp, ALU.add))
                link(v.tensor_tensor(fr, fr, den, ALU.mult))
                link(v.tensor_tensor(fi, aim, cols("lam_re"), ALU.mult))
                link(v.tensor_tensor(tmp, zr_, cols("lam_im"), ALU.mult))
                link(v.tensor_tensor(fi, fi, tmp, ALU.subtract))
                link(v.tensor_tensor(fi, fi, den, ALU.mult))
                dve.wait_ge(loaded, 64)
                link(v.tensor_tensor(c1[:], cre[:], bc(fr, 32), ALU.mult))
                link(v.tensor_tensor(c2[:], cim[:], bc(fi, 32), ALU.mult))
                link(v.tensor_tensor(c1[:], c1[:], c2[:], ALU.subtract))
                link(v.tensor_tensor(cre[:], cre[:], bc(fi, 32), ALU.mult))
                link(v.tensor_tensor(cim[:], cim[:], bc(fr, 32), ALU.mult))
                link(v.tensor_tensor(c2[:], cre[:], cim[:], ALU.add))
                link(v.tensor_scalar(c2[:], c2[:], -1.0, None, ALU.mult))
                link(v.tensor_scalar(cre[:], c1[:], -1.0, None, ALU.mult))
                link(v.tensor_copy(power[:, 0, 0, :], cs))
                link(v.tensor_copy(power[:, 0, 1, :], sn))
                for k in range(8):
                    c_, s_, c2_, s2_ = power[:, k, 0, :], power[:, k, 1, :], power[:, k + 1, 0, :], power[:, k + 1, 1, :]
                    link(v.tensor_tensor(tmp, s_, s_, ALU.mult))
                    link(v.tensor_tensor(c2_, c_, c_, ALU.mult))
                    link(v.tensor_tensor(c2_, c2_, tmp, ALU.subtract))
                    link(v.scalar_tensor_tensor(s2_, s_, 2.0, c_, ALU.mult, ALU.mult))
                link(v.memset(Er[:, :, 0:1], 1.0))
                link(v.memset(Ei[:, :, 0:1], 0.0))
                for k in range(9):
                    n = 1 << k
                    for t0 in range(0, N, 4):
                        ts_ = slice(t0, t0 + 4)
                        c_, s_ = bc(power[:, k, 0, ts_], n), bc(power[:, k, 1, ts_], n)
                        link(v.tensor_tensor(big[:, :, 0:n], Ei[:, ts_, 0:n], s_, ALU.mult))
                        link(v.tensor_tensor(Er[:, ts_, n:2 * n], Er[:, ts_, 0:n], c_, ALU.mult))
                        link(v.tensor_tensor(Er[:, ts_, n:2 * n], Er[:, ts_, n:2 * n], big[:, :, 0:n], ALU.subtract))
                        link(v.tensor_tensor(big[:, :, 0:n], Er[:, ts_, 0:n], s_, ALU.mult))
                        link(v.tensor_tensor(Ei[:, ts_, n:2 * n], Ei[:, ts_, 0:n], c_, ALU.mult))
                        link(v.tensor_tensor(Ei[:, ts_, n:2 * n], Ei[:, ts_, n:2 * n], big[:, :, 0:n], ALU.add))

        w = scratch
        with stage(nc, "b_ready turned_in scanned products y_ready y_summed y_activated dve_step pool_step") as (
                block, b_ready, rotated, scanned, products, y_ready, summed, activated, dve_step, pool_step):

            @block.tensor
            def _(pe):
                def project(i):
                    g, k = divmod(i, 4)
                    s = slice(32 * k, 32 * k + 32)
                    if i >= 1:
                        pe.wait_ge(rotated, i)
                    nc.tensor.matmul(banks[0], bre[s, g, :], uT[s, g, :], start=True, stop=True)
                    nc.tensor.matmul(banks[1], bim[s, g, :], uT[s, g, :], start=True, stop=True).then_inc(b_ready, 1)
                project(0)
                for i in range(N):
                    g, k = divmod(i, 4)
                    if i + 1 < N:
                        project(i + 1)
                    pe.wait_ge(products, i + 1)
                    for n, c in enumerate((c1, cre, c2, c2)):
                        last = nc.tensor.matmul(banks[4 + g][32 * k:32 * k + 32, :], c[:, i, :], w[:, 4 + n, :],
                                                start=(n == 0), stop=(n == 3), skip_group_check=True)
                    last.then_inc(y_ready, 1)

            @block.vector
            def _(dve):
                v = nc.vector
                link = Chain(dve, dve_step)
                for i in range(N):
                    dve.wait_ge(b_ready, i + 1)
                    link(v.tensor_tensor(w[:, 0, :], banks[0], Er[:, i, :], ALU.mult))
                    link(v.tensor_tensor(w[:, 1, :], banks[1], Ei[:, i, :], ALU.mult))
                    link(v.tensor_tensor(w[:, 0, :], w[:, 0, :], w[:, 1, :], ALU.add))
                    link(v.tensor_tensor(w[:, 1, :], banks[1], Er[:, i, :], ALU.mult))
                    if i:
                        dve.wait_ge(products, i)
                    v.tensor_tensor(w[:, 2, :], banks[0], Ei[:, i, :], ALU.mult).then_inc(rotated, 1)
                    dve.wait_ge(rotated, i + 1)
                    link(v.tensor_tensor(w[:, 1, :], w[:, 1, :], w[:, 2, :], ALU.subtract))
                    m = mag[:, i:i + 1].to_broadcast([P, T])
                    link(v.tensor_tensor_scan(w[:, 2, :], m, w[:, 0, :], 0.0, ALU.mult, ALU.add))
                    v.tensor_tensor_scan(w[:, 3, :], m, w[:, 1, :], 0.0, ALU.mult, ALU.add).then_inc(scanned, 1)
                for g in range(4):
                    dve.wait_ge(y_ready, 4 * g + 4)
                    v.scalar_tensor_tensor(uT[:, g, :], uT[:, g, :], col("ssm_d", g), banks[4 + g], ALU.mult, ALU.add)\
                        .then_inc(summed, 1)

            @block.gpsimd
            def _(pool):
                for i in range(N):
                    pool.wait_ge(scanned, i + 1)
                    if i:
                        pool.wait_ge(y_ready, i)
                    nc.gpsimd.tensor_tensor(w[:, 4, :], w[:, 2, :], Er[:, i, :], ALU.mult)
                    nc.gpsimd.tensor_tensor(w[:, 5, :], w[:, 3, :], Ei[:, i, :], ALU.mult)
                    nc.gpsimd.tensor_tensor(w[:, 6, :], w[:, 3, :], Er[:, i, :], ALU.mult)
                    nc.gpsimd.tensor_tensor(w[:, 7, :], w[:, 2, :], Ei[:, i, :], ALU.mult).then_inc(products, 1)

            @block.scalar
            def _(act):
                for g in range(4):
                    act.wait_ge(summed, g + 1)
                    nc.scalar.activation(uT[:, g, :], uT[:, g, :], ACT.Gelu).then_inc(activated, 1)

        bglu = cols("b_glu")
        with stage(nc, "glu_loaded glu_done gate_ready gated") as (block, loaded, done, gate, gated):
            glu = ring[:, :, :].rearrange("p s n -> p (s n)")

            @block.sync
            def _(sp):
                for f in range(4):
                    sp.dma_start(glu[:, f * 512:(f + 1) * 512], row(dram["w_glu"], f)).then_inc(loaded, 16)

            @block.tensor
            def _(pe):
                pe.wait_ge(loaded, 64)
                for f in range(4):
                    for c in range(4):
                        last = nc.tensor.matmul(banks[f], glu[:, f * 512 + c * P:f * 512 + (c + 1) * P], uT[:, c, :],
                                                start=(c == 0), stop=(c == 3))
                    last.then_inc(done, 1)

            @block.scalar
            def _(act):
                for f in range(4):
                    act.wait_ge(done, f + 1)
                    nc.scalar.activation(scratch[:, f, :], banks[f], ACT.Sigmoid, bias=bglu[:, f:f + 1]).then_inc(gate, 1)

            @block.vector
            def _(dve):
                for f in range(4):
                    dve.wait_ge(gate, f + 1)
                    nc.vector.tensor_tensor(mixT[:, 4 + f, :], uT[:, f, :], scratch[:, f, :], ALU.mult).then_inc(gated, 1)



PH, PK, TOP = 8, 128, 16
GROUP = 4
LOWEST = -3e38


def experts(nc, dram, hT, xnT, scratch, ring, banks, ident):
    with ExitStack() as held:
        first = held.enter_context(nc.sbuf_tensor("firstT", [P, T], F32))
        second = held.enter_context(nc.sbuf_tensor("secondT", [P, T], F32))
        gateT = held.enter_context(nc.sbuf_tensor("gateT", [P, T], F32))
        iota = held.enter_context(nc.sbuf_tensor("iota", [P, PK], F32))
        with stage(nc, "iota_ready") as (block, ready):
            @block.gpsimd
            def _(pool):
                nc.gpsimd.iota(iota[:], pattern=[[1, PK]], base=0, channel_multiplier=0,
                               allow_small_or_imprecise_dtypes=True).then_inc(ready, 1)
        choose_experts(nc, dram, xnT, ring, banks, ident, first, second, gateT, iota)
        build_gates(nc, dram, scratch, ring, banks, first, second, gateT, iota)
    stream_experts(nc, dram, hT, xnT, scratch, ring, banks)


def choose_experts(nc, dram, xnT, ring, banks, ident, first, second, gateT, iota):
    with ExitStack() as held:
        def sb(name, shape, dt=F32):
            return held.enter_context(nc.sbuf_tensor(name, shape, dt))
        qT = sb("peer_qT", [P, 2 * PH, T])
        keys = sb("peer_keys_sb", [P, 2 * PH, PK])
        qs = sb("q_tile", [P, 2 * PH, P])
        s1 = sb("key_scores", [P, 2 * PH, PK])
        s2 = sb("key_scores_rest", [P, 2 * PH, PK])
        sv = sb("key_top", [P, 2 * PH, TOP])
        si = sb("key_index", [P, 2 * PH, TOP], U32)
        sif = sb("key_index_f", [P, 2 * PH, TOP])
        top = sb("pair_top", [P, PH, TOP])
        pos = sb("pair_index", [P, PH, TOP], U32)
        ab = sb("pair_ab", [P, 2, PH * TOP], U32)
        abf = sb("pair_ab_f", [P, 2, PH * TOP])
        tab = sb("to_turn", [P, 3, PH * TOP])
        sums = sb("gate_sums", [P, PH])
        linear(nc, "w_peer_q", dram["w_peer_q"], 0, 2 * PH, lambda c: xnT[:, c, :], DC, ring, banks, "scalar",
               lambda nc, f, ps: nc.scalar.copy(qT[:, bass.ds(f, 1), :].squeeze(1), ps))
        with stage(nc, "keys_loaded") as (block, loaded):
            @block.sync
            def _(sp):
                sp.dma_start(keys[:].rearrange("p h n -> p (h n)"), dram["peer_keys"]).then_inc(loaded, 16)
                sp.wait_ge(loaded, 16)
        with nc.Fori(0, TT) as t:
            with stage(nc, "q_copied keys_scored scores_stored") as (block, copied, scored, kept):
                @block.scalar
                def _(act):
                    nc.scalar.copy(qs[:], qT[:, :, bass.ds(t * P, P)]).then_inc(copied, 1)
                    for b in range(4):
                        act.wait_ge(scored, b + 1)
                        nc.scalar.copy(s1[:, 4 * b:4 * b + 4, :], banks[b].rearrange("p (h n) -> p h n", n=PK)).then_inc(kept, 1)

                @block.tensor
                def _(pe):
                    pe.wait_ge(copied, 1)
                    for b in range(4):
                        for k in range(4):
                            last = nc.tensor.matmul(banks[b][:, k * PK:(k + 1) * PK], qs[:, 4 * b + k, :], keys[:, 4 * b + k, :],
                                                    start=True, stop=True)
                        last.then_inc(scored, 1)

            with stage(nc, "dve_step logits_ready exps_done gates_ready turned") as (
                    block, dve_step, logits, exps, gates, turned):
                @block.vector
                def _(dve):
                    v = nc.vector
                    link = Chain(dve, dve_step)

                    def top16(n, values, rest, best, index):
                        for k in range(n):
                            last = v.max(best[:, k, 0:8], values[:, k, :])
                        link(last)
                        for k in range(n):
                            v.max_index(index[:, k, 0:8], best[:, k, 0:8], values[:, k, :])
                            last = v.match_replace(rest[:, k, :], best[:, k, 0:8], values[:, k, :], LOWEST)
                        link(last)
                        for k in range(n):
                            last = v.max(best[:, k, 8:16], rest[:, k, :])
                        link(last)
                        for k in range(n):
                            last = v.max_index(index[:, k, 8:16], best[:, k, 8:16], rest[:, k, :])
                        link(last)

                    top16(2 * PH, s1, s2, sv, si)
                    link(v.tensor_copy(sif[:], si[:]))
                    cand = s1[:].rearrange("p (h two) n -> p h (two n)", two=2)
                    rest = s2[:].rearrange("p (h two) n -> p h (two n)", two=2)
                    by_side = sv[:].rearrange("p (h two) a -> p h two a", two=2)
                    for h in range(PH):
                        last = v.tensor_tensor(cand[:, h, :].rearrange("p (a b) -> p a b", b=TOP),
                                               bc(by_side[:, h, 0, :], TOP),
                                               by_side[:, h, 1:2, :].to_broadcast([P, TOP, TOP]), ALU.add)
                    link(last)
                    top16(PH, cand, rest, top, pos)
                    flat = pos[:].rearrange("p h k -> p (h k)")
                    link(v.tensor_scalar(ab[:, 0, :], flat, 4, None, ALU.logical_shift_right))
                    link(v.tensor_scalar(ab[:, 1, :], flat, 15, None, ALU.bitwise_and))
                    link(v.tensor_copy(abf[:], ab[:]))
                    tops = top[:]
                    gate = tab[:, 2, :].rearrange("p (h k) -> p h k", k=TOP)
                    v.tensor_tensor(gate, tops, top[:, :, 0:1].to_broadcast([P, PH, TOP]), ALU.subtract).then_inc(logits, 1)
                    for side in range(2):
                        eq = s1[:].rearrange("p h n -> p (h n)").rearrange("p (x a) -> p x a", a=TOP)
                        link(v.tensor_tensor(eq, bc(abf[:, side, :], TOP),
                                             iota[:, 0:TOP].unsqueeze(1).to_broadcast([P, PH * TOP, TOP]), ALU.is_equal))
                        for h in range(PH):
                            e = eq[:, h * TOP:(h + 1) * TOP, :]
                            last = v.tensor_tensor(e, e, sif[:, 2 * h + side, :].unsqueeze(1).to_broadcast([P, TOP, TOP]), ALU.mult)
                        link(last)
                        link(v.tensor_reduce(tab[:, side, :], eq, AX.X, ALU.add))
                    dve.wait_ge(exps, 1)
                    link(v.tensor_reduce(sums[:], gate, AX.X, ALU.add))
                    link(v.reciprocal(sums[:], sums[:]))
                    v.tensor_tensor(gate, gate, bc(sums[:], TOP), ALU.mult).then_inc(gates, 1)

                @block.scalar
                def _(act):
                    act.wait_ge(logits, 1)
                    nc.scalar.activation(tab[:, 2, :], tab[:, 2, :], ACT.Exp).then_inc(exps, 1)
                    for n, dst in enumerate((first, second, gateT)):
                        act.wait_ge(turned, n + 1)
                        last = nc.scalar.copy(dst[:, bass.ds(t * P, P)], banks[n][:, 0:P])
                    last.then_inc(exps, 1)

                @block.tensor
                def _(pe):
                    pe.wait_ge(gates, 1)
                    for n in range(3):
                        nc.tensor.transpose(banks[n][:, 0:P], tab[:, n, :], ident).then_inc(turned, 1)


ONEHOT = 16


def build_gates(nc, dram, scratch, ring, banks, first, second, gateT, iota):
    a_ = scratch[:].rearrange("p c n -> p (c n)").rearrange("p (b t i) -> p b t i", b=2, i=PK)
    b_ = ring[:].rearrange("p c n -> p (c n)").rearrange("p (b t i) -> p b t i", b=2, i=PK)
    iota_b = iota[:].unsqueeze(1).to_broadcast([P, ONEHOT, PK])
    per_block = P // ONEHOT
    with ExitStack() as held:
        G = held.enter_context(nc.sbuf_tensor("gate_block", [P, 2, PK, P], F32))
        with stage(nc, "first_onehot second_onehot gated block_used tokens_done copied stored_0 stored_1") as (
                block, first_hot, second_hot, gated, used, tokens_done, copied, stored_0, stored_1):
            stored = [stored_0, stored_1]

            @block.vector
            def _(dve):
                for tb in range(TT):
                    def pair(i, tb=tb):
                        for u in range(2):
                            n = tb * per_block + 2 * i + u
                            at = bass.ds(n * ONEHOT, ONEHOT)
                            if tb or not isinstance(i, int):
                                dve.wait_ge(used, n - 1)
                            nc.vector.tensor_tensor(a_[:, u], bc(first[:, at], PK), iota_b, ALU.is_equal).then_inc(first_hot, 1)
                            nc.vector.tensor_tensor(b_[:, u], bc(second[:, at], PK), iota_b, ALU.is_equal).then_inc(second_hot, 1)
                    pair(0)
                    with dve.Fori(1, per_block // 2) as i:
                        pair(i)

            @block.gpsimd
            def _(pool):
                for tb in range(TT):
                    with pool.Fori(0, per_block // 2) as i:
                        for u in range(2):
                            n = tb * per_block + 2 * i + u
                            pool.wait_ge(first_hot, n + 1)
                            nc.gpsimd.tensor_tensor(a_[:, u], a_[:, u], bc(gateT[:, bass.ds(n * ONEHOT, ONEHOT)], PK),
                                                    ALU.mult).then_inc(gated, 1)

            @block.tensor
            def _(pe):
                for tb in range(TT):
                    def pair(i, tb=tb):
                        for u in range(2):
                            n = tb * per_block + 2 * i + u
                            pe.wait_ge(second_hot, n + 1)
                            pe.wait_ge(gated, n + 1)
                            for k in range(ONEHOT):
                                bank = u * 4 + k // 4
                                if k % 4 == 0 and (tb or not isinstance(i, int)):
                                    pe.wait_ge(copied, 4 * n + k // 4 - 7)
                                last = nc.tensor.matmul(banks[bank][:, (k % 4) * P:(k % 4 + 1) * P], b_[:, u, k, :], a_[:, u, k, :],
                                                        start=True, stop=True)
                                if k % 4 == 3 and k < ONEHOT - 1:
                                    last.then_inc(tokens_done, 1)
                            last.then_inc(used, 1)
                    pair(0)
                    with pe.Fori(1, per_block // 2) as i:
                        pair(i)

            @block.scalar
            def _(act):
                for tb in range(TT):
                    if tb >= 2:
                        act.wait_ge(stored[tb % 2], 64)
                    with act.Fori(0, per_block // 2) as i:
                        for u in range(2):
                            n = tb * per_block + 2 * i + u
                            for q in range(4):
                                if q < 3:
                                    act.wait_ge(tokens_done, 3 * n + q + 1)
                                else:
                                    act.wait_ge(used, n + 1)
                                nc.scalar.copy(G[:, tb % 2, :, bass.ds((2 * i + u) * ONEHOT + 4 * q, 4)],
                                               banks[u * 4 + q].rearrange("p (t i) -> p i t", i=PK)).then_inc(copied, 1)

            @block.sync
            def _(sp):
                for tb in range(TT):
                    sp.wait_ge(copied, 4 * per_block * (tb + 1))
                    for part in range(4):
                        r = slice(32 * part, 32 * part + 32)
                        sp.dma_start(dram["gates"][r, :, tb * P:(tb + 1) * P].rearrange("i j t -> j i t"),
                                     G[:, tb % 2, r, :]).then_inc(stored[tb % 2], 16)
                sp.wait_ge(stored_0, 128)
                sp.wait_ge(stored_1, 128)


def stream_experts(nc, dram, hT, xnT, scratch, ring, banks):
    groups = PK // GROUP
    with ExitStack() as held:
        def sb(name, shape, dt=F32):
            return held.enter_context(nc.sbuf_tensor(name, shape, dt))
        xH = sb("xn_high", [P, DC, T], F32R)
        xL = sb("xn_low", [P, DC, T], F32R)
        uH = sb("in_high", [P, 2, D], F32R)
        uL = sb("in_low", [P, 2, D], F32R)
        vH = sb("out_high", [P, GROUP, D], F32R)
        vL = sb("out_low", [P, GROUP, D], F32R)
        aH = sb("act_high", [P, 2 * GROUP, T], F32R)
        aL = sb("act_low", [P, 2 * GROUP, T], F32R)
        alone(nc, "xn", Split(nc, chunks_of(xnT), DC, (chunks_of(xH), chunks_of(xL))))
        G = xnT[:, 0:GROUP, :]
        A = xnT[:, GROUP:2 * GROUP, :]
        U = ring
        V = scratch[:].rearrange("p (s two) n -> p s (two n)", two=2)
        names = [f"{k}{u}_loaded" for k in ("in", "out", "gate") for u in range(GROUP)]
        with stage(nc, "in_high_ready in_low_ready out_high_ready out_low_ready dots_done activated gated "
                       "act_high_ready act_low_ready summed added " + " ".join(names)) as (
                block, in_high, in_low, out_high, out_low, dots, activated, gated, act_high, act_low, summed, added, *loads):
            u_in, v_in, g_in = loads[0:4], loads[4:8], loads[8:12]

            def pairs(eng, body):
                body(0, 0)
                body(1, 1)
                with eng.Fori(1, groups // 2) as k:
                    body(2 * k, 0)
                    body(2 * k + 1, 1)

            def is_first(g):
                return isinstance(g, int) and g == 0

            @block.sync
            def _(sp):
                def load_out(g):
                    for u in range(GROUP):
                        if not is_first(g):
                            sp.wait_ge(out_low, GROUP * (g - 1) + u + 1)
                        sp.dma_start(V[:, u, :], row(dram["peer_v"], g * GROUP + u)).then_inc(v_in[u], 16)

                def body(g, half):
                    for u in range(GROUP):
                        if not is_first(g):
                            sp.wait_ge(in_low, GROUP * (g - 1) + u + 1)
                        sp.dma_start(U[:, u, :], row(dram["peer_u"], g * GROUP + u)).then_inc(u_in[u], 16)
                        if not is_first(g):
                            sp.wait_ge(gated, GROUP * (g - 1) + u + 1)
                        sp.dma_start(G[:, u, :], row(dram["gates"], g * GROUP + u)).then_inc(g_in[u], 16)
                    if is_first(g):
                        return
                    load_out(g - 1)
                pairs(sp, body)
                load_out(groups - 1)

            @block.scalar
            def _(act):
                def split_in(n, g, u, first):
                    act.wait_ge(u_in[u], 16 * (g + 1))
                    if not first:
                        act.wait_ge(dots, n - 1)
                    nc.scalar.copy(uH[:, u % 2, :], U[:, u, :]).then_inc(in_high, 1)

                def split_out(g, u):
                    act.wait_ge(v_in[u], 16 * (g + 1))
                    if not is_first(g):
                        act.wait_ge(summed, DC * g)
                    nc.scalar.copy(vH[:, u, :], V[:, u, :]).then_inc(out_high, 1)

                def body(g, half, last=False):
                    for u in range(GROUP):
                        n = g * GROUP + u
                        if not is_first(g):
                            split_out(g - 1, u)
                        act.wait_ge(dots, n + 1)
                        if not is_first(g):
                            act.wait_ge(act_low, n - GROUP + 1)
                        nc.scalar.activation(A[:, u, :], banks[u % 2], ACT.Gelu).then_inc(activated, 1)
                        if not (last and u >= 2):
                            split_in(n + 2, g + (u + 2) // GROUP, (u + 2) % GROUP, False)
                split_in(0, 0, 0, True)
                split_in(1, 0, 1, True)
                body(0, 0)
                body(1, 1)
                with act.Fori(1, groups // 2 - 1) as k:
                    body(2 * k, 0)
                    body(2 * k + 1, 1)
                body(groups - 2, 0)
                body(groups - 1, 1, last=True)
                for u in range(GROUP):
                    split_out(groups - 1, u)

            @block.gpsimd
            def _(pool):
                def split_in(n, u):
                    pool.wait_ge(in_high, n + 1)
                    nc.gpsimd.tensor_tensor(uL[:, u % 2, :], U[:, u, :], uH[:, u % 2, :].bitcast(F32), ALU.subtract)\
                        .then_inc(in_low, 1)

                def split_out(g, u):
                    pool.wait_ge(out_high, g * GROUP + u + 1)
                    nc.gpsimd.tensor_tensor(vL[:, u, :], V[:, u, :], vH[:, u, :].bitcast(F32), ALU.subtract)\
                        .then_inc(out_low, 1)

                def body(g, half, last=False):
                    for u in range(GROUP):
                        if not is_first(g):
                            split_out(g - 1, u)
                        if not (last and u >= 2):
                            split_in(g * GROUP + u + 2, (u + 2) % GROUP)
                split_in(0, 0)
                split_in(1, 1)
                body(0, 0)
                body(1, 1)
                with pool.Fori(1, groups // 2 - 1) as k:
                    body(2 * k, 0)
                    body(2 * k + 1, 1)
                body(groups - 2, 0)
                body(groups - 1, 1, last=True)
                for u in range(GROUP):
                    split_out(groups - 1, u)

            @block.tensor
            def _(pe):
                def dot(g, half):
                    for u in range(GROUP):
                        n = g * GROUP + u
                        pe.wait_ge(in_low, n + 1)
                        if u >= 2 or not is_first(g):
                            pe.wait_ge(activated, n - 1)
                        for c in range(DC):
                            w = slice(c * P, (c + 1) * P)
                            last = product(nc, banks[u % 2], uH[:, u % 2, w], uL[:, u % 2, w], xH[:, c, :], xL[:, c, :],
                                           c == 0, c == DC - 1)
                        last.then_inc(dots, 1)

                def combine(g, half):
                    for d in range(DC):
                        if d == 0:
                            pe.wait_ge(act_low, GROUP * (g + 1))
                            pe.wait_ge(out_low, GROUP * (g + 1))
                        if d >= 4 or not is_first(g):
                            pe.wait_ge(added, g * DC + d - 3)
                        for u in range(GROUP):
                            w = slice(d * P, (d + 1) * P)
                            s = half * GROUP + u
                            last = product(nc, banks[2 + d % 4], vH[:, u, w], vL[:, u, w], aH[:, s, :], aL[:, s, :],
                                           u == 0, u == GROUP - 1)
                        last.then_inc(summed, 1)

                dot(0, 0)
                dot(1, 1)
                combine(0, 0)
                with pe.Fori(1, groups // 2) as k:
                    dot(2 * k, 0)
                    combine(2 * k - 1, 1)
                    dot(2 * k + 1, 1)
                    combine(2 * k, 0)
                combine(groups - 1, 1)

            @block.vector
            def _(dve):
                def weigh(g, half):
                    for u in range(GROUP):
                        n = g * GROUP + u
                        s = half * GROUP + u
                        dve.wait_ge(activated, n + 1)
                        dve.wait_ge(g_in[u], 16 * (g + 1))
                        nc.vector.tensor_tensor(A[:, u, :], A[:, u, :], G[:, u, :], ALU.mult).then_inc(gated, 1)
                        if not isinstance(g, int):
                            dve.wait_ge(summed, DC * (g - 1))
                        dve.wait_ge(gated, n + 1)
                        nc.vector.tensor_copy(aH[:, s, :], A[:, u, :]).then_inc(act_high, 1)
                        dve.wait_ge(act_high, n + 1)
                        nc.vector.tensor_tensor(aL[:, s, :], A[:, u, :], aH[:, s, :].bitcast(F32), ALU.subtract).then_inc(act_low, 1)

                def add(g, half):
                    for d in range(DC):
                        dve.wait_ge(summed, g * DC + d + 1)
                        if not is_first(g):
                            dve.wait_ge(added, g * DC + d + 1 - DC)
                        nc.vector.tensor_tensor(hT[:, d, :], hT[:, d, :], banks[2 + d % 4], ALU.add).then_inc(added, 1)

                weigh(0, 0)
                weigh(1, 1)
                add(0, 0)
                with dve.Fori(1, groups // 2) as k:
                    weigh(2 * k, 0)
                    add(2 * k - 1, 1)
                    weigh(2 * k + 1, 1)
                    add(2 * k, 0)
                add(groups - 1, 1)



CONST = dict(neg128=(0, 128), neg64=(128, 128), strict64=(256, 128), level=(384, 768), causal=(1152, 512), inv_freq=(1664, 1))
CONST_N = 1665
VEC2 = dict(norm1=(0, 8), conv_ssd=(8, 48), conv_ssd_b=(56, 12), small_b=(68, 1), a_log=(69, 1), ssd_d=(70, 8),
            ssd_g=(78, 8), mla_q_g=(86, 4), mla_kv_g=(90, 2), conv_gdn=(92, 64), gdn_g=(156, 1), norm2=(157, 8))
VEC2_N = 165
DT_ROWS, BETA_ROWS, A_ROWS = 0, 32, 64
SSD_HEADS, GDN_HEADS = 16, 8
GDN_SCALE = 128 ** -0.5


def rope_tables(nc, dram, const, cosT, sinT, scratch):
    turns_int = scratch[:, 3, :].bitcast(I32)
    pos = scratch[:, 0, :].bitcast(I32)
    ang, turns, tmp = scratch[:, 1, :], scratch[:, 2, :], scratch[:, 4, :]
    with stage(nc, "positions_loaded reduced sines_done dve_step") as (block, loaded, reduced, sines, dve_step):
        @block.sync
        def _(sp):
            sp.dma_start(const[:], dram["consts"]).then_inc(loaded, 16)
            sp.dma_start(pos, dram["positions"]).then_inc(loaded, 16)

        @block.vector
        def _(dve):
            link = Chain(dve, dve_step)
            dve.wait_ge(loaded, 32)
            link(nc.vector.tensor_copy(ang, pos))
            link(nc.vector.tensor_scalar(ang, ang, const[:, CONST["inv_freq"][0]:CONST["inv_freq"][0] + 1], None, ALU.mult))
            sine(nc, link, ang, turns, turns_int, sinT, cosT).then_inc(reduced, 1)
            dve.wait_ge(sines, 2)
            double_angle(nc, link, sinT, cosT, tmp)

        @block.scalar
        def _(act):
            act.wait_ge(reduced, 1)
            nc.scalar.activation(sinT, sinT, ACT.Sin).then_inc(sines, 1)
            nc.scalar.activation(cosT, cosT, ACT.Sin).then_inc(sines, 1)


def conv_steps(nc, xp, weight, bias, acc):
    def tile(f, k=0):
        return xp[:, bass.ds(f, 1), k:k + T].squeeze(1)

    def first_tap(f, ps, s):
        if bias is None:
            return nc.vector.tensor_scalar(acc[s], tile(f, 3), weight(f, 3), None, ALU.mult)
        return nc.vector.tensor_scalar(acc[s], tile(f, 3), weight(f, 3), bias(f), ALU.mult, ALU.add)

    def tap(k):
        return lambda f, ps, s: nc.vector.scalar_tensor_tensor(acc[s], tile(f, k), weight(f, k), acc[s], ALU.mult, ALU.add)
    return [("act", True, lambda f, ps, s: nc.scalar.copy(tile(f, 3), ps)), ("dve", False, first_tap),
            ("dve", False, tap(2)), ("dve", False, tap(1)), ("dve", False, tap(0)),
            ("act", False, lambda f, ps, s: nc.scalar.activation(tile(f), acc[s], ACT.Silu))]


def second_block(nc, dram, psum, hT, scratch, ring, rstd, ones, ident, upto=None):
    banks = [psum[:, b, :] for b in range(8)]
    with ExitStack() as held:
        def sb(name, shape, dt=F32):
            return held.enter_context(nc.sbuf_tensor(name, shape, dt))
        const = sb("consts_sb", [P, CONST_N])
        cosT = sb("cosT", [P, T])
        sinT = sb("sinT", [P, T])
        vec = sb("vec2", [P, VEC2_N])
        small = sb("small", [P, T])
        cum = sb("cum", [P, T])
        smallN = sb("smallN", [P, TT, P])
        cumN = sb("cumN", [P, TT, P])
        xH = sb("x_high", [P, DC, T], F32R)
        xL = sb("x_low", [P, DC, T], F32R)
        xn = (chunks_of(xH), chunks_of(xL))
        acc = [scratch[:, s, :] for s in range(SLOTS)]
        rope_tables(nc, dram, const, cosT[:], sinT[:], scratch)

        def col(name, k=0):
            return vec[:, bass.ds(VEC2[name][0] + k, 1)]

        def cst(name, k=0, n=None):
            a, w = CONST[name]
            return const[:, a + k:a + (k + n if n else w)]

        def act_to(dst, func=None):
            if func is None:
                return ("act", True, lambda f, ps, s: nc.scalar.copy(part(dst, f), ps))
            return ("act", True, lambda f, ps, s: nc.scalar.activation(part(dst, f), ps, func))

        def times(dst, src):
            return ("dve", False, lambda f, ps, s: nc.vector.tensor_tensor(part(dst, f), part(dst, f), part(src, f), ALU.mult))

        def parts_of(src, high, low):
            return [("act", False, lambda f, ps, s: nc.scalar.copy(part(high, f), part(src, f))),
                    ("dve", False, lambda f, ps, s: nc.vector.tensor_tensor(part(low, f), part(src, f), part(high, f).bitcast(F32),
                                                                            ALU.subtract))]

        def norm_to(high, low, x, gain, group=DC, width=D):
            return Norm(nc, x, None, DC, group, ones, width, lambda c: col(gain, c), chunks_of(scratch), rstd, banks,
                        pair=(chunks_of(high), chunks_of(low)))

        def gate_and_out(name, n, y, mixT, last=False):
            gate = Linear(f"{name}_gate", dram["w_gate"], layer * 24 + 8 * n, 8, DC, xn, [act_to(scratch, ACT.Sigmoid)])
            if n == 2:
                steps = [("dve", True, lambda f, ps, s: nc.vector.tensor_tensor(part(mixT, f), part(scratch, f), ps, ALU.mult))]
            else:
                steps = [("dve", True, lambda f, ps, s: nc.vector.tensor_tensor(part(scratch, f), part(scratch, f), ps, ALU.mult)),
                         ("dve", False, lambda f, ps, s: nc.vector.tensor_tensor(part(mixT, f), part(mixT, f), part(scratch, f),
                                                                                 ALU.add))]
            return [gate, Linear(f"{name}_out", dram[f"w_{name}_out"], layer * 8, 8, DC, y, steps, behind="gdn_z" if n == 2 else None, fed=(n != 2))]

        with nc.Fori(0, LAYERS if upto == "final" else 1) as layer:
            with stage(nc, "vec_loaded") as (block, loaded):
                @block.sync
                def _(sp):
                    sp.dma_start(vec[:], row(dram["vec2"], layer)).then_inc(loaded, 16)
                    sp.wait_ge(loaded, 16)
            yT = hT
            delta_rule(nc, dram, layer, yT, small, cum, smallN, cumN, col, cst, ones, ring, banks, ident, scratch, rstd,
                       xn, norm_to(xH, xL, chunks_of(hT), "norm1"), acc, hT)
            with ExitStack() as mix:
                mixT = mix.enter_context(nc.sbuf_tensor("mixed", [P, 8, T], F32))
                with ExitStack() as mla:
                    c8 = mla.enter_context(nc.sbuf_tensor("mla_c", [P, 8, T], F32))
                    with ExitStack() as tail:
                        yH = tail.enter_context(nc.sbuf_tensor("gdn_y_high", [P, 8, T], F32R))
                        yL = tail.enter_context(nc.sbuf_tensor("gdn_y_low", [P, 8, T], F32R))
                        linears(nc, "gdn_tail", [
                            Linear("gdn_z", dram["w_gdn_z"], layer * 8, 8, DC, xn,
                                   [act_to(scratch, ACT.Silu), times(yT, scratch)] + parts_of(yT, yH, yL)),
                            *gate_and_out("gdn", 2, (chunks_of(yH), chunks_of(yL)), mixT),
                            Linear("mla_in", dram["w_mla_in"], layer * 8, 8, DC, xn, [act_to(c8)])], ring, banks)
                    latent_attention(nc, dram, layer, c8, yT, col, cst, ones, ring, banks, ident, scratch, rstd, cosT, sinT)
                with ExitStack() as tail:
                    yH = tail.enter_context(nc.sbuf_tensor("mla_y_high", [P, 8, T], F32R))
                    yL = tail.enter_context(nc.sbuf_tensor("mla_y_low", [P, 8, T], F32R))
                    pair = (chunks_of(yH), chunks_of(yL))
                    linears(nc, "mla_tail", gate_and_out("mla", 1, pair, mixT), ring, banks, pre=Split(nc, chunks_of(yT), DC, pair))
                duality(nc, dram, layer, xn, yT, small, cum, smallN, cumN, col, cst, ones, ring, banks, ident, scratch, acc)
                linears(nc, "ssd_gate_z", [Linear("ssd_z", dram["w_ssd_z"], layer * 8, 8, DC, xn,
                                                  [act_to(scratch, ACT.Silu), times(yT, scratch)])], ring, banks)
                with ExitStack() as tail:
                    yH = tail.enter_context(nc.sbuf_tensor("ssd_y_high", [P, 8, T], F32R))
                    yL = tail.enter_context(nc.sbuf_tensor("ssd_y_low", [P, 8, T], F32R))
                    gate, ssd_out = gate_and_out("ssd", 0, (chunks_of(yH), chunks_of(yL)), mixT)
                    ssd_out.steps += parts_of(mixT, xH, xL)
                    linears(nc, "ssd_tail", [gate, ssd_out, Linear("w_mix", dram["w_mix"], layer * 8, 8, DC, xn, add_steps(nc, hT),
                                                                   behind="ssd_out")], ring, banks,
                            pre=norm_to(yH, yL, chunks_of(yT), "ssd_g", 4, 512),
                            fill=(hT[:].rearrange("p c n -> p (c n)"), dram["stream"]))
            with ExitStack() as mlp:
                upH = mlp.enter_context(nc.sbuf_tensor("up_high", [P, 8, T], F32R))
                upL = mlp.enter_context(nc.sbuf_tensor("up_low", [P, 8, T], F32R))
                square = ("dve", False, lambda f, ps, s: nc.vector.tensor_tensor(part(scratch, f), part(scratch, f),
                                                                                 part(scratch, f), ALU.mult))
                quarters = []
                for q in range(4):
                    quarters += [Linear(f"w_up{q}", dram["w_up"], layer * 32 + 8 * q, 8, DC, xn,
                                        [act_to(scratch, ACT.Relu), square] + parts_of(scratch, upH, upL), fed=(q == 0)),
                                 Linear(f"w_down{q}", dram["w_down"], layer * 32 + 8 * q, 8, DC, (chunks_of(upH), chunks_of(upL)),
                                        add_steps(nc, hT), behind=f"w_up{q}")]
                linears(nc, "mlp", quarters, ring, banks, pre=norm_to(xH, xL, chunks_of(hT), "norm2"))


def narrow_rows(nc, small, cum, smallN, cumN, col, ones, banks, ident, scratch):
    x, neg_abs, e, rate = scratch[:, 7, :], scratch[:, 1, :], scratch[:, 2, :], scratch[:, 3, 0:1]
    with stage(nc, "shifted magnitude logs rates beta_ready dve_step rows_ready turned copied") as (
            block, shifted, magnitude, logs, rates, beta, dve_step, rows_ready, turned, copied):
        @block.tensor
        def _(pe):
            pe.wait_ge(rows_ready, 1)
            for n, src in enumerate((small, cum)):
                for t in range(TT):
                    last = nc.tensor.transpose(banks[2 + n][:, t * P:(t + 1) * P], src[:, t * P:(t + 1) * P], ident)
                last.then_inc(turned, 1)

        @block.scalar
        def _(act):
            nc.scalar.activation(small[32:64, :], x[32:64, :], ACT.Sigmoid).then_inc(beta, 1)
            act.wait_ge(shifted, 1)
            nc.scalar.activation(e, neg_abs, ACT.Exp).then_inc(magnitude, 1)
            nc.scalar.activation(rate, col("a_log"), ACT.Exp).then_inc(rates, 1)
            act.wait_ge(magnitude, 1)
            nc.scalar.activation(e, e, ACT.Ln, bias=1.0).then_inc(logs, 1)
            for n, dst in enumerate((smallN, cumN)):
                act.wait_ge(turned, n + 1)
                nc.scalar.copy(dst[:].rearrange("p a b -> p (a b)"), banks[2 + n]).then_inc(copied, 1)

        @block.vector
        def _(dve):
            v = nc.vector
            link = Chain(dve, dve_step)
            link(v.tensor_scalar(neg_abs, x, -1.0, None, ALU.mult))
            v.tensor_tensor(neg_abs, x, neg_abs, ALU.min).then_inc(shifted, 1)
            link(v.memset(cum[:], 0.0))
            dve.wait_ge(rates, 1)
            dve.wait_ge(logs, 1)
            dve.wait_ge(beta, 1)
            link(v.scalar_tensor_tensor(x, x, 0.0, e, ALU.max, ALU.add))
            v.tensor_copy(small[0:32, :], x[0:32, :])
            v.tensor_copy(small[64:128, :], x[64:128, :])
            link(v.tensor_scalar(e, x, rate, -1.0, ALU.mult, ALU.mult))
            for t in range(TT):
                s = slice(t * P, (t + 1) * P)
                v.tensor_tensor_scan(cum[0:32, s], ones[0:32, :], e[0:32, s], 0.0, ALU.mult, ALU.add)
            for t in range(2 * TT):
                s = slice(t * 64, (t + 1) * 64)
                last = v.tensor_tensor_scan(cum[64:96, s], ones[64:96, 0:64], e[64:96, s], 0.0, ALU.mult, ALU.add)
            last.then_inc(rows_ready, 1)


def spread_row(nc, bank, src, base, h, ident):
    rows = slice(base, base + 32)
    return nc.tensor.matmul(bank, ident[rows, base + h:base + h + 1].to_broadcast([32, P]), src[rows, :], start=True, stop=True)


def wide(ap):
    return ap.unsqueeze(1).to_broadcast([ap.shape[0], TT, P])


def tiles4(bank):
    return bank.rearrange("p (t n) -> p t n", n=P)


def duality(nc, dram, layer, xn, yT, small, cum, smallN, cumN, col, cst, ones, ring, banks, ident, scratch, acc):
    with ExitStack() as held:
        def sb(name, shape, dt=F32):
            return held.enter_context(nc.sbuf_tensor(name, shape, dt))
        xp = sb("ssd_xbc", [P, 12, T + 3])
        with stage(nc, "ssd_zeroed") as (block, zeroed):
            @block.vector
            def _(dve):
                nc.vector.memset(xp[:, :, 0:3], 0.0)
        linears(nc, "ssd_in", [Linear("ssd_xbc", dram["w_ssd_xbc"], layer * 12, 12, DC, xn, conv_steps(
            nc, xp, lambda f, k: col("conv_ssd", f * 4 + k), lambda f: col("conv_ssd_b", f), acc))], ring, banks)
        xdt = sb("ssd_xdt", [P, TT, D])
        xdd = scratch[:].rearrange("p (t c) n -> p t (c n)", c=2)[:, 0:3]
        Bn = sb("ssd_Bn", [P, 2, TT, P])
        CBT = sb("ssd_CBT", [P, 2, TT, P])
        H = ring
        last_cum = sb("ssd_last", [P, SSD_HEADS, TT])
        state_decay = sb("ssd_state_decay", [P, SSD_HEADS, TT])
        decay_end = sb("ssd_decay_end", [P, TT, SSD_HEADS])
        with stage(nc, "turned scaled b_turned b_copied cb_done cb_copied row_spread last_copied exps dve_step ends_ready") as (
                block, turned, scaled, b_turned, b_copied, cb_done, cb_copied, spread, last_copied, exps, dve_step, ends):
            @block.tensor
            def _(pe):
                for j in range(8):
                    t, half = divmod(j, 2)
                    if j >= 2:
                        pe.wait_ge(scaled, j - 1)
                    for k in range(4):
                        last = nc.tensor.transpose(banks[j % 2][:, k * P:(k + 1) * P], xp[:, 4 * half + k, t * P:(t + 1) * P], ident)
                    last.then_inc(turned, 1)
                for g in range(2):
                    for t in range(TT):
                        last = nc.tensor.transpose(banks[2 + g][:, t * P:(t + 1) * P], xp[:, 8 + g, t * P:(t + 1) * P], ident)
                    last.then_inc(b_turned, 1)
                    for t in range(TT):
                        s = slice(t * P, (t + 1) * P)
                        last = nc.tensor.matmul(banks[4 + g][:, s], xp[:, 8 + g, s], xp[:, 10 + g, s], start=True, stop=True)
                    last.then_inc(cb_done, 1)
                for h in range(SSD_HEADS):
                    if h >= 2:
                        pe.wait_ge(last_copied, h - 1)
                    spread_row(nc, banks[6 + h % 2], cum, DT_ROWS, h, ident).then_inc(spread, 1)

            @block.scalar
            def _(act):
                for g in range(2):
                    act.wait_ge(b_turned, g + 1)
                    nc.scalar.copy(Bn[:, g], tiles4(banks[2 + g])).then_inc(b_copied, 1)
                    act.wait_ge(cb_done, g + 1)
                    nc.scalar.copy(CBT[:, g], tiles4(banks[4 + g])).then_inc(cb_copied, 1)
                for h in range(SSD_HEADS):
                    act.wait_ge(spread, h + 1)
                    nc.scalar.copy(last_cum[:, h, :], tiles4(banks[6 + h % 2])[:, :, P - 1:P].squeeze(2)).then_inc(last_copied, 1)
                act.wait_ge(last_copied, SSD_HEADS)
                nc.scalar.activation(state_decay[:], last_cum[:], ACT.Exp).then_inc(exps, 1)
                act.wait_ge(ends, 1)
                nc.scalar.activation(decay_end[:], decay_end[:], ACT.Exp).then_inc(exps, 1)

            @block.vector
            def _(dve):
                v = nc.vector
                link = Chain(dve, dve_step)
                for j in range(8):
                    t, half = divmod(j, 2)
                    dve.wait_ge(turned, j + 1)
                    v.tensor_tensor(xdt[:, t, 512 * half:512 * half + 512].rearrange("p (h d) -> p h d", d=64),
                                    banks[j % 2].rearrange("p (h d) -> p h d", d=64),
                                    bc(smallN[:, t, 8 * half:8 * half + 8], 64), ALU.mult).then_inc(scaled, 1)
                dve.wait_ge(last_copied, SSD_HEADS)
                v.tensor_tensor(decay_end[:], last_cum[:].rearrange("p h t -> p t h"), cumN[:, :, 0:SSD_HEADS], ALU.subtract)\
                    .then_inc(ends, 1)
                dve.wait_ge(exps, 2)
                dve.wait_ge(scaled, 8)
                for t in range(3):
                    link(v.tensor_tensor(xdd[:, t, :].rearrange("p (h d) -> p h d", d=64),
                                         xdt[:, t, :].rearrange("p (h d) -> p h d", d=64), bc(decay_end[:, t, :], 64), ALU.mult))
        with stage(nc, "states_done dve_step") as (block, done, dve_step):
            @block.tensor
            def _(pe):
                for t in range(3):
                    for g in range(2):
                        nc.tensor.matmul(banks[2 * t + g], Bn[:, g, t, :], xdd[:, t, 512 * g:512 * g + 512],
                                         start=True, stop=True).then_inc(done, 1)

            @block.vector
            def _(dve):
                v = nc.vector
                link = Chain(dve, dve_step)
                for t in range(3):
                    for g in range(2):
                        dve.wait_ge(done, 2 * t + g + 1)
                        s = slice(512 * g, 512 * g + 512)
                        if t == 0:
                            link(v.tensor_copy(H[:, 0, s], banks[g]))
                        else:
                            link(v.tensor_tensor(H[:, t, s].rearrange("p (h d) -> p h d", d=64),
                                                 H[:, t - 1, s].rearrange("p (h d) -> p h d", d=64),
                                                 bc(state_decay[:, 8 * g:8 * g + 8, t], 64), ALU.mult))
                            link(v.tensor_tensor(H[:, t, s], H[:, t, s], banks[2 * t + g], ALU.add))
        L = sb("ssd_L", [P, 2, T])
        CE = sb("ssd_CE", [P, 2, T])
        with stage(nc, "row_spread differences masked exps weighted c_scaled y_done y_stored") as (
                block, spread, differences, masked, exps, weighted, c_scaled, y_done, y_stored):
            @block.tensor
            def _(pe):
                def row_of(h):
                    if h >= 2:
                        pe.wait_ge(exps, 2 * (h - 1))
                    spread_row(nc, banks[h % 2], cum, DT_ROWS, h, ident).then_inc(spread, 1)
                row_of(0)
                for h in range(SSD_HEADS):
                    if h + 1 < SSD_HEADS:
                        row_of(h + 1)
                    out = banks[2 + (h // 2) % 2][64 * (h % 2):64 * (h % 2) + 64, :]
                    pe.wait_ge(weighted, h + 1)
                    pe.wait_ge(c_scaled, h + 1)
                    if h % 2 == 0 and h >= 4:
                        pe.wait_ge(y_stored, h // 2 - 1)
                    for t in range(TT):
                        s = slice(t * P, (t + 1) * P)
                        last = nc.tensor.matmul(out[:, s], xdt[:, t, 64 * h:64 * h + 64], L[:, h % 2, s], start=True, stop=(t == 0))
                        if t:
                            last = nc.tensor.matmul(out[:, s], H[:, t - 1, 64 * h:64 * h + 64], CE[:, h % 2, s], start=False, stop=True)
                    last.then_inc(y_done, 1)

            @block.vector
            def _(dve):
                v = nc.vector

                def finish(c):
                    dve.wait_ge(y_done, 2 * c + 2)
                    v.scalar_tensor_tensor(yT[:, c, :], xp[:, c, 0:T], col("ssd_d", c), banks[2 + c % 2], ALU.mult, ALU.add)\
                        .then_inc(y_stored, 1)

                def differ(h):
                    dve.wait_ge(spread, h + 1)
                    if h >= 2:
                        dve.wait_ge(y_done, h - 1)
                    v.tensor_tensor(tiles4(L[:, h % 2]), tiles4(banks[h % 2]), cumN[:, :, h:h + 1].to_broadcast([P, TT, P]),
                                    ALU.subtract).then_inc(differences, 1)
                    dve.wait_ge(differences, h + 1)
                    v.tensor_tensor(tiles4(L[:, h % 2]), tiles4(L[:, h % 2]), wide(cst("neg128")), ALU.add).then_inc(masked, 1)

                differ(0)
                for h in range(SSD_HEADS):
                    if h + 1 < SSD_HEADS:
                        differ(h + 1)
                    dve.wait_ge(exps, 2 * h + 2)
                    v.tensor_tensor(tiles4(L[:, h % 2]), tiles4(L[:, h % 2]), CBT[:, h // 8], ALU.mult).then_inc(weighted, 1)
                    if h % 2 == 1 and h >= 3:
                        finish(h // 2 - 1)
                finish(7)

            @block.scalar
            def _(act):
                for h in range(SSD_HEADS):
                    act.wait_ge(differences, h + 1)
                    if h >= 2:
                        act.wait_ge(y_done, h - 1)
                    nc.scalar.activation(CE[:, h % 2, :], banks[h % 2], ACT.Exp).then_inc(exps, 1)
                    act.wait_ge(masked, h + 1)
                    nc.scalar.activation(L[:, h % 2, :], L[:, h % 2, :], ACT.Exp).then_inc(exps, 1)

            @block.gpsimd
            def _(pool):
                for h in range(SSD_HEADS):
                    pool.wait_ge(exps, 2 * h + 1)
                    nc.gpsimd.tensor_tensor(CE[:, h % 2, :], CE[:, h % 2, :], xp[:, 10 + h // 8, 0:T], ALU.mult).then_inc(c_scaled, 1)


def latent_attention(nc, dram, layer, c8, yT, col, cst, ones, ring, banks, ident, scratch, rstd, cosT, sinT):
    def into(dst):
        return lambda nc, f, ps: nc.scalar.copy(part(dst, f), ps)
    with ExitStack() as held:
        def sb(name, shape, dt=F32):
            return held.enter_context(nc.sbuf_tensor(name, shape, dt))
        q = sb("mla_q", [P, 12, T])
        kn = sb("mla_k", [P, 4, T])
        vals = sb("mla_v", [P, TT, D])
        rmsnorm(nc, "mla_norm_q", lambda c: c8[:, c, :], lambda c: c8[:, c, :], 4, 4, ones, 512, lambda c: col("mla_q_g", c),
                lambda c: scratch[:, c, :], rstd, banks)
        rmsnorm(nc, "mla_norm_kv", lambda c: c8[:, 4 + c, :], lambda c: c8[:, 4 + c, :], 2, 2, ones, 256, lambda c: col("mla_kv_g", c),
                lambda c: scratch[:, c, :], rstd, banks)
        linear(nc, "mla_uq", dram["w_mla_uq"], layer * 12, 12, lambda c: c8[:, c, :], 4, ring, banks, "scalar", into(q))
        for n, dst in enumerate((c8, kn)):
            linear(nc, f"mla_uk{n}", dram["w_mla_uk"], layer * 8 + 4 * n, 4, lambda c: c8[:, 4 + c, :], 2, ring, banks, "scalar",
                   into(dst))
        for n in range(2):
            linear_tokens(nc, f"mla_uv{n}", dram["w_mla_uv"], layer * 2 + n, lambda c: c8[:, 4 + c, :], 2, ring, banks, TT,
                          lambda t, n=n: vals[:, t, n * 512:(n + 1) * 512])
        with stage(nc, "rotate_step rotate_step_pool pool_done") as (block, step, pool_step, pool_done):
            def rotate(eng, ops, sem, a, b, t0, t1):
                link = Chain(eng, sem)
                for x, y in zip(a, b):
                    link(ops.tensor_tensor(t0, x, sinT[:], ALU.mult))
                    link(ops.tensor_tensor(t1, y, sinT[:], ALU.mult))
                    link(ops.tensor_tensor(x, x, cosT[:], ALU.mult))
                    link(ops.tensor_tensor(x, x, t1, ALU.subtract))
                    link(ops.tensor_tensor(y, y, cosT[:], ALU.mult))
                    link(ops.tensor_tensor(y, y, t0, ALU.add))

            @block.vector
            def _(dve):
                rotate(dve, nc.vector, step, [q[:, 8, :], q[:, 9, :]], [q[:, 10, :], q[:, 11, :]], scratch[:, 0, :], scratch[:, 1, :])

            @block.gpsimd
            def _(pool):
                rotate(pool, nc.gpsimd, pool_step, [c8[:, 6, :]], [c8[:, 7, :]], scratch[:, 2, :], scratch[:, 3, :])
        sc = scratch[:, 4:6, :]
        pr = scratch[:, 6:8, :]
        pt = ring[:].rearrange("p s n -> p (s n)").rearrange("p (b k n) -> p b k n", b=2, k=4)
        stats = rstd[0][:, 0:8]

        def scores(h, qt):
            r = slice(32 * (h % 4), 32 * (h % 4) + 32)
            qs, ks = slice(qt * P, (qt + 1) * P), slice(0, (qt + 1) * P)
            return [(q[:, h, qs], (c8 if h < 4 else kn)[:, h % 4, ks]), (q[r, 8 + h // 4, qs], c8[r, 6, ks]), (q[r, 10 + h // 4, qs], c8[r, 7, ks])]
        attention(nc, "latent", 8, scores, lambda qt: qt + 1, 192 ** -0.5, lambda h, qt: cst("causal", 384 - P * qt, P * (qt + 1)),
                  lambda h, k: vals[:, k, h * P:(h + 1) * P], P, lambda h: slice(0, P), lambda h: yT[:, h, :],
                  banks, sc, pr, pt, stats, ident)


def delta_rule(nc, dram, layer, yT, small, cum, smallN, cumN, col, cst, ones, ring, banks, ident, scratch, rstd,
               xn, norm, acc, hT):
    B4 = 4
    with ExitStack() as held:
        def sb(name, shape, dt=F32):
            return held.enter_context(nc.sbuf_tensor(name, shape, dt))
        xp = sb("gdn_qkv", [P, 16, T + 3])
        with stage(nc, "gdn_zeroed") as (block, zeroed):
            @block.vector
            def _(dve):
                nc.vector.memset(xp[:, :, 0:3], 0.0)
        linears(nc, "gdn_in", [
            Linear("narrow", dram["w_narrow"], layer, 1, DC, xn,
                   [("dve", True, lambda f, ps, s: nc.vector.tensor_scalar(scratch[:, 7, :], ps, col("small_b"), None, ALU.add))],
                   fed=True),
            Linear("gdn_qkv", dram["w_gdn_qkv"], layer * 16, 16, DC, xn,
                   conv_steps(nc, xp, lambda f, k: col("conv_gdn", f * 4 + k), None, acc))],
            ring, banks, pre=norm, spill=(dram["stream"], hT[:].rearrange("p c n -> p (c n)")))
        narrow_rows(nc, small, cum, smallN, cumN, col, ones, banks, ident, scratch)
        rmsnorm(nc, "gdn_l2", lambda c: xp[:, c, 0:T], lambda c: xp[:, c, 0:T], 8, 1, ones, 1.0, None,
                lambda c: scratch[:, c, :], rstd, banks, mean=False)
        acT = sb("gdn_acT", [P, B4, TT, P])
        qg = sb("gdn_qg", [P, B4, T])
        kd = sb("gdn_kd", [P, B4, TT, P])
        uN = yT[:].rearrange("p c (t n) -> p c t n", n=P)[:, 0:4]
        wT = yT[:, 4:8, :]
        AT = scratch[:].rearrange("p c (t n) -> p c t n", n=P)[:, 0:4]
        Tn = scratch[:].rearrange("p c (t n) -> p c t n", n=P)[:, 4:8]
        Tt = sb("gdn_Tt", [P, B4, TT, P])
        vb = sb("gdn_vb", [P, B4, TT, P])
        kb = sb("gdn_kb", [P, B4, TT, P])
        ring4 = ring[:].rearrange("p s (a t n) -> p s a t n", t=TT, n=P)
        Dm = [ring4[:, 0, 0], ring4[:, 0, 1]]
        eg = [ring4[:, 1, 0], ring4[:, 1, 1]]
        am = [ring4[:, 2, 0], ring4[:, 2, 1]]
        Wb = [ring4[:, 3, 0], ring4[:, 3, 1]]
        S = rstd[0].rearrange("p (x n) -> p x n", n=P)
        Sd = rstd[1].rearrange("p (x n) -> p x n", n=P)
        vn = sb("gdn_vn", [P, B4, P])
        g_last = sb("gdn_last", [P, B4, 8])
        g_end = sb("gdn_end", [P, B4, TT])
        kbs = sb("gdn_kbs", [P, TT, B4])

        for hb in range(2):
            heads = [4 * hb + x for x in range(B4)]
            g0 = A_ROWS + 4 * hb
            b0 = BETA_ROWS + 4 * hb
            with stage(nc, "products_done differ masked exps ends_done dve_step banks_used ends_exp") as (
                    block, products, differ, masked, exps, ends, dve_step, used, ends_exp):
                @block.tensor
                def _(pe):
                    for x, h in enumerate(heads):
                        b = 4 * (x % 2)
                        if x >= 2:
                            pe.wait_ge(used, x - 1)
                        q_, k_ = xp[:, h // 2, :], xp[:, 4 + h // 2, :]
                        spread_row(nc, banks[b], cum, A_ROWS, h, ident)
                        spread_row(nc, banks[b + 1], small, BETA_ROWS, h, ident)
                        for n, r in ((2, q_), (3, k_)):
                            for t in range(TT):
                                s = slice(t * P, (t + 1) * P)
                                last = nc.tensor.matmul(banks[b + n][:, s], k_[:, s], r[:, s], start=True, stop=True)
                        last.then_inc(products, 1)

                @block.vector
                def _(dve):
                    v = nc.vector
                    link = Chain(dve, dve_step)
                    for x, h in enumerate(heads):
                        b = 4 * (x % 2)
                        dve.wait_ge(products, x + 1)
                        v.tensor_tensor(Dm[x % 2], tiles4(banks[b]), cumN[:, :, A_ROWS + h:A_ROWS + h + 1].to_broadcast([P, TT, P]),
                                        ALU.subtract).then_inc(differ, 1)
                        dve.wait_ge(differ, x + 1)
                        v.tensor_tensor(Dm[x % 2], Dm[x % 2], wide(cst("neg64")), ALU.add).then_inc(masked, 1)
                        v.tensor_copy(g_last[:, x, :], banks[b].rearrange("p (c n) -> p c n", n=64)[:, :, 63:64].squeeze(2))
                        t_ = tiles4(banks[b])
                        v.tensor_copy(g_end[0:64, x, :], t_[0:64, :, 63:64].squeeze(2))
                        link(v.tensor_copy(g_end[64:128, x, :], t_[64:128, :, 127:128].squeeze(2)))
                        v.tensor_tensor(g_end[:, x, :], g_end[:, x, :], cumN[:, :, A_ROWS + h:A_ROWS + h + 1].squeeze(2), ALU.subtract)\
                            .then_inc(ends, 1)
                        dve.wait_ge(exps, 2 * x + 2)
                        v.scalar_tensor_tensor(acT[:, x].rearrange("p t n -> p (t n)"), banks[b + 2], GDN_SCALE,
                                               Dm[x % 2].rearrange("p t n -> p (t n)"), ALU.mult, ALU.mult)
                        link(v.tensor_tensor(AT[:, x], tiles4(banks[b + 3]), Dm[x % 2], ALU.mult))
                        link(v.tensor_tensor(AT[:, x], AT[:, x], tiles4(banks[b + 1]), ALU.mult))
                        link(v.tensor_tensor(AT[:, x], AT[:, x], wide(cst("strict64")), ALU.mult))
                        v.scalar_tensor_tensor(qg[:, x, :], xp[:, h // 2, 0:T], GDN_SCALE, eg[x % 2].rearrange("p t n -> p (t n)"),
                                               ALU.mult, ALU.mult).then_inc(used, 1)
                    dve.wait_ge(ends_exp, 3)
                    v.tensor_tensor(kbs[:], kbs[:], smallN[:, :, b0:b0 + B4], ALU.mult)

                @block.scalar
                def _(act):
                    for x in range(B4):
                        act.wait_ge(ends, x + 1)
                        if x >= 2:
                            act.wait_ge(used, x - 1)
                        nc.scalar.activation(eg[x % 2], tiles4(banks[4 * (x % 2)]), ACT.Exp).then_inc(exps, 1)
                        act.wait_ge(masked, x + 1)
                        nc.scalar.activation(Dm[x % 2], Dm[x % 2], ACT.Exp).then_inc(exps, 1)
                    act.wait_ge(ends, B4)
                    nc.scalar.activation(g_end[:], g_end[:], ACT.Exp).then_inc(ends_exp, 1)
                    nc.scalar.activation(g_last[:], g_last[:], ACT.Exp).then_inc(ends_exp, 1)
                    nc.scalar.activation(kbs[:], cumN[:, :, g0:g0 + B4], ACT.Exp).then_inc(ends_exp, 1)

            with stage(nc, "turned scaled dve_step t_ready t_turned t_copied") as (
                    block, turned, scaled, dve_step, t_ready, t_turned, t_copied):
                @block.tensor
                def _(pe):
                    for x, h in enumerate(heads):
                        b = 2 * (x % 2)
                        if x >= 2:
                            pe.wait_ge(scaled, x - 1)
                        for n, c in enumerate((8 + h, 4 + h // 2)):
                            for t in range(TT):
                                s = slice(t * P, (t + 1) * P)
                                last = nc.tensor.transpose(banks[b + n][:, s], xp[:, c, s], ident)
                        last.then_inc(turned, 1)
                    for x in range(B4):
                        pe.wait_ge(t_ready, x + 1)
                        for t in range(TT):
                            last = nc.tensor.transpose(banks[4 + x][:, t * P:(t + 1) * P], Tt[:, x, t, :], ident)
                        last.then_inc(t_turned, 1)

                @block.vector
                def _(dve):
                    v = nc.vector
                    link = Chain(dve, dve_step)
                    for x, h in enumerate(heads):
                        b = 2 * (x % 2)
                        dve.wait_ge(turned, x + 1)
                        v.tensor_tensor(vb[:, x], tiles4(banks[b]), smallN[:, :, BETA_ROWS + h:BETA_ROWS + h + 1].to_broadcast([P, TT, P]), ALU.mult)
                        v.tensor_tensor(kb[:, x], tiles4(banks[b + 1]), kbs[:, :, x:x + 1].to_broadcast([P, TT, P]), ALU.mult)
                        v.tensor_tensor(kd[:, x], tiles4(banks[b + 1]), bc(g_end[:, x, :], P), ALU.mult).then_inc(scaled, 1)
                    for x in range(B4):
                        link(v.tensor_tensor(Tt[:, x], AT[:, x], wide(cst("level", 0, P)), ALU.mult))
                        v.tensor_tensor(Tt[:, x], wide(ident), Tt[:, x], ALU.subtract).then_inc(t_ready, 1)

                @block.scalar
                def _(act):
                    for x in range(B4):
                        act.wait_ge(t_turned, x + 1)
                        nc.scalar.copy(Tn[:, x], tiles4(banks[4 + x])).then_inc(t_copied, 1)

            jobs = [(k, x) for k in range(1, 6) for x in range(B4)]
            with stage(nc, "level_ready w_done w_copied v_done half_updated updated") as (
                    block, level_ready, w_done, w_copied, v_done, half_updated, updated):
                @block.gpsimd
                def _(pool):
                    for j, (k, x) in enumerate(jobs):
                        if j >= 2:
                            pool.wait_ge(w_done, j - 1)
                        nc.gpsimd.tensor_tensor(am[j % 2], AT[:, x], wide(cst("level", k * P, P)), ALU.mult).then_inc(level_ready, 1)

                @block.tensor
                def _(pe):
                    def w(j):
                        k, x = jobs[j]
                        pe.wait_ge(level_ready, j + 1)
                        if j >= 4:
                            pe.wait_ge(updated, j - 3)
                        if j >= 2:
                            pe.wait_ge(w_copied, j - 1)
                        for t in range(TT):
                            last = nc.tensor.matmul(banks[j % 2][:, t * P:(t + 1) * P], am[j % 2][:, t, :], Tn[:, x, t, :], start=True, stop=True)
                        last.then_inc(w_done, 1)

                    w(0)
                    for j, (k, x) in enumerate(jobs):
                        if j + 1 < len(jobs):
                            w(j + 1)
                        pe.wait_ge(w_copied, j + 1)
                        if j >= 2:
                            pe.wait_ge(updated, j - 1)
                        for t in range(TT):
                            s = slice(t * P, (t + 1) * P)
                            last = nc.tensor.matmul(banks[2 + j % 2][:, s], Wb[j % 2][:, t, :], Tt[:, x, t, :], start=True, stop=True)
                            if k < 5:
                                last = nc.tensor.matmul(banks[4 + j % 2][:, s], Tt[:, x, t, :], Wb[j % 2][:, t, :], start=True, stop=True)
                        last.then_inc(v_done, 1)

                @block.scalar
                def _(act):
                    for j in range(len(jobs)):
                        act.wait_ge(w_done, j + 1)
                        if j >= 2:
                            act.wait_ge(v_done, j - 1)
                        nc.scalar.copy(Wb[j % 2], tiles4(banks[j % 2])).then_inc(w_copied, 1)

                @block.vector
                def _(dve):
                    for j, (k, x) in enumerate(jobs):
                        dve.wait_ge(v_done, j + 1)
                        last = nc.vector.tensor_tensor(Tt[:, x], Tt[:, x], tiles4(banks[2 + j % 2]), ALU.subtract)
                        if k < 5:
                            last = nc.vector.tensor_tensor(Tn[:, x], Tn[:, x], tiles4(banks[4 + j % 2]), ALU.subtract)
                        last.then_inc(updated, 1)

            with stage(nc, "solved u_copied w_copied") as (block, solved, u_copied, w_copied):
                @block.tensor
                def _(pe):
                    for x in range(B4):
                        if x >= 2:
                            pe.wait_ge(u_copied, x - 1)
                            pe.wait_ge(w_copied, x - 1)
                        for t in range(TT):
                            s = slice(t * P, (t + 1) * P)
                            nc.tensor.matmul(banks[x % 2][:, s], Tt[:, x, t, :], vb[:, x, t, :], start=True, stop=True)
                            last = nc.tensor.matmul(banks[2 + x % 2][:, s], kb[:, x, t, :], Tt[:, x, t, :], start=True, stop=True)
                        last.then_inc(solved, 1)

                @block.scalar
                def _(act):
                    for x in range(B4):
                        act.wait_ge(solved, x + 1)
                        nc.scalar.copy(uN[:, x], tiles4(banks[x % 2])).then_inc(u_copied, 1)

                @block.vector
                def _(dve):
                    for x in range(B4):
                        dve.wait_ge(solved, x + 1)
                        nc.vector.tensor_copy(wT[:, x, :], banks[2 + x % 2]).then_inc(w_copied, 1)

            with stage(nc, "state_ready ws_done v_new_ready o_done ds_done o_copied decayed") as (
                    block, state_ready, ws_done, v_new, o_done, ds_done, o_copied, decayed):
                @block.tensor
                def _(pe):
                    for c in range(8):
                        t, half = divmod(c, 2)
                        r = slice(64 * half, 64 * half + 64)
                        s = slice(64 * c, 64 * c + 64)
                        pe.wait_ge(state_ready, c + 1)
                        for x in range(B4):
                            last = nc.tensor.matmul(banks[0][r, x * P:(x + 1) * P], wT[:, x, s], S[:, x, :], start=True, stop=True)
                        last.then_inc(ws_done, 1)
                        pe.wait_ge(v_new, c + 1)
                        if c >= 1:
                            pe.wait_ge(o_copied, c)
                        for x in range(B4):
                            o = banks[1][:, x * 64:(x + 1) * 64]
                            nc.tensor.matmul(o, S[:, x, :], qg[:, x, s], start=True, stop=False)
                            last = nc.tensor.matmul(o, vn[r, x, :], acT[r, x, t, 64 * half:64 * half + 64], start=False, stop=True)
                        last.then_inc(o_done, 1)
                        for x in range(B4):
                            last = nc.tensor.matmul(banks[2][:, x * P:(x + 1) * P], kd[r, x, t, :], vn[r, x, :], start=True, stop=True)
                        last.then_inc(ds_done, 1)

                @block.vector
                def _(dve):
                    v = nc.vector
                    v.memset(S[:], 0.0).then_inc(state_ready, 1)
                    dve.wait_ge(state_ready, 1)
                    for c in range(8):
                        t, half = divmod(c, 2)
                        r = slice(64 * half, 64 * half + 64)
                        dve.wait_ge(ws_done, c + 1)
                        v.tensor_tensor(vn[r], uN[r, :, t, :], banks[0][r, :].rearrange("p (x n) -> p x n", n=P), ALU.subtract)\
                            .then_inc(v_new, 1)
                        v.tensor_tensor(Sd[:], S[:], g_last[:, :, c:c + 1].to_broadcast([P, B4, P]), ALU.mult).then_inc(decayed, 1)
                        dve.wait_ge(decayed, c + 1)
                        dve.wait_ge(ds_done, c + 1)
                        v.tensor_tensor(S[:], Sd[:], banks[2].rearrange("p (x n) -> p x n", n=P), ALU.add).then_inc(state_ready, 1)
                        dve.wait_ge(state_ready, c + 2)

                @block.scalar
                def _(act):
                    for c in range(8):
                        act.wait_ge(o_done, c + 1)
                        nc.scalar.copy(xp[:, 8 + 4 * hb:12 + 4 * hb, 64 * c:64 * c + 64],
                                       banks[1][:, 0:256].rearrange("p (x n) -> p x n", n=64)).then_inc(o_copied, 1)
        rmsnorm(nc, "gdn_norm", lambda c: xp[:, 8 + c, 0:T], lambda c: yT[:, c, :], 8, 1, ones, P, lambda c: col("gdn_g"),
                lambda c: scratch[:, c, :], rstd, banks)


def program(nc, dram, out, upto="final", start=None):
    with ExitStack() as held:
        def sb(name, shape, dt=F32):
            return held.enter_context(nc.sbuf_tensor(name, shape, dt))
        psum = held.enter_context(nc.psum_tensor("banks", [P, 8, 512], F32))
        hT = sb("hT", [P, DC, T])
        scratch = sb("scratch", [P, 8, T])
        ring = sb("ring", [P, SLOTS, 8 * P])
        rs = sb("rstd", [P, 2, T])
        rstd = [rs[:, i, :] for i in range(2)]
        ones = sb("ones", [P, P])
        halves = sb("halves", [P, P])
        ident = sb("ident", [P, P])
        with stage(nc, "filled made") as (block, filled, made):
            @block.gpsimd
            def _(pool):
                nc.gpsimd.memset(ident[:], 0.0).then_inc(filled, 1)
                pool.wait_ge(filled, 1)
                nc.gpsimd.affine_select(out=ident[:], in_=ident[:], compare_op=ALU.not_equal, fill=1.0, base=0,
                                        pattern=[[-1, P]], channel_multiplier=1)

            @block.vector
            def _(dve):
                nc.vector.memset(ones[:], 1.0)
                nc.vector.memset(halves[:], 0.0).then_inc(made, 1)
                dve.wait_ge(made, 1)
                for k in range(2):
                    nc.vector.memset(halves[64 * k:64 * k + 64, 64 * k:64 * k + 64], 1.0)

        def finished():
            with stage(nc, "stored") as (block, stored):
                @block.sync
                def _(sp):
                    sp.dma_start(out, hT[:].rearrange("p c n -> p (c n)")).then_inc(stored, 16)
                    sp.wait_ge(stored, 16)

        if start in (None, "h1", "h2"):
            with nc.sbuf_tensor("xnT", [P, DC, T], F32) as xnT:
                first_block(nc, dram, sb, psum, hT, xnT, scratch, ring, rstd, ones[:], halves[:], ident[:], upto, start)
        else:
            with stage(nc, "h_loaded") as (block, loaded):
                @block.sync
                def _(sp):
                    sp.dma_start(hT[:].rearrange("p c n -> p (c n)"), dram["xT"]).then_inc(loaded, 16)
                    sp.wait_ge(loaded, 16)
        if upto in ("h1", "h2", "h3"):
            return finished()
        second_block(nc, dram, psum, hT, scratch, ring, rstd, ones[:], ident[:], upto)
        if upto == "final":
            final_g = sb("final_g", [P, DC])
            banks = [psum[:, b, :] for b in range(8)]
            with stage(nc, "final_g_loaded") as (block, loaded):
                @block.sync
                def _(sp):
                    sp.dma_start(final_g[:], dram["final_g"]).then_inc(loaded, 16)
                    sp.wait_ge(loaded, 16)
            rmsnorm(nc, "final_norm", lambda c: hT[:, c, :], lambda c: hT[:, c, :], DC, DC, ones[:], D,
                    lambda c: final_g[:, c:c + 1], lambda c: scratch[:, c, :], rstd, banks)
        finished()



def _tiles(w):
    import numpy as np
    k, n = w.shape
    return np.ascontiguousarray(w.reshape(k // P, P, n // P, P).transpose(2, 1, 0, 3)).reshape(n // P, P, k)


def _strips(w, n=512):
    import numpy as np
    k, m = w.shape
    return np.ascontiguousarray(w.reshape(k // P, P, m // n, n).transpose(2, 1, 0, 3)).reshape(m // n, P, k // P * n)


def _cols(v):
    return v.reshape(-1, P).T


def _chunks(x):
    import numpy as np
    k, n = x.shape
    return np.ascontiguousarray(x.reshape(k // P, P, n).transpose(1, 0, 2)).reshape(P, -1)


def _layout_first(a):
    import numpy as np
    d = {}
    d["xT"] = _chunks(a["x"][0].T)
    d["memT"] = _chunks(a["mem"][0].T)
    w = a["w_in"][0]
    d["w_in"] = np.concatenate([_tiles(w[:, 0:1024]), _tiles(w[:, 1536:2048])])
    d["w_in_v"] = _strips(w[:, 1024:1536])
    dist = np.arange(P)[:, None] - (np.arange(512)[None, :] - 384)
    d["bias"] = np.ascontiguousarray(a["rel_bias"][0][:, np.clip(dist, -63, 128) + 63].transpose(1, 0, 2)).reshape(P, -1)
    c = {n: np.zeros((P, 16, 32), np.float32) for n in ("c_re", "c_im")}
    b = {n: np.zeros((P, 4, 128), np.float32) for n in ("b_re", "b_im")}
    for n in ("re", "im"):
        src_c, src_b = a["ssm_c_" + n][0], a["ssm_b_" + n][0]
        for g in range(32):
            i, k = divmod(g, 2)
            c["c_" + n][64 * k:64 * k + 64, i, 16 * k:16 * k + 16] = src_c[g].T
            p = 32 * (i % 4) + 16 * k
            b["b_" + n][p:p + 16, i // 4, 64 * k:64 * k + 64] = src_b[g].T
    for n, v in list(c.items()) + list(b.items()):
        d[n] = v.reshape(P, -1)
    d["w_glu"] = _tiles(a["ssm_w_glu"][0])
    d["w_out"] = _tiles(a["w_out"][0])
    for n in ("w_mem_q", "w_mem_k", "w_mem_o"):
        d[n] = _tiles(a[n][0])
    d["w_mem_v"] = _strips(a["w_mem_v"][0])
    d["w_peer_q"] = _tiles(a["w_peer_q"][0])
    d["peer_keys"] = np.ascontiguousarray(a["peer_keys"][0].reshape(16, P, P).transpose(2, 0, 1)).reshape(P, -1)
    d["peer_u"] = _tiles(a["peer_u"][0].T)
    d["peer_v"] = a["peer_v"][0].reshape(P, P, D)
    state = lambda v: v.reshape(16, P).T
    parts = dict(mix_g=_cols(a["norm_mix_g"][0]), att_q_g=_cols(np.tile(a["att_q_g"][0], 2)),
                 att_k_g=_cols(np.tile(a["att_k_g"][0], 2)), lam_re=state(a["ssm_lam_re"][0]),
                 lam_im=state(a["ssm_lam_im"][0]), log_step=state(np.repeat(a["ssm_log_step"][0], 64)),
                 ssm_d=_cols(a["ssm_d"][0].reshape(-1)), b_glu=_cols(a["ssm_b_glu"][0]),
                 mixed_g=np.concatenate([_cols(a["att_out_g"][0]), _cols(a["ssm_out_g"][0])], axis=1),
                 mem_g=_cols(a["norm_mem_g"][0]), memkv_g=_cols(a["norm_memkv_g"][0]), mem_q_g=_cols(a["mem_q_g"][0]),
                 mem_k_g=_cols(a["mem_k_g"][0]), peer_g=_cols(a["norm_peer_g"][0]))
    assert list(parts) == list(VEC1)
    d["vec1"] = np.concatenate([parts[n] for n in VEC1], axis=1)
    return d


def _layout_second(a):
    import numpy as np
    d = {}
    a = {n[:-2]: v for n, v in a.items() if n.endswith("_2")}
    both = lambda f: np.concatenate([f(l) for l in range(LAYERS)])
    at = np.cumsum([0, 1024, 1536, 16, 512, 256, 64, 2048, 1024, 8, 8, 3072])
    part = lambda l, n: a["w_in"][l][:, at[n]:at[n + 1]]
    d["w_ssd_z"] = both(lambda l: _tiles(part(l, 0)))
    d["w_ssd_xbc"] = both(lambda l: _tiles(part(l, 1)))
    d["w_gdn_qkv"] = both(lambda l: _tiles(part(l, 6)))
    d["w_gdn_z"] = both(lambda l: _tiles(part(l, 7)))
    d["w_gate"] = both(lambda l: _tiles(part(l, 10)))

    def narrow(l):
        w = np.zeros((D, P), np.float32)
        w[:, DT_ROWS:DT_ROWS + 16] = part(l, 2)
        w[:, BETA_ROWS:BETA_ROWS + 8] = part(l, 8)
        w[:, A_ROWS:A_ROWS + 8] = part(l, 9)
        return _tiles(w)
    d["w_narrow"] = both(narrow)

    def mla_in(l):
        kr = part(l, 5)
        return _tiles(np.concatenate([part(l, 3), part(l, 4), np.tile(kr[:, 0:32], (1, 4)), np.tile(kr[:, 32:64], (1, 4))], axis=1))
    d["w_mla_in"] = both(mla_in)

    def uq(l):
        w = a["mla_w_uq"][l].reshape(512, 8, 192)
        return _tiles(np.concatenate([w[:, :, n0:n1].reshape(512, -1) for n0, n1 in ((0, 128), (128, 160), (160, 192))], axis=1))
    d["w_mla_uq"] = both(uq)
    ukv = lambda l: a["mla_w_ukv"][l].reshape(256, 8, 256)
    d["w_mla_uk"] = both(lambda l: _tiles(ukv(l)[:, :, 0:128].reshape(256, -1)))
    d["w_mla_uv"] = both(lambda l: _strips(ukv(l)[:, :, 128:256].reshape(256, -1)))
    for n, src in (("w_ssd_out", "w_ssd_out"), ("w_mla_out", "w_mla_out"), ("w_gdn_out", "w_gdn_out"), ("w_mix", "w_out"),
                   ("w_up", "w_up")):
        d[n] = both(lambda l: _tiles(a[src][l]))
    d["w_down"] = both(lambda l: np.ascontiguousarray(
        _tiles(a["w_down"][l]).reshape(8, P, 4, 1024).transpose(2, 0, 1, 3)).reshape(32, P, 1024))
    d["positions"] = np.tile(a["positions"].reshape(1, T), (P, 1))

    m, l = np.arange(P)[:, None], np.arange(P)[None, :]
    neg = lambda keep: np.where(keep, 0.0, NEG)
    levels = [((m ^ l) >= 1 << k) & ((m ^ l) < 2 << k) & (l > m) for k in range(6)]
    inv = 10000.0 ** (-np.arange(0, 64, 2, dtype=np.float32) / np.float32(64))
    parts = dict(neg128=neg(l >= m), neg64=neg((l >= m) & (l // 64 == m // 64)), strict64=(l > m) & (l // 64 == m // 64),
                 level=np.concatenate(levels, axis=1), causal=np.concatenate([np.zeros((P, 384)), neg(l <= m)], axis=1),
                 inv_freq=np.tile(inv, 4)[:, None])
    assert list(parts) == list(CONST)
    d["consts"] = np.concatenate([np.asarray(v, np.float32) for v in parts.values()], axis=1)

    def vec(l):
        conv = lambda w: w.reshape(4, -1, P).transpose(2, 1, 0).reshape(P, -1)
        small = np.zeros((2, P, 1), np.float32)
        small[0, DT_ROWS:DT_ROWS + 16, 0], small[0, A_ROWS:A_ROWS + 8, 0] = a["ssd_dt_bias"][l], a["gdn_dt_bias"][l]
        small[1, DT_ROWS:DT_ROWS + 16, 0], small[1, A_ROWS:A_ROWS + 8, 0] = a["ssd_a_log"][l], a["gdn_a_log"][l]
        parts = dict(norm1=_cols(a["norm1_g"][l]), conv_ssd=conv(a["ssd_conv_w"][l]), conv_ssd_b=_cols(a["ssd_conv_b"][l]),
                     small_b=small[0], a_log=small[1], ssd_d=_cols(np.repeat(a["ssd_d"][l], 64)), ssd_g=_cols(a["ssd_norm_g"][l]),
                     mla_q_g=_cols(a["mla_q_norm_g"][l]), mla_kv_g=_cols(a["mla_kv_norm_g"][l]), conv_gdn=conv(a["gdn_conv_w"][l]),
                     gdn_g=_cols(a["gdn_norm_g"][l]), norm2=_cols(a["norm2_g"][l]))
        assert list(parts) == list(VEC2)
        return np.concatenate(list(parts.values()), axis=1)
    d["vec2"] = np.stack([vec(l) for l in range(LAYERS)])
    d["final_g"] = _cols(a["final_norm_g"])
    return d


def layout(a):
    import numpy as np
    a = {n: np.asarray(v) for n, v in a.items()}
    d = _layout_first(a)
    d.update(_layout_second(a))
    return {n: np.ascontiguousarray(v) for n, v in d.items()}


def kernel(**inputs):
    import numpy as np
    import concourse.bacc as bacc
    from concourse.bass_utils import run_bass_kernel_spmd

    nc = bacc.Bacc("TRN2", target_bir_lowering=False, num_devices=1)
    arrays = {f"in_{n}": v for n, v in layout(inputs).items()}
    dram = {n[3:]: nc.dram_tensor(n, v.shape, mybir.dt.from_np(v.dtype), kind="ExternalInput").ap()
            for n, v in arrays.items()}
    dram["gates"] = nc.dram_tensor("gates", (PK, PK, T), F32, kind="Internal").ap()
    dram["stream"] = nc.dram_tensor("stream", (P, DC * T), F32, kind="Internal").ap()
    out = nc.dram_tensor("out", (P, DC * T), F32, kind="ExternalOutput").ap()
    program(nc, dram, out)
    result = run_bass_kernel_spmd(nc, [arrays], core_ids=[0]).results[0]["out"]
    return np.ascontiguousarray(np.asarray(result).reshape(P, DC, T).transpose(2, 1, 0)).reshape(1, T, D)
```

```python
import math
from contextlib import ExitStack, contextmanager

import concourse.bass as bass
from concourse import mybir

F32 = mybir.dt.float32
F32R = mybir.dt.float32r
I32 = mybir.dt.int32
U32 = mybir.dt.uint32
ALU = mybir.AluOpType
ACT = mybir.ActivationFunctionType
AX = mybir.AxisListType

P = 128
T = 512
TT = T // P
D = 1024
DC = D // P
EPS = 1e-6
NEG = -1e30
SLOTS = 4
LAYERS = 2

TWO_PI = 2.0 * math.pi
PI_HIGH = 6.28125
PI_LOW = TWO_PI - PI_HIGH


@contextmanager
def stage(nc, names):
    with ExitStack() as held:
        sems = [held.enter_context(nc.semaphore(n)) for n in names.split()]
        with nc.Block() as block:
            yield (block, *sems)
        for s in sems:
            nc.gpsimd.sem_clear(s)
        nc.all_engine_barrier()


class Chain:

    def __init__(self, eng, sem):
        self.eng, self.sem, self.n = eng, sem, 0

    def __call__(self, ins):
        ins.then_inc(self.sem, 1)
        self.n += 1
        self.eng.wait_ge(self.sem, self.n)


def over(eng, n, body):
    body(0, True)
    if n > 1:
        with eng.Fori(1, n) as i:
            body(i, False)


def row(w, i):
    return w[bass.ds(i, 1)].rearrange("o p n -> p (o n)")


def product(nc, out, w_high, w_low, x_high, x_low, start, stop):
    nc.tensor.matmul(out, w_high, x_high, start=start, stop=False)
    nc.tensor.matmul(out, w_high, x_low, start=False, stop=False)
    return nc.tensor.matmul(out, w_low, x_high, start=False, stop=stop)


class Norm:
    NAMES = "squared_act squared_dve summed rooted inverse spread scaled high low"

    def __init__(self, nc, x, y, chunks, group, tools, width, gain, scratch, banks, pair=None, mean=True, parts=1):
        self.nc, self.x, self.chunks, self.group, self.width, self.gain = nc, x, chunks, group, width, gain
        self.scratch, self.banks, self.pair, self.mean, self.parts = scratch, banks, pair, mean, parts
        buffer, self.eps, self.ident, columns = tools
        self.columns = columns[:, 0:1] if parts == 1 else columns[:, 1:3]
        self.y = scratch if pair else y
        self.groups = chunks // group
        self.tiles = x(0).shape[-1] // P
        n = self.groups * self.tiles * parts
        self.sums, self.root = banks[4][:, 0:n], buffer[:, 0:n]

    def take(self, sems):
        (self.squared_act, self.squared_dve, self.summed, self.rooted, self.inverse, self.spread, self.scaled, self.high,
         self.low) = sems

    def act(self, act):
        nc = self.nc
        for c in range(0, self.chunks, 2):
            nc.scalar.activation(self.scratch(c), self.x(c), ACT.Square).then_inc(self.squared_act, 1)
        act.wait_ge(self.summed, 1)
        nc.scalar.activation(self.root, self.sums, ACT.Sqrt, scale=1.0 / self.width if self.mean else 1.0, bias=self.eps)\
            .then_inc(self.rooted, 1)
        if self.pair:
            for c in range(self.chunks):
                act.wait_ge(self.scaled, c + 1)
                nc.scalar.copy(self.pair[0](c), self.y(c)).then_inc(self.high, 1)

    def pe(self, pe):
        nc = self.nc
        for g in range(self.groups):
            for t in range(self.tiles):
                n = (g * self.tiles + t) * self.parts
                for k in range(self.group):
                    c = g * self.group + k
                    if t == 0:
                        pe.wait_ge(self.squared_dve if c % 2 else self.squared_act, c // 2 + 1)
                    last = nc.tensor.matmul(self.sums[:, n:n + self.parts], self.scratch(c)[:, t * P:(t + 1) * P], self.columns,
                                            start=(k == 0), stop=(k == self.group - 1))
        last.then_inc(self.summed, 1)
        pe.wait_ge(self.inverse, 1)
        for g in range(self.groups):
            if g >= 3:
                pe.wait_ge(self.scaled, (g - 2) * self.group)
            for t in range(self.tiles):
                n = (g * self.tiles + t) * self.parts
                w = P // self.parts
                for k in range(self.parts):
                    last = nc.tensor.matmul(self.banks[5 + g % 3][k * w:(k + 1) * w, t * P:(t + 1) * P],
                                            self.root[:, n + k:n + k + 1].to_broadcast([P, w]), self.ident, start=True, stop=True)
            last.then_inc(self.spread, 1)

    def dve(self, dve):
        nc = self.nc
        for c in range(1, self.chunks, 2):
            nc.vector.tensor_tensor(self.scratch(c), self.x(c), self.x(c), ALU.mult).then_inc(self.squared_dve, 1)
        dve.wait_ge(self.rooted, 1)
        nc.vector.reciprocal(self.root, self.root).then_inc(self.inverse, 1)
        for g in range(self.groups):
            r = self.banks[5 + g % 3][:, 0:self.tiles * P]
            dve.wait_ge(self.spread, g + 1)
            for k in range(self.group):
                c = g * self.group + k
                if self.gain is None:
                    nc.vector.tensor_tensor(self.y(c), self.x(c), r, ALU.mult).then_inc(self.scaled, 1)
                else:
                    nc.vector.scalar_tensor_tensor(self.y(c), self.x(c), self.gain(c), r, ALU.mult, ALU.mult)\
                        .then_inc(self.scaled, 1)

    def pool(self, pool):
        if self.pair:
            for c in range(self.chunks):
                pool.wait_ge(self.high, c + 1)
                self.nc.gpsimd.tensor_tensor(self.pair[1](c), self.y(c), self.pair[0](c).bitcast(F32), ALU.subtract)\
                    .then_inc(self.low, 1)


class Split:
    NAMES = "high low"

    def __init__(self, nc, x, chunks, pair):
        self.nc, self.x, self.chunks, self.pair = nc, x, chunks, pair

    def take(self, sems):
        self.high, self.low = sems

    def act(self, act):
        for c in range(self.chunks):
            self.nc.scalar.copy(self.pair[0](c), self.x(c)).then_inc(self.high, 1)

    def pe(self, pe):
        pass

    def dve(self, dve):
        for c in range(self.chunks):
            dve.wait_ge(self.high, c + 1)
            self.nc.vector.tensor_tensor(self.pair[1](c), self.x(c), self.pair[0](c).bitcast(F32), ALU.subtract)\
                .then_inc(self.low, 1)

    def pool(self, pool):
        pass


def alone(nc, name, work):
    with stage(nc, " ".join(f"{name}_{n}" for n in work.NAMES.split())) as (block, *sems):
        work.take(sems)
        block.scalar(work.act)
        block.tensor(work.pe)
        block.vector(work.dve)
        block.gpsimd(work.pool)


def walk(eng, tiles, body):
    m = max(1, (tiles - 2) // SLOTS)
    for f in range(min(SLOTS, tiles)):
        body(0, f)
    if m > 1:
        with eng.Fori(1, m) as i:
            for s in range(SLOTS):
                body(i, s)
    for f in range(SLOTS * m, tiles):
        body(f // SLOTS, f % SLOTS)


class Linear:

    def __init__(self, name, w, at, tiles, kc, x, steps, n=T, behind=None, fed=False, lag=False):
        self.fed, self.lag = fed, lag
        self.name, self.w, self.at, self.tiles, self.kc, self.x, self.steps, self.n, self.behind = \
            name, w, at, tiles, kc, x, steps, n, behind


def linears(nc, name, specs, ring, banks, pre=None, spill=None, fill=None):
    names = [f"{name}_w{u}_loaded" for u in range(SLOTS)] + [f"{name}_w_high", f"{name}_w_low", f"{name}_tile_done"]
    pre_names = [f"{name}_{n}" for n in pre.NAMES.split()] if pre else []
    step_names = [f"{sp.name}_step{k}" for sp in specs for k in range(len(sp.steps))]
    extra = [f"{name}_moved"]
    with ExitStack() as held:
        wH = held.enter_context(nc.sbuf_tensor(f"{name}_high_part", [P, 2, D], F32R))
        wL = held.enter_context(nc.sbuf_tensor(f"{name}_low_part", [P, 2, D], F32R))
        _linears(nc, names, pre_names, step_names, extra, specs, ring, wH, wL, banks, pre, spill, fill)


def _linears(nc, names, pre_names, step_names, extra, specs, ring, wH, wL, banks, pre, spill, fill):
    with stage(nc, " ".join(names + pre_names + step_names + extra)) as (block, *sems):
        moved = sems.pop()
        loaded, (w_high, w_low, tile_done) = sems[0:SLOTS], sems[SLOTS:SLOTS + 3]
        sems = sems[SLOTS + 3:]
        if pre:
            pre.take(sems[:len(pre_names)])
            sems = sems[len(pre_names):]
        g0 = 0
        for sp in specs:
            sp.g0 = g0
            g0 += sp.tiles
            sp.done, sems = sems[:len(sp.steps)], sems[len(sp.steps):]
            sp.bank_read = sp.done[max(k for k, st in enumerate(sp.steps) if st[1])]
        total = g0

        def spec_of(g):
            return next(sp for sp in specs if sp.g0 <= g < sp.g0 + sp.tiles)

        def first_four(sp, i, s):
            return isinstance(i, int) and sp.g0 + SLOTS * i + s < SLOTS

        @block.sync
        def _(eng):
            for n, sp in enumerate(specs):
                if fill and n == 1:
                    eng.wait_ge(pre.low, pre.chunks)
                    eng.dma_start(*fill).then_inc(moved, 16)

                def load(i, s, sp=sp):
                    g = sp.g0 + SLOTS * i + s
                    if not first_four(sp, i, s):
                        eng.wait_ge(w_low, g - SLOTS + 1)
                    slot = (sp.g0 + s) % SLOTS
                    eng.dma_start(ring[:, slot, 0:sp.kc * P], row(sp.w, sp.at + SLOTS * i + s)).then_inc(loaded[slot], 16)
                walk(eng, sp.tiles, load)
            if spill:
                eng.dma_start(*spill).then_inc(moved, 16)
            if spill or fill:
                eng.wait_ge(moved, 16)

        def split_high(eng, sp, i, s, behind=True):
            slot, g = (sp.g0 + s) % SLOTS, sp.g0 + SLOTS * i + s
            eng.wait_ge(loaded[slot], 16 * ((sp.g0 + s) // SLOTS + i + 1))
            if behind:
                eng.wait_ge(tile_done, g - 1)
            w = sp.kc * P
            nc.scalar.copy(wH[:, (sp.g0 + s) % 2, 0:w], ring[:, slot, 0:w]).then_inc(w_high, 1)

        def run_steps(eng, which, sp, i, s, only=None):
            f = SLOTS * i + s
            for k, (engine, reads, fn) in enumerate(sp.steps):
                if engine == which and (only is None or reads == only):
                    if k == 0:
                        eng.wait_ge(tile_done, sp.g0 + f + 1)
                    else:
                        eng.wait_ge(sp.done[k - 1], f + 1)
                    fn(f, banks[(sp.g0 + s) % SLOTS][:, 0:sp.n], s).then_inc(sp.done[k], 1)

        @block.scalar
        def _(eng):
            if pre:
                pre.act(eng)
            for g in range(min(2, total)):
                sp = spec_of(g)
                split_high(eng, sp, 0, g - sp.g0, behind=False)
            for sp in specs:
                def body(i, s, sp=sp):
                    nxt = SLOTS * i + s + 2 if isinstance(i, int) else None
                    if nxt is not None and nxt >= sp.tiles:
                        g = sp.g0 + nxt
                        if g < total:
                            to = spec_of(g)
                            split_high(eng, to, (g - to.g0) // SLOTS, (g - to.g0) % SLOTS)
                    elif nxt is not None:
                        split_high(eng, sp, nxt // SLOTS, nxt % SLOTS)
                    elif s < 2:
                        split_high(eng, sp, i, s + 2)
                    else:
                        split_high(eng, sp, i + 1, s - 2)
                    if not sp.lag:
                        run_steps(eng, "act", sp, i, s)
                        return
                    run_steps(eng, "act", sp, i, s, only=True)
                    if s > 0:
                        run_steps(eng, "act", sp, i, s - 1, only=False)
                    elif not (isinstance(i, int) and i == 0):
                        run_steps(eng, "act", sp, i - 1, SLOTS - 1, only=False)
                walk(eng, sp.tiles, body)
                if sp.lag:
                    run_steps(eng, "act", sp, (sp.tiles - 1) // SLOTS, (sp.tiles - 1) % SLOTS, only=False)

        @block.gpsimd
        def _(eng):
            if pre:
                pre.pool(eng)
            for sp in specs:
                def body(i, s, sp=sp):
                    g = sp.g0 + SLOTS * i + s
                    w, slot, half = sp.kc * P, (sp.g0 + s) % SLOTS, (sp.g0 + s) % 2
                    eng.wait_ge(w_high, g + 1)
                    nc.gpsimd.tensor_tensor(wL[:, half, 0:w], ring[:, slot, 0:w], wH[:, half, 0:w].bitcast(F32), ALU.subtract)\
                        .then_inc(w_low, 1)
                walk(eng, sp.tiles, body)

        @block.tensor
        def _(eng):
            if pre:
                pre.pe(eng)
            for n, sp in enumerate(specs):
                if sp.behind:
                    maker = next(x for x in specs if x.name == sp.behind)
                    eng.wait_ge(maker.done[-1], maker.tiles)

                def body(i, s, sp=sp, n=n):
                    g = sp.g0 + SLOTS * i + s
                    half = (sp.g0 + s) % 2
                    eng.wait_ge(w_low, g + 1)
                    if isinstance(i, int) and i == 0:
                        if g >= SLOTS:
                            before = spec_of(g - SLOTS)
                            eng.wait_ge(before.bank_read, g - SLOTS - before.g0 + 1)
                    else:
                        eng.wait_ge(sp.bank_read, SLOTS * (i - 1) + s + 1)
                    for c in range(sp.kc):
                        if sp.fed and isinstance(i, int) and i == 0 and s == 0:
                            eng.wait_ge(pre.low, c + 1)
                        w = slice(c * P, (c + 1) * P)
                        last = product(nc, banks[(sp.g0 + s) % SLOTS][:, 0:sp.n], wH[:, half, w], wL[:, half, w],
                                       sp.x[0](c), sp.x[1](c), c == 0, c == sp.kc - 1)
                    last.then_inc(tile_done, 1)
                walk(eng, sp.tiles, body)

        @block.vector
        def _(eng):
            if pre:
                pre.dve(eng)
            for sp in specs:
                walk(eng, sp.tiles, lambda i, s, sp=sp: run_steps(eng, "dve", sp, i, s))


def part(t, f):
    return t[:, bass.ds(f, 1), 0:T].squeeze(1)


def add_steps(nc, hT):
    return [("dve", True, lambda f, ps, s: nc.vector.tensor_tensor(part(hT, f), part(hT, f), ps, ALU.add))]


def chunks_of(t, base=0, n=T):
    return lambda c: t[:, base + c, 0:n]


def linear(nc, name, w, at, tiles, x, kc, ring, banks, write):
    slots = [f"{name}_w{u}_loaded" for u in range(SLOTS)]
    with stage(nc, f"{name}_tile_done {name}_tile_written " + " ".join(slots)) as (block, tile_done, tile_written, *loaded):

        @block.sync
        def _(sp):
            def step(i, first):
                for u in range(SLOTS):
                    if not first:
                        sp.wait_ge(tile_done, (i - 1) * SLOTS + u + 1)
                    sp.dma_start(ring[:, u, 0:kc * P], row(w, at + i * SLOTS + u)).then_inc(loaded[u], 16)
            over(sp, tiles // SLOTS, step)

        @block.tensor
        def _(pe):
            def step(i, first):
                for u in range(SLOTS):
                    pe.wait_ge(loaded[u], 16 * (i + 1))
                    if not first:
                        pe.wait_ge(tile_written, (i - 1) * SLOTS + u + 1)
                    for c in range(kc):
                        last = nc.tensor.matmul(banks[u], ring[:, u, c * P:(c + 1) * P], x(c), start=(c == 0), stop=(c == kc - 1))
                    last.then_inc(tile_done, 1)
            over(pe, tiles // SLOTS, step)

        @block.scalar
        def _(act):
            def step(i, first):
                for u in range(SLOTS):
                    act.wait_ge(tile_done, i * SLOTS + u + 1)
                    write(nc, i * SLOTS + u, banks[u]).then_inc(tile_written, 1)
            over(act, tiles // SLOTS, step)


def linear_tokens(nc, name, w, at, x, kc, ring, banks, rows, out, aside=None):
    weights = ring[:, :, :].rearrange("p s n -> p (s n)")[:, 0:kc * 512]
    with stage(nc, f"{name}_loaded {name}_done {name}_aside_dve {name}_aside_pool") as (block, loaded, done, *others):
        if aside:
            aside(block, *others)

        @block.sync
        def _(sp):
            sp.dma_start(weights, row(w, at)).then_inc(loaded, 16)

        @block.tensor
        def _(pe):
            pe.wait_ge(loaded, 16)
            for t in range(rows):
                for c in range(kc):
                    last = nc.tensor.matmul(banks[t], x(c)[:, t * P:(t + 1) * P], weights[:, c * 512:(c + 1) * 512],
                                            start=(c == 0), stop=(c == kc - 1))
                last.then_inc(done, 1)

        @block.scalar
        def _(act):
            for t in range(rows):
                act.wait_ge(done, t + 1)
                nc.scalar.copy(out(t), banks[t])


def rmsnorm(nc, name, x, y, chunks, group, tools, width, gain, scratch, banks, mean=True, parts=1):
    alone(nc, name, Norm(nc, x, y, chunks, group, tools, width, gain, scratch, banks, mean=mean, parts=parts))


def turn(nc, name, src, dst, chunks, tiles, banks, ident):
    with stage(nc, f"{name}_turned {name}_copied") as (block, turned, copied):
        @block.tensor
        def _(pe):
            for c in range(chunks):
                if c >= 4:
                    pe.wait_ge(copied, c - 3)
                for t in range(tiles):
                    last = nc.tensor.transpose(banks[c % 4][:, t * P:(t + 1) * P], src(c)[:, t * P:(t + 1) * P], ident)
                last.then_inc(turned, 1)

        @block.scalar
        def _(act):
            for c in range(chunks):
                act.wait_ge(turned, c + 1)
                nc.scalar.copy(dst[:, :, c * P:(c + 1) * P], banks[c % 4][:, 0:tiles * P].rearrange("p (t n) -> p t n", n=P))\
                    .then_inc(copied, 1)


def attention_memory(scratch, ring, spare):
    return (scratch[:, 3:5, :], scratch[:, 5:8, :],
            ring[:].rearrange("p s n -> p (s n)").rearrange("p (b k n) -> p b k n", b=2, k=4), spare[:, 0, 0:8])


def attention(nc, name, heads, scores, keys, scale, bias, values, depth, place, out, banks, sc, pr, pt, stats, ident,
              aside=None):
    jobs = [(h, q) for h in range(heads) for q in range(TT)]
    with stage(nc, f"{name}_scored {name}_masked {name}_max {name}_exp {name}_inv {name}_probs {name}_turned "
                   f"{name}_copied {name}_mixed {name}_stored {name}_aside") as (
            block, scored, masked, maxed, exped, inverted, normed, turned, copied, mixed, stored, aside_step):
        if aside:
            @block.gpsimd
            def _(pool):
                aside(pool, nc.gpsimd, aside_step)

        score_banks = [banks[0], banks[1], banks[6]]

        @block.tensor
        def _(pe):
            def turn(j):
                h, q = jobs[j]
                pe.wait_ge(normed, j + 1)
                if j >= 2:
                    pe.wait_ge(copied, j - 1)
                for k in range(keys(q)):
                    last = nc.tensor.transpose(banks[2 + j % 2][:, k * P:(k + 1) * P], pr[:, j % 3, k * P:(k + 1) * P], ident)
                last.then_inc(turned, 1)

            def mix(h):
                pe.wait_ge(copied, TT * (h + 1))
                if h >= 2:
                    pe.wait_ge(stored, h - 1)
                for k in range(keys(TT - 1)):
                    first_q = min(x for x in range(TT) if keys(x) > k) * P
                    last = nc.tensor.matmul(banks[4 + h % 2][place(h), first_q:T], values(h, k), pt[:, h % 2, k, first_q:T],
                                            start=(k == 0), stop=(k == keys(TT - 1) - 1))
                last.then_inc(mixed, 1)

            for j in range(len(jobs) + 3):
                if j < len(jobs):
                    h, q = jobs[j]
                    if j >= 3:
                        pe.wait_ge(masked, j - 2)
                    pairs = scores(h, q)
                    for n, (a, b) in enumerate(pairs):
                        last = nc.tensor.matmul(score_banks[j % 3][:, 0:keys(q) * P], a, b, start=(n == 0), stop=(n == len(pairs) - 1))
                    last.then_inc(scored, 1)
                if 0 <= j - 2 < len(jobs):
                    turn(j - 2)
                if j >= 3 and jobs[j - 3][1] == TT - 1:
                    mix(jobs[j - 3][0])

        @block.vector
        def _(dve):
            def normalize(j):
                h, q = jobs[j]
                w = keys(q) * P
                dve.wait_ge(exped, j + 1)
                nc.vector.reciprocal(stats[:, 4 + j % 2:5 + j % 2], stats[:, 2 + j % 2:3 + j % 2]).then_inc(inverted, 1)
                dve.wait_ge(inverted, j + 1)
                nc.vector.tensor_scalar(pr[:, j % 3, 0:w], pr[:, j % 3, 0:w], stats[:, 4 + j % 2:5 + j % 2], None,
                                        ALU.mult).then_inc(normed, 1)

            for j, (h, q) in enumerate(jobs):
                w = keys(q) * P
                dve.wait_ge(scored, j + 1)
                b = bias(h, q)
                if b is None:
                    nc.vector.tensor_scalar(sc[:, j % 2, 0:w], score_banks[j % 3][:, 0:w], scale, None, ALU.mult).then_inc(masked, 1)
                else:
                    nc.vector.scalar_tensor_tensor(sc[:, j % 2, 0:w], score_banks[j % 3][:, 0:w], scale, b, ALU.mult, ALU.add)\
                        .then_inc(masked, 1)
                dve.wait_ge(masked, j + 1)
                nc.vector.tensor_reduce(stats[:, j % 2:j % 2 + 1], sc[:, j % 2, 0:w], AX.X, ALU.max, negate=True)\
                    .then_inc(maxed, 1)
                if j:
                    normalize(j - 1)
            normalize(len(jobs) - 1)

        @block.scalar
        def _(act):
            def copy(j):
                h, q = jobs[j]
                act.wait_ge(turned, j + 1)
                if h >= 2 and q == 0:
                    act.wait_ge(mixed, h - 1)
                w = keys(q) * P
                nc.scalar.copy(pt[:, h % 2, 0:keys(q), q * P:(q + 1) * P],
                               banks[2 + j % 2][:, 0:w].rearrange("p (k n) -> p k n", n=P)).then_inc(copied, 1)

            def store(h):
                act.wait_ge(mixed, h + 1)
                nc.scalar.copy(out(h), banks[4 + h % 2][place(h), :]).then_inc(stored, 1)

            for j in range(len(jobs) + 4):
                if j < len(jobs):
                    h, q = jobs[j]
                    w = keys(q) * P
                    act.wait_ge(maxed, j + 1)
                    if j >= 3:
                        act.wait_ge(turned, j - 2)
                    nc.scalar.activation(pr[:, j % 3, 0:w], sc[:, j % 2, 0:w], ACT.Exp, bias=stats[:, j % 2:j % 2 + 1],
                                         accum_out=stats[:, 2 + j % 2:3 + j % 2]).then_inc(exped, 1)
                if 0 <= j - 2 < len(jobs):
                    copy(j - 2)
                if j >= 4 and jobs[j - 4][1] == TT - 1:
                    store(jobs[j - 4][0])


def sine(nc, link, angle, turns, turns_int, s, c):
    v = nc.vector
    link(v.tensor_scalar(turns, angle, 1.0 / TWO_PI, None, ALU.mult))
    link(v.tensor_copy(turns_int, turns))
    link(v.tensor_copy(turns, turns_int))
    link(v.scalar_tensor_tensor(s, turns, -PI_HIGH, angle, ALU.mult, ALU.add))
    link(v.scalar_tensor_tensor(s, turns, -PI_LOW, s, ALU.mult, ALU.add))
    link(v.tensor_scalar(s, s, 0.125, None, ALU.mult))
    return v.tensor_scalar(c, s, math.pi / 2, None, ALU.add)


def double_angle(nc, link, s, c, tmp, times=3):
    v = nc.vector
    for _ in range(times):
        link(v.tensor_tensor(tmp, s, c, ALU.mult))
        link(v.tensor_tensor(c, s, s, ALU.mult))
        link(v.tensor_scalar(c, c, -2.0, 1.0, ALU.mult, ALU.add))
        link(v.tensor_scalar(s, tmp, 2.0, None, ALU.mult))


def bc(ap, n):
    return ap.unsqueeze(2).to_broadcast([ap.shape[0], ap.shape[1], n])



HEADS1, HD1 = 8, 64
SSM_TILES = 16
MEM = 256
VEC1 = dict(mix_g=(0, 8), att_q_g=(8, 1), att_k_g=(9, 1), lam_re=(10, 16), lam_im=(26, 16), log_step=(42, 16),
            ssm_d=(58, 4), b_glu=(62, 4), mixed_g=(66, 8), mem_g=(74, 8), memkv_g=(82, 8), mem_q_g=(90, 2),
            mem_k_g=(92, 2), peer_g=(94, 8))
VEC1_N = 102


def first_block(nc, dram, psum, hT, scratch, ring, tools, spare, ident):
    banks = [psum[:, b, :] for b in range(8)]
    with ExitStack() as held:
        vec = held.enter_context(nc.sbuf_tensor("vec1", [P, VEC1_N], F32))

        def col(name, k=0):
            return vec[:, VEC1[name][0] + k:VEC1[name][0] + k + 1]

        def cols(name):
            return vec[:, VEC1[name][0]:VEC1[name][0] + VEC1[name][1]]

        with stage(nc, "inputs_loaded") as (block, loaded):
            @block.sync
            def _(sp):
                sp.dma_start(hT[:].rearrange("p c n -> p (c n)"), dram["xT"]).then_inc(loaded, 16)
                sp.dma_start(vec[:], dram["vec1"]).then_inc(loaded, 16)
                sp.wait_ge(loaded, 32)

        def norm_to(high, low, gain):
            return Norm(nc, chunks_of(hT), None, DC, DC, tools, D, lambda c: col(gain, c), chunks_of(scratch), banks,
                        pair=(chunks_of(high), chunks_of(low)))

        def act_to(dst, n=T):
            return [("act", True, lambda f, ps, s: nc.scalar.copy(dst[:, bass.ds(f, 1), 0:n].squeeze(1), ps))]

        def mix():
            with ExitStack() as phase:
                qkT = phase.enter_context(nc.sbuf_tensor("qkT", [P, 8, T], F32))
                uT = phase.enter_context(nc.sbuf_tensor("uT", [P, 4, T], F32))
                vS = phase.enter_context(nc.sbuf_tensor("vS", [P, TT, 512], F32))
                mixT = phase.enter_context(nc.sbuf_tensor("mixT", [P, 8, T], F32))
                with ExitStack() as projection:
                    xH = projection.enter_context(nc.sbuf_tensor("mix_x_high", [P, DC, T], F32R))
                    xL = projection.enter_context(nc.sbuf_tensor("mix_x_low", [P, DC, T], F32R))
                    vT = projection.enter_context(nc.sbuf_tensor("vT", [P, 4, T], F32))
                    x = (chunks_of(xH), chunks_of(xL))
                    linears(nc, "mix_in", [Linear("mix_qk", dram["w_in"], 0, 8, DC, x, act_to(qkT), fed=True),
                                           Linear("mix_v", dram["w_in"], 8, 4, DC, x, act_to(vT)),
                                           Linear("mix_u", dram["w_in"], 12, 4, DC, x, act_to(uT))],
                            ring, banks, pre=norm_to(xH, xL, "mix_g"))
                    turn(nc, "mix_v", chunks_of(vT), vS, 4, TT, banks, ident)
                rmsnorm(nc, "norm_qk", chunks_of(qkT), chunks_of(qkT), 8, 1, tools, HD1,
                        lambda c: col("att_q_g" if c < 4 else "att_k_g"), chunks_of(scratch), banks, parts=2)
                with ExitStack() as tables:
                    ssm = StateTables(nc, tables)
                    with ExitStack() as att:
                        bias = att.enter_context(nc.sbuf_tensor("bias", [P, HEADS1, 512], F32))
                        ssm.prepare(dram, col, cols, bias)

                        def half(h):
                            return slice(64 * (h % 2), 64 * (h % 2) + 64)
                        attention(nc, "band", HEADS1,
                                  lambda h, q: [(qkT[half(h), h // 2, q * P:(q + 1) * P], qkT[half(h), 4 + h // 2, 0:(q + 1) * P])],
                                  lambda q: q + 1, HD1 ** -0.5, lambda h, q: bias[:, h, 384 - 128 * q:512],
                                  lambda h, k: vS[:, k, h * HD1:(h + 1) * HD1], HD1, half,
                                  lambda h: mixT[half(h), h // 2, :], banks, *attention_memory(scratch, ring, spare), ident,
                                  aside=ssm.rotations)
                    state_space(nc, ssm, col, uT, banks, scratch, ring)
                gated_unit(nc, dram, cols, uT, mixT, ring, banks, scratch)
                with ExitStack() as out:
                    yH = out.enter_context(nc.sbuf_tensor("mixed_high", [P, DC, T], F32R))
                    yL = out.enter_context(nc.sbuf_tensor("mixed_low", [P, DC, T], F32R))
                    pair = (chunks_of(yH), chunks_of(yL))
                    linears(nc, "mix_out", [Linear("mix_w_out", dram["w_out"], 0, 8, DC, pair, add_steps(nc, hT), fed=True)], ring, banks,
                            pre=Norm(nc, chunks_of(mixT), None, 8, 4, tools, 512, lambda c: col("mixed_g", c), chunks_of(scratch),
                                     banks, pair=pair))


        def memory():
            with ExitStack() as phase:
                mqT = phase.enter_context(nc.sbuf_tensor("mqT", [P, 8, T], F32))
                mkT = phase.enter_context(nc.sbuf_tensor("mkT", [P, 8, MEM], F32))
                mv = phase.enter_context(nc.sbuf_tensor("mv", [P, 2, D], F32))
                moT = phase.enter_context(nc.sbuf_tensor("moT", [P, 8, T], F32))

                def short(c):
                    return scratch[:, c, 0:MEM]
                with ExitStack() as projection:
                    memT = projection.enter_context(nc.sbuf_tensor("memT", [P, 8, MEM], F32))
                    mvT = projection.enter_context(nc.sbuf_tensor("mvT", [P, 8, MEM], F32))
                    xH = projection.enter_context(nc.sbuf_tensor("mem_x_high", [P, DC, T], F32R))
                    xL = projection.enter_context(nc.sbuf_tensor("mem_x_low", [P, DC, T], F32R))
                    memH = projection.enter_context(nc.sbuf_tensor("mem_high", [P, DC, MEM], F32R))
                    memL = projection.enter_context(nc.sbuf_tensor("mem_low", [P, DC, MEM], F32R))
                    with stage(nc, "memory_loaded") as (block, loaded):
                        @block.sync
                        def _(sp):
                            sp.dma_start(memT[:].rearrange("p c n -> p (c n)"), dram["memT"]).then_inc(loaded, 16)
                            sp.wait_ge(loaded, 16)
                    m = (chunks_of(memH, n=MEM), chunks_of(memL, n=MEM))
                    alone(nc, "norm_memkv", Norm(nc, chunks_of(memT, n=MEM), None, 8, 8, tools, D, lambda c: col("memkv_g", c), short,
                                                 banks, pair=m))
                    linears(nc, "mem_in", [
                        Linear("mem_q", dram["w_mem_q"], 0, 8, DC, (chunks_of(xH), chunks_of(xL)), act_to(mqT), fed=True),
                        Linear("mem_k", dram["w_mem_k"], 0, 8, DC, m, act_to(mkT, MEM), n=MEM),
                        Linear("mem_v", dram["w_mem_v"], 0, 8, DC, m, act_to(mvT, MEM), n=MEM)],
                        ring, banks, pre=norm_to(xH, xL, "mem_g"))
                    turn(nc, "mem_v", chunks_of(mvT, n=MEM), mv, 8, 2, banks, ident)
                rmsnorm(nc, "norm_mq", chunks_of(mqT), chunks_of(mqT), 8, 2, tools, 256,
                        lambda c: col("mem_q_g", c % 2), chunks_of(scratch), banks)
                rmsnorm(nc, "norm_mk", chunks_of(mkT, n=MEM), chunks_of(mkT, n=MEM), 8, 2, tools, 256,
                        lambda c: col("mem_k_g", c % 2), short, banks)
                attention(nc, "memory", 8,
                          lambda h, q: [(mqT[:, 2 * (h // 2) + c, q * P:(q + 1) * P], mkT[:, 2 * (h // 2) + c, :]) for c in range(2)],
                          lambda q: 2, 256 ** -0.5, lambda h, q: None,
                          lambda h, k: mv[:, k, h * P:(h + 1) * P], P, lambda h: slice(0, P),
                          lambda h: moT[:, h, :], banks, *attention_memory(scratch, ring, spare), ident)
                with ExitStack() as out:
                    yH = out.enter_context(nc.sbuf_tensor("mem_y_high", [P, DC, T], F32R))
                    yL = out.enter_context(nc.sbuf_tensor("mem_y_low", [P, DC, T], F32R))
                    pair = (chunks_of(yH), chunks_of(yL))
                    linears(nc, "mem_out", [Linear("mem_o", dram["w_mem_o"], 0, 8, DC, pair, add_steps(nc, hT), fed=True)], ring, banks,
                            pre=Split(nc, chunks_of(moT), DC, pair))

        mix()
        memory()
        experts(nc, dram, hT, lambda high, low: norm_to(high, low, "peer_g"), scratch, ring, banks, ident)


class StateTables:

    def __init__(self, nc, held):
        def sb(name, shape, dt=F32):
            return held.enter_context(nc.sbuf_tensor(name, shape, dt))
        N = SSM_TILES
        self.nc = nc
        self.par = sb("ssm_par", [P, 13, N])
        self.mag = self.par[:, 2, :]
        self.turns_int = sb("turns_int", [P, N], I32)
        self.power = sb("power", [P, 9, 2, N])
        self.Er = sb("Er", [P, N, T])
        self.Ei = sb("Ei", [P, N, T])
        self.cre = sb("cre", [P, N, 32])
        self.cim = sb("cim", [P, N, 32])
        self.c1 = sb("c1", [P, N, 32])
        self.c2 = sb("c2", [P, N, 32])
        self.big = sb("rot_tmp", [P, 1024])
        self.bre = sb("bre", [P, 4, 128])
        self.bim = sb("bim", [P, 4, 128])

    def prepare(self, dram, col, cols, bias):
        nc, power, cre, cim, c1, c2 = self.nc, self.power, self.cre, self.cim, self.c1, self.c2
        step, lre, mag, sn, cs, tmp, turns, fr, fi, den, zr_, th, aim = (self.par[:, i, :] for i in range(13))
        with stage(nc, "c_loaded step_done angles_ready exps_done sines_done dve_step bias_loaded bias_masked") as (
                block, loaded, step_done, angles, exps, sines, dve_step, bias_loaded, masked):

            @block.sync
            def _(sp):
                sp.dma_start(cre[:].rearrange("p a b -> p (a b)"), dram["c_re"]).then_inc(loaded, 16)
                sp.dma_start(cim[:].rearrange("p a b -> p (a b)"), dram["c_im"]).then_inc(loaded, 16)
                sp.dma_start(self.bre[:].rearrange("p a b -> p (a b)"), dram["b_re"]).then_inc(loaded, 16)
                sp.dma_start(self.bim[:].rearrange("p a b -> p (a b)"), dram["b_im"]).then_inc(loaded, 16)
                sp.dma_start(bias[:].rearrange("p h n -> p (h n)"), dram["bias"]).then_inc(bias_loaded, 16)

            @block.gpsimd
            def _(pool):
                pool.wait_ge(bias_loaded, 16)
                nc.gpsimd.memset(bias[0:64, :, 448:512], NEG).then_inc(masked, 1)

            @block.scalar
            def _(act):
                nc.scalar.activation(step, cols("log_step"), ACT.Exp).then_inc(step_done, 1)
                act.wait_ge(angles, 1)
                nc.scalar.activation(mag, lre, ACT.Exp).then_inc(exps, 1)
                act.wait_ge(angles, 2)
                nc.scalar.activation(sn, sn, ACT.Sin).then_inc(sines, 1)
                nc.scalar.activation(cs, cs, ACT.Sin).then_inc(sines, 1)

            @block.vector
            def _(dve):
                v = nc.vector
                link = Chain(dve, dve_step)
                dve.wait_ge(step_done, 1)
                link(v.tensor_tensor(th, cols("lam_im"), step, ALU.mult))
                v.tensor_tensor(lre, cols("lam_re"), step, ALU.mult).then_inc(angles, 1)
                sine(nc, link, th, turns, self.turns_int[:], sn, cs).then_inc(angles, 1)
                dve.wait_ge(exps, 1)
                dve.wait_ge(sines, 2)
                double_angle(nc, link, sn, cs, tmp)
                link(v.tensor_tensor(zr_, mag, cs, ALU.mult))
                link(v.tensor_scalar(zr_, zr_, -1.0, None, ALU.add))
                link(v.tensor_tensor(aim, mag, sn, ALU.mult))
                link(v.tensor_tensor(den, cols("lam_re"), cols("lam_re"), ALU.mult))
                link(v.tensor_tensor(tmp, cols("lam_im"), cols("lam_im"), ALU.mult))
                link(v.tensor_tensor(den, den, tmp, ALU.add))
                link(v.reciprocal(den, den))
                link(v.tensor_tensor(fr, zr_, cols("lam_re"), ALU.mult))
                link(v.tensor_tensor(tmp, aim, cols("lam_im"), ALU.mult))
                link(v.tensor_tensor(fr, fr, tmp, ALU.add))
                link(v.tensor_tensor(fr, fr, den, ALU.mult))
                link(v.tensor_tensor(fi, aim, cols("lam_re"), ALU.mult))
                link(v.tensor_tensor(tmp, zr_, cols("lam_im"), ALU.mult))
                link(v.tensor_tensor(fi, fi, tmp, ALU.subtract))
                link(v.tensor_tensor(fi, fi, den, ALU.mult))
                dve.wait_ge(loaded, 64)
                link(v.tensor_tensor(c1[:], cre[:], bc(fr, 32), ALU.mult))
                link(v.tensor_tensor(c2[:], cim[:], bc(fi, 32), ALU.mult))
                link(v.tensor_tensor(c1[:], c1[:], c2[:], ALU.subtract))
                link(v.tensor_tensor(cre[:], cre[:], bc(fi, 32), ALU.mult))
                link(v.tensor_tensor(cim[:], cim[:], bc(fr, 32), ALU.mult))
                link(v.tensor_tensor(c2[:], cre[:], cim[:], ALU.add))
                link(v.tensor_scalar(c2[:], c2[:], -1.0, None, ALU.mult))
                link(v.tensor_scalar(cre[:], c1[:], -1.0, None, ALU.mult))
                link(v.tensor_copy(power[:, 0, 0, :], cs))
                link(v.tensor_copy(power[:, 0, 1, :], sn))
                for k in range(8):
                    c_, s_, c2_, s2_ = power[:, k, 0, :], power[:, k, 1, :], power[:, k + 1, 0, :], power[:, k + 1, 1, :]
                    link(v.tensor_tensor(tmp, s_, s_, ALU.mult))
                    link(v.tensor_tensor(c2_, c_, c_, ALU.mult))
                    link(v.tensor_tensor(c2_, c2_, tmp, ALU.subtract))
                    link(v.scalar_tensor_tensor(s2_, s_, 2.0, c_, ALU.mult, ALU.mult))

    def rotations(self, eng, ops, step):
        N, power, Er, Ei, big = SSM_TILES, self.power, self.Er, self.Ei, self.big
        link = Chain(eng, step)
        link(ops.memset(Er[:, :, 0:1], 1.0))
        link(ops.memset(Ei[:, :, 0:1], 0.0))
        for k in range(9):
            n = 1 << k
            m = min(N, 1024 // n)
            tmp = big[:, 0:m * n].rearrange("p (m n) -> p m n", n=n)
            for t0 in range(0, N, m):
                t = slice(t0, t0 + m)
                c_, s_ = bc(power[:, k, 0, t], n), bc(power[:, k, 1, t], n)
                link(ops.tensor_tensor(tmp, Ei[:, t, 0:n], s_, ALU.mult))
                link(ops.tensor_tensor(Er[:, t, n:2 * n], Er[:, t, 0:n], c_, ALU.mult))
                link(ops.tensor_tensor(Er[:, t, n:2 * n], Er[:, t, n:2 * n], tmp, ALU.subtract))
                link(ops.tensor_tensor(tmp, Er[:, t, 0:n], s_, ALU.mult))
                link(ops.tensor_tensor(Ei[:, t, n:2 * n], Ei[:, t, 0:n], c_, ALU.mult))
                link(ops.tensor_tensor(Ei[:, t, n:2 * n], Ei[:, t, n:2 * n], tmp, ALU.add))


def state_space(nc, tables, col, uT, banks, scratch, ring):
    N = SSM_TILES
    mag, Er, Ei, cre, c1, c2, bre, bim = (tables.mag, tables.Er, tables.Ei, tables.cre, tables.c1, tables.c2, tables.bre,
                                          tables.bim)
    sets = [scratch[:], ring[:].rearrange("p s (two n) -> p (s two) n", two=2)]
    with stage(nc, "b_ready turned_in scanned products y_ready y_summed y_activated dve_step pool_step") as (
            block, b_ready, rotated, scanned, products, y_ready, summed, activated, dve_step, pool_step):

        @block.tensor
        def _(pe):
            def project(i):
                g, k = divmod(i, 4)
                s = slice(32 * k, 32 * k + 32)
                if i >= 2:
                    pe.wait_ge(rotated, i - 1)
                nc.tensor.matmul(banks[2 * (i % 2)], bre[s, g, :], uT[s, g, :], start=True, stop=True)
                nc.tensor.matmul(banks[2 * (i % 2) + 1], bim[s, g, :], uT[s, g, :], start=True, stop=True).then_inc(b_ready, 1)
            project(0)
            project(1)
            for i in range(N):
                g, k = divmod(i, 4)
                if i + 2 < N:
                    project(i + 2)
                pe.wait_ge(products, i + 1)
                for n, c in enumerate((c1, cre, c2, c2)):
                    last = nc.tensor.matmul(banks[4 + g][32 * k:32 * k + 32, :], c[:, i, :], sets[i % 2][:, 4 + n, :],
                                            start=(n == 0), stop=(n == 3), skip_group_check=True)
                last.then_inc(y_ready, 1)

        @block.vector
        def _(dve):
            v = nc.vector
            link = Chain(dve, dve_step)
            for i in range(N):
                w, b0, b1 = sets[i % 2], banks[2 * (i % 2)], banks[2 * (i % 2) + 1]
                dve.wait_ge(b_ready, i + 1)
                link(v.tensor_tensor(w[:, 0, :], b0, Er[:, i, :], ALU.mult))
                link(v.tensor_tensor(w[:, 1, :], b1, Ei[:, i, :], ALU.mult))
                link(v.tensor_tensor(w[:, 0, :], w[:, 0, :], w[:, 1, :], ALU.add))
                link(v.tensor_tensor(w[:, 1, :], b1, Er[:, i, :], ALU.mult))
                if i >= 2:
                    dve.wait_ge(products, i - 1)
                v.tensor_tensor(w[:, 2, :], b0, Ei[:, i, :], ALU.mult).then_inc(rotated, 1)
                dve.wait_ge(rotated, i + 1)
                link(v.tensor_tensor(w[:, 1, :], w[:, 1, :], w[:, 2, :], ALU.subtract))
                m = mag[:, i:i + 1].to_broadcast([P, T])
                link(v.tensor_tensor_scan(w[:, 2, :], m, w[:, 0, :], 0.0, ALU.mult, ALU.add))
                v.tensor_tensor_scan(w[:, 3, :], m, w[:, 1, :], 0.0, ALU.mult, ALU.add).then_inc(scanned, 1)
            for g in range(4):
                dve.wait_ge(y_ready, 4 * g + 4)
                v.scalar_tensor_tensor(uT[:, g, :], uT[:, g, :], col("ssm_d", g), banks[4 + g], ALU.mult, ALU.add)\
                    .then_inc(summed, 1)

        @block.gpsimd
        def _(pool):
            for i in range(N):
                pool.wait_ge(scanned, i + 1)
                if i >= 2:
                    pool.wait_ge(y_ready, i - 1)
                w = sets[i % 2]
                nc.gpsimd.tensor_tensor(w[:, 4, :], w[:, 2, :], Er[:, i, :], ALU.mult)
                nc.gpsimd.tensor_tensor(w[:, 5, :], w[:, 3, :], Ei[:, i, :], ALU.mult)
                nc.gpsimd.tensor_tensor(w[:, 6, :], w[:, 3, :], Er[:, i, :], ALU.mult)
                nc.gpsimd.tensor_tensor(w[:, 7, :], w[:, 2, :], Ei[:, i, :], ALU.mult).then_inc(products, 1)

        @block.scalar
        def _(act):
            for g in range(4):
                act.wait_ge(summed, g + 1)
                nc.scalar.activation(uT[:, g, :], uT[:, g, :], ACT.Gelu).then_inc(activated, 1)


def gated_unit(nc, dram, cols, uT, mixT, ring, banks, scratch):
    bglu = cols("b_glu")
    with stage(nc, "glu_loaded glu_done gate_ready gated") as (block, loaded, done, gate, gated):
        glu = ring[:, :, :].rearrange("p s n -> p (s n)")

        @block.sync
        def _(sp):
            for f in range(4):
                sp.dma_start(glu[:, f * 512:(f + 1) * 512], row(dram["w_glu"], f)).then_inc(loaded, 16)

        @block.tensor
        def _(pe):
            pe.wait_ge(loaded, 64)
            for f in range(4):
                for c in range(4):
                    last = nc.tensor.matmul(banks[f], glu[:, f * 512 + c * P:f * 512 + (c + 1) * P], uT[:, c, :],
                                            start=(c == 0), stop=(c == 3))
                last.then_inc(done, 1)

        @block.scalar
        def _(act):
            for f in range(4):
                act.wait_ge(done, f + 1)
                nc.scalar.activation(scratch[:, f, :], banks[f], ACT.Sigmoid, bias=bglu[:, f:f + 1]).then_inc(gate, 1)

        @block.vector
        def _(dve):
            for f in range(4):
                dve.wait_ge(gate, f + 1)
                nc.vector.tensor_tensor(mixT[:, 4 + f, :], uT[:, f, :], scratch[:, f, :], ALU.mult).then_inc(gated, 1)



PH, PK, TOP = 8, 128, 16
GROUP = 4
LOWEST = -3e38


def experts(nc, dram, hT, norm_to, scratch, ring, banks, ident):
    with ExitStack() as held:
        first = held.enter_context(nc.sbuf_tensor("firstT", [P, T], F32))
        second = held.enter_context(nc.sbuf_tensor("secondT", [P, T], F32))
        gateT = held.enter_context(nc.sbuf_tensor("gateT", [P, T], F32))
        iota = held.enter_context(nc.sbuf_tensor("iota", [P, PK], F32))
        with stage(nc, "iota_ready") as (block, ready):
            @block.gpsimd
            def _(pool):
                nc.gpsimd.iota(iota[:], pattern=[[1, PK]], base=0, channel_multiplier=0,
                               allow_small_or_imprecise_dtypes=True).then_inc(ready, 1)
        choose_experts(nc, dram, norm_to, ring, banks, ident, first, second, gateT, iota)
        build_gates(nc, dram, scratch, ring, banks, first, second, gateT, iota)
    stream_experts(nc, dram, hT, norm_to, scratch, ring, banks)


def choose_experts(nc, dram, norm_to, ring, banks, ident, first, second, gateT, iota):
    with ExitStack() as held:
        def sb(name, shape, dt=F32):
            return held.enter_context(nc.sbuf_tensor(name, shape, dt))
        qT = sb("peer_qT", [P, 2 * PH, T])
        keys = sb("peer_keys_sb", [P, 2 * PH, PK])
        qs = sb("q_tile", [P, 2 * PH, P])
        s0 = sb("key_scores", [P, 2 * PH, PK])
        s1 = sb("pair_scores", [P, 2 * PH, PK])
        s2 = sb("key_scores_rest", [P, 2 * PH, PK])
        sv = sb("key_top", [P, 2 * PH, TOP])
        si = sb("key_index", [P, 2 * PH, TOP], U32)
        sif = sb("key_index_f", [P, 2 * PH, TOP])
        top = sb("pair_top", [P, PH, TOP])
        pos = sb("pair_index", [P, PH, TOP], U32)
        ab = sb("pair_ab", [P, 2, PH * TOP], U32)
        abf = sb("pair_ab_f", [P, 2, PH * TOP])
        tab = sb("to_turn", [P, 3, PH * TOP])
        sums = sb("gate_sums", [P, PH])
        with ExitStack() as projection:
            xH = projection.enter_context(nc.sbuf_tensor("peer_x_high", [P, DC, T], F32R))
            xL = projection.enter_context(nc.sbuf_tensor("peer_x_low", [P, DC, T], F32R))
            linears(nc, "peer_in", [Linear("peer_q", dram["w_peer_q"], 0, 2 * PH, DC, (chunks_of(xH), chunks_of(xL)),
                                           [("act", True, lambda f, ps, s: nc.scalar.copy(part(qT, f), ps))], fed=True)],
                    ring, banks, pre=norm_to(xH, xL), spill=(keys[:].rearrange("p h n -> p (h n)"), dram["peer_keys"]))

        def score_act(act, t, copied, scored, kept, used=None):
            nc.scalar.copy(qs[:], qT[:, :, bass.ds(t * P, P)]).then_inc(copied, 1)
            if used:
                act.wait_ge(used, 1)
            for b in range(4):
                act.wait_ge(scored, b + 1)
                nc.scalar.copy(s0[:, 4 * b:4 * b + 4, :], banks[3 + b].rearrange("p (h n) -> p h n", n=PK)).then_inc(kept, 1)

        def score_pe(pe, copied, scored):
            pe.wait_ge(copied, 1)
            for b in range(4):
                for k in range(4):
                    last = nc.tensor.matmul(banks[3 + b][:, k * PK:(k + 1) * PK], qs[:, 4 * b + k, :], keys[:, 4 * b + k, :],
                                            start=True, stop=True)
                last.then_inc(scored, 1)

        with stage(nc, "q_copied keys_scored scores_stored") as (block, copied, scored, kept):
            block.scalar(lambda act: score_act(act, 0, copied, scored, kept))
            block.tensor(lambda pe: score_pe(pe, copied, scored))

        def choose(t, last_tile):
            with stage(nc, "dve_step logits_ready exps_done gates_ready turned scores_read q_copied keys_scored scores_stored") as (
                    block, dve_step, logits, exps, gates, turned, scores_read, copied, scored, kept):
                @block.vector
                def _(dve):
                    v = nc.vector
                    link = Chain(dve, dve_step)

                    def top16(n, values, rest, best, index, read=None):
                        for k in range(n):
                            last = v.max(best[:, k, 0:8], values[:, k, :])
                        link(last)
                        for k in range(n):
                            v.max_index(index[:, k, 0:8], best[:, k, 0:8], values[:, k, :])
                            last = v.match_replace(rest[:, k, :], best[:, k, 0:8], values[:, k, :], LOWEST)
                        if read:
                            last.then_inc(read, 1)
                            dve.wait_ge(read, 1)
                        else:
                            link(last)
                        for k in range(n):
                            last = v.max(best[:, k, 8:16], rest[:, k, :])
                        link(last)
                        for k in range(n):
                            last = v.max_index(index[:, k, 8:16], best[:, k, 8:16], rest[:, k, :])
                        link(last)

                    top16(2 * PH, s0, s2, sv, si, scores_read)
                    link(v.tensor_copy(sif[:], si[:]))
                    cand = s1[:].rearrange("p (h two) n -> p h (two n)", two=2)
                    rest = s2[:].rearrange("p (h two) n -> p h (two n)", two=2)
                    by_side = sv[:].rearrange("p (h two) a -> p h two a", two=2)
                    for h in range(PH):
                        last = v.tensor_tensor(cand[:, h, :].rearrange("p (a b) -> p a b", b=TOP),
                                               bc(by_side[:, h, 0, :], TOP),
                                               by_side[:, h, 1:2, :].to_broadcast([P, TOP, TOP]), ALU.add)
                    link(last)
                    top16(PH, cand, rest, top, pos)
                    flat = pos[:].rearrange("p h k -> p (h k)")
                    link(v.tensor_scalar(ab[:, 0, :], flat, 4, None, ALU.logical_shift_right))
                    link(v.tensor_scalar(ab[:, 1, :], flat, 15, None, ALU.bitwise_and))
                    link(v.tensor_copy(abf[:], ab[:]))
                    tops = top[:]
                    gate = tab[:, 2, :].rearrange("p (h k) -> p h k", k=TOP)
                    v.tensor_tensor(gate, tops, top[:, :, 0:1].to_broadcast([P, PH, TOP]), ALU.subtract).then_inc(logits, 1)
                    for side in range(2):
                        eq = s1[:].rearrange("p h n -> p (h n)").rearrange("p (x a) -> p x a", a=TOP)
                        link(v.tensor_tensor(eq, bc(abf[:, side, :], TOP),
                                             iota[:, 0:TOP].unsqueeze(1).to_broadcast([P, PH * TOP, TOP]), ALU.is_equal))
                        for h in range(PH):
                            e = eq[:, h * TOP:(h + 1) * TOP, :]
                            last = v.tensor_tensor(e, e, sif[:, 2 * h + side, :].unsqueeze(1).to_broadcast([P, TOP, TOP]), ALU.mult)
                        link(last)
                        link(v.tensor_reduce(tab[:, side, :], eq, AX.X, ALU.add))
                    dve.wait_ge(exps, 1)
                    link(v.tensor_reduce(sums[:], gate, AX.X, ALU.add))
                    link(v.reciprocal(sums[:], sums[:]))
                    v.tensor_tensor(gate, gate, bc(sums[:], TOP), ALU.mult).then_inc(gates, 1)

                @block.scalar
                def _(act):
                    if not last_tile:
                        score_act(act, t + 1, copied, scored, kept, scores_read)
                    act.wait_ge(logits, 1)
                    nc.scalar.activation(tab[:, 2, :], tab[:, 2, :], ACT.Exp).then_inc(exps, 1)
                    for n, dst in enumerate((first, second, gateT)):
                        act.wait_ge(turned, n + 1)
                        last = nc.scalar.copy(dst[:, bass.ds(t * P, P)], banks[n][:, 0:P])
                    last.then_inc(exps, 1)

                @block.tensor
                def _(pe):
                    if not last_tile:
                        score_pe(pe, copied, scored)
                    pe.wait_ge(gates, 1)
                    for n in range(3):
                        nc.tensor.transpose(banks[n][:, 0:P], tab[:, n, :], ident).then_inc(turned, 1)

        with nc.Fori(0, TT - 1) as t:
            choose(t, False)
        choose(TT - 1, True)


ONEHOT = 8
BUFFERS = 4


def build_gates(nc, dram, scratch, ring, banks, first, second, gateT, iota):
    a_ = scratch[:].rearrange("p c n -> p (c n)").rearrange("p (b t i) -> p b t i", b=BUFFERS, i=PK)
    b_ = ring[:].rearrange("p c n -> p (c n)").rearrange("p (b t i) -> p b t i", b=BUFFERS, i=PK)
    iota_b = iota[:].unsqueeze(1).to_broadcast([P, ONEHOT, PK])
    per_block = P // ONEHOT
    with ExitStack() as held:
        G = held.enter_context(nc.sbuf_tensor("gate_block", [P, 2, PK, P], F32))
        with stage(nc, "first_onehot second_onehot gated block_used tokens_done copied stored_0 stored_1") as (
                block, first_hot, second_hot, gated, used, tokens_done, copied, stored_0, stored_1):
            stored = [stored_0, stored_1]

            @block.vector
            def _(dve):
                for tb in range(TT):
                    def pair(i, tb=tb):
                        for u in range(BUFFERS):
                            n = tb * per_block + BUFFERS * i + u
                            at = bass.ds(n * ONEHOT, ONEHOT)
                            if tb or not isinstance(i, int):
                                dve.wait_ge(used, n - BUFFERS + 1)
                            nc.vector.tensor_tensor(a_[:, u], bc(first[:, at], PK), iota_b, ALU.is_equal).then_inc(first_hot, 1)
                            nc.vector.tensor_tensor(b_[:, u], bc(second[:, at], PK), iota_b, ALU.is_equal).then_inc(second_hot, 1)
                    pair(0)
                    with dve.Fori(1, per_block // BUFFERS) as i:
                        pair(i)

            @block.gpsimd
            def _(pool):
                for tb in range(TT):
                    with pool.Fori(0, per_block // BUFFERS) as i:
                        for u in range(BUFFERS):
                            n = tb * per_block + BUFFERS * i + u
                            pool.wait_ge(first_hot, n + 1)
                            nc.gpsimd.tensor_tensor(a_[:, u], a_[:, u], bc(gateT[:, bass.ds(n * ONEHOT, ONEHOT)], PK),
                                                    ALU.mult).then_inc(gated, 1)

            @block.tensor
            def _(pe):
                for tb in range(TT):
                    def pair(i, tb=tb):
                        for u in range(BUFFERS):
                            n = tb * per_block + BUFFERS * i + u
                            pe.wait_ge(second_hot, n + 1)
                            pe.wait_ge(gated, n + 1)
                            for k in range(ONEHOT):
                                bank = u * 2 + k // 4
                                if k % 4 == 0 and (tb or not isinstance(i, int)):
                                    pe.wait_ge(copied, 2 * n + k // 4 - 7)
                                last = nc.tensor.matmul(banks[bank][:, (k % 4) * P:(k % 4 + 1) * P], b_[:, u, k, :], a_[:, u, k, :],
                                                        start=True, stop=True)
                                if k % 4 == 3 and k < ONEHOT - 1:
                                    last.then_inc(tokens_done, 1)
                            last.then_inc(used, 1)
                    pair(0)
                    with pe.Fori(1, per_block // BUFFERS) as i:
                        pair(i)

            @block.scalar
            def _(act):
                for tb in range(TT):
                    if tb >= 2:
                        act.wait_ge(stored[tb % 2], 64)
                    with act.Fori(0, per_block // BUFFERS) as i:
                        for u in range(BUFFERS):
                            n = tb * per_block + BUFFERS * i + u
                            for q in range(2):
                                if q == 0:
                                    act.wait_ge(tokens_done, n + 1)
                                else:
                                    act.wait_ge(used, n + 1)
                                nc.scalar.copy(G[:, tb % 2, :, bass.ds((BUFFERS * i + u) * ONEHOT + 4 * q, 4)],
                                               banks[u * 2 + q].rearrange("p (t i) -> p i t", i=PK)).then_inc(copied, 1)

            @block.sync
            def _(sp):
                for tb in range(TT):
                    sp.wait_ge(copied, 2 * per_block * (tb + 1))
                    for part in range(4):
                        r = slice(32 * part, 32 * part + 32)
                        sp.dma_start(dram["gates"][r, :, tb * P:(tb + 1) * P].rearrange("i j t -> j i t"),
                                     G[:, tb % 2, r, :]).then_inc(stored[tb % 2], 16)
                sp.wait_ge(stored_0, 128)
                sp.wait_ge(stored_1, 128)


def stream_experts(nc, dram, hT, norm_to, scratch, ring, banks):
    groups = PK // GROUP
    with ExitStack() as held:
        def sb(name, shape, dt=F32):
            return held.enter_context(nc.sbuf_tensor(name, shape, dt))
        xH = sb("xn_high", [P, DC, T], F32R)
        xL = sb("xn_low", [P, DC, T], F32R)
        uH = sb("in_high", [P, 2, D], F32R)
        uL = sb("in_low", [P, 2, D], F32R)
        vH = sb("out_high", [P, GROUP, D], F32R)
        vL = sb("out_low", [P, GROUP, D], F32R)
        aH = sb("act_high", [P, 2 * GROUP, T], F32R)
        aL = sb("act_low", [P, 2 * GROUP, T], F32R)
        G = sb("gates_in", [P, GROUP, T])
        A = sb("activations", [P, GROUP, T])
        alone(nc, "norm_stream", norm_to(xH, xL))
        U = ring
        V = scratch[:].rearrange("p (s two) n -> p s (two n)", two=2)
        names = [f"{k}{u}_loaded" for k in ("in", "out", "gate") for u in range(GROUP)]
        with stage(nc, "in_high_ready in_low_ready out_high_ready out_low_ready dots_done activated gated "
                       "act_high_ready act_low_ready summed added " + " ".join(names)) as (
                block, in_high, in_low, out_high, out_low, dots, activated, gated, act_high, act_low, summed, added, *loads):
            u_in, v_in, g_in = loads[0:4], loads[4:8], loads[8:12]

            def pairs(eng, body):
                body(0, 0)
                body(1, 1)
                with eng.Fori(1, groups // 2) as k:
                    body(2 * k, 0)
                    body(2 * k + 1, 1)

            def is_first(g):
                return isinstance(g, int) and g == 0

            @block.sync
            def _(sp):
                def load_out(g):
                    for u in range(GROUP):
                        if not is_first(g):
                            sp.wait_ge(out_low, GROUP * (g - 1) + u + 1)
                        sp.dma_start(V[:, u, :], row(dram["peer_v"], g * GROUP + u)).then_inc(v_in[u], 16)

                def body(g, half):
                    for u in range(GROUP):
                        if not is_first(g):
                            sp.wait_ge(in_low, GROUP * (g - 1) + u + 1)
                        sp.dma_start(U[:, u, :], row(dram["peer_u"], g * GROUP + u)).then_inc(u_in[u], 16)
                        if not is_first(g):
                            sp.wait_ge(gated, GROUP * (g - 1) + u + 1)
                        sp.dma_start(G[:, u, :], row(dram["gates"], g * GROUP + u)).then_inc(g_in[u], 16)
                    if is_first(g):
                        return
                    load_out(g - 1)
                pairs(sp, body)
                load_out(groups - 1)

            @block.scalar
            def _(act):
                def split_in(n, g, u, first):
                    act.wait_ge(u_in[u], 16 * (g + 1))
                    if not first:
                        act.wait_ge(dots, n - 1)
                    nc.scalar.copy(uH[:, u % 2, :], U[:, u, :]).then_inc(in_high, 1)

                def split_out(g, u):
                    act.wait_ge(v_in[u], 16 * (g + 1))
                    if not is_first(g):
                        act.wait_ge(summed, DC * g)
                    nc.scalar.copy(vH[:, u, :], V[:, u, :]).then_inc(out_high, 1)

                def body(g, half, last=False):
                    for u in range(GROUP):
                        n = g * GROUP + u
                        if not is_first(g):
                            split_out(g - 1, u)
                        act.wait_ge(dots, n + 1)
                        if not is_first(g):
                            act.wait_ge(act_low, n - GROUP + 1)
                        nc.scalar.activation(A[:, u, :], banks[u % 2], ACT.Gelu).then_inc(activated, 1)
                        if not (last and u >= 2):
                            split_in(n + 2, g + (u + 2) // GROUP, (u + 2) % GROUP, False)
                split_in(0, 0, 0, True)
                split_in(1, 0, 1, True)
                body(0, 0)
                body(1, 1)
                with act.Fori(1, groups // 2 - 1) as k:
                    body(2 * k, 0)
                    body(2 * k + 1, 1)
                body(groups - 2, 0)
                body(groups - 1, 1, last=True)
                for u in range(GROUP):
                    split_out(groups - 1, u)

            @block.gpsimd
            def _(pool):
                def split_in(n, u):
                    pool.wait_ge(in_high, n + 1)
                    nc.gpsimd.tensor_tensor(uL[:, u % 2, :], U[:, u, :], uH[:, u % 2, :].bitcast(F32), ALU.subtract)\
                        .then_inc(in_low, 1)

                def split_out(g, u):
                    pool.wait_ge(out_high, g * GROUP + u + 1)
                    nc.gpsimd.tensor_tensor(vL[:, u, :], V[:, u, :], vH[:, u, :].bitcast(F32), ALU.subtract)\
                        .then_inc(out_low, 1)

                def body(g, half, last=False):
                    for u in range(GROUP):
                        if not is_first(g):
                            split_out(g - 1, u)
                        if not (last and u >= 2):
                            split_in(g * GROUP + u + 2, (u + 2) % GROUP)
                split_in(0, 0)
                split_in(1, 1)
                body(0, 0)
                body(1, 1)
                with pool.Fori(1, groups // 2 - 1) as k:
                    body(2 * k, 0)
                    body(2 * k + 1, 1)
                body(groups - 2, 0)
                body(groups - 1, 1, last=True)
                for u in range(GROUP):
                    split_out(groups - 1, u)

            @block.tensor
            def _(pe):
                def dot(g, half):
                    for u in range(GROUP):
                        n = g * GROUP + u
                        pe.wait_ge(in_low, n + 1)
                        if u >= 2 or not is_first(g):
                            pe.wait_ge(activated, n - 1)
                        for c in range(DC):
                            w = slice(c * P, (c + 1) * P)
                            last = product(nc, banks[u % 2], uH[:, u % 2, w], uL[:, u % 2, w], xH[:, c, :], xL[:, c, :],
                                           c == 0, c == DC - 1)
                        last.then_inc(dots, 1)

                def combine(g, half):
                    for d in range(DC):
                        if d == 0:
                            pe.wait_ge(act_low, GROUP * (g + 1))
                            pe.wait_ge(out_low, GROUP * (g + 1))
                        if d >= 4 or not is_first(g):
                            pe.wait_ge(added, g * DC + d - 3)
                        for u in range(GROUP):
                            w = slice(d * P, (d + 1) * P)
                            s = half * GROUP + u
                            last = product(nc, banks[2 + d % 4], vH[:, u, w], vL[:, u, w], aH[:, s, :], aL[:, s, :],
                                           u == 0, u == GROUP - 1)
                        last.then_inc(summed, 1)

                dot(0, 0)
                dot(1, 1)
                combine(0, 0)
                with pe.Fori(1, groups // 2) as k:
                    dot(2 * k, 0)
                    combine(2 * k - 1, 1)
                    dot(2 * k + 1, 1)
                    combine(2 * k, 0)
                combine(groups - 1, 1)

            @block.vector
            def _(dve):
                def weigh(g, half):
                    for u in range(GROUP):
                        n = g * GROUP + u
                        s = half * GROUP + u
                        dve.wait_ge(activated, n + 1)
                        dve.wait_ge(g_in[u], 16 * (g + 1))
                        nc.vector.tensor_tensor(A[:, u, :], A[:, u, :], G[:, u, :], ALU.mult).then_inc(gated, 1)
                        if not isinstance(g, int):
                            dve.wait_ge(summed, DC * (g - 1))
                        dve.wait_ge(gated, n + 1)
                        nc.vector.tensor_copy(aH[:, s, :], A[:, u, :]).then_inc(act_high, 1)
                        dve.wait_ge(act_high, n + 1)
                        nc.vector.tensor_tensor(aL[:, s, :], A[:, u, :], aH[:, s, :].bitcast(F32), ALU.subtract).then_inc(act_low, 1)

                def add(g, half):
                    for d in range(DC):
                        dve.wait_ge(summed, g * DC + d + 1)
                        if not is_first(g):
                            dve.wait_ge(added, g * DC + d + 1 - DC)
                        nc.vector.tensor_tensor(hT[:, d, :], hT[:, d, :], banks[2 + d % 4], ALU.add).then_inc(added, 1)

                weigh(0, 0)
                weigh(1, 1)
                add(0, 0)
                with dve.Fori(1, groups // 2) as k:
                    weigh(2 * k, 0)
                    add(2 * k - 1, 1)
                    weigh(2 * k + 1, 1)
                    add(2 * k, 0)
                add(groups - 1, 1)



CONST = dict(neg128=(0, 128), neg64=(128, 128), strict64=(256, 128), level=(384, 768), causal=(1152, 512), inv_freq=(1664, 1))
CONST_N = 1665
VEC2 = dict(norm1=(0, 8), conv_ssd=(8, 48), conv_ssd_b=(56, 12), small_b=(68, 1), a_log=(69, 1), ssd_d=(70, 8),
            ssd_g=(78, 8), mla_q_g=(86, 4), mla_kv_g=(90, 2), conv_gdn=(92, 64), gdn_g=(156, 1), norm2=(157, 8))
VEC2_N = 165
DT_ROWS, BETA_ROWS, A_ROWS = 0, 32, 64
SSD_HEADS, GDN_HEADS = 16, 8
GDN_SCALE = 128 ** -0.5


def rope_tables(nc, dram, const, cosT, sinT, scratch):
    turns_int = scratch[:, 3, :].bitcast(I32)
    pos = scratch[:, 0, :].bitcast(I32)
    ang, turns, tmp = scratch[:, 1, :], scratch[:, 2, :], scratch[:, 4, :]
    with stage(nc, "positions_loaded reduced sines_done dve_step") as (block, loaded, reduced, sines, dve_step):
        @block.sync
        def _(sp):
            sp.dma_start(const[:], dram["consts"]).then_inc(loaded, 16)
            sp.dma_start(pos, dram["positions"]).then_inc(loaded, 16)

        @block.vector
        def _(dve):
            link = Chain(dve, dve_step)
            dve.wait_ge(loaded, 32)
            link(nc.vector.tensor_copy(ang, pos))
            link(nc.vector.tensor_scalar(ang, ang, const[:, CONST["inv_freq"][0]:CONST["inv_freq"][0] + 1], None, ALU.mult))
            sine(nc, link, ang, turns, turns_int, sinT, cosT).then_inc(reduced, 1)
            dve.wait_ge(sines, 2)
            double_angle(nc, link, sinT, cosT, tmp)

        @block.scalar
        def _(act):
            act.wait_ge(reduced, 1)
            nc.scalar.activation(sinT, sinT, ACT.Sin).then_inc(sines, 1)
            nc.scalar.activation(cosT, cosT, ACT.Sin).then_inc(sines, 1)


def conv_steps(nc, xp, weight, bias, acc):
    def tile(f, k=0):
        return xp[:, bass.ds(f, 1), k:k + T].squeeze(1)

    def first_tap(f, ps, s):
        if bias is None:
            return nc.vector.tensor_scalar(acc[s], tile(f, 3), weight(f, 3), None, ALU.mult)
        return nc.vector.tensor_scalar(acc[s], tile(f, 3), weight(f, 3), bias(f), ALU.mult, ALU.add)

    def tap(k):
        return lambda f, ps, s: nc.vector.scalar_tensor_tensor(acc[s], tile(f, k), weight(f, k), acc[s], ALU.mult, ALU.add)
    return [("act", True, lambda f, ps, s: nc.scalar.copy(tile(f, 3), ps)), ("dve", False, first_tap),
            ("dve", False, tap(2)), ("dve", False, tap(1)), ("dve", False, tap(0)),
            ("act", False, lambda f, ps, s: nc.scalar.activation(tile(f), acc[s], ACT.Silu))]


def second_block(nc, dram, psum, hT, scratch, ring, tools, spare, ones, ident):
    banks = [psum[:, b, :] for b in range(8)]
    with ExitStack() as held:
        def sb(name, shape, dt=F32):
            return held.enter_context(nc.sbuf_tensor(name, shape, dt))
        const = sb("consts_sb", [P, CONST_N])
        cosT = sb("cosT", [P, T])
        sinT = sb("sinT", [P, T])
        vec = sb("vec2", [P, VEC2_N])
        small = sb("small", [P, T])
        cum = sb("cum", [P, T])
        smallN = sb("smallN", [P, TT, P])
        cumN = sb("cumN", [P, TT, P])
        xH = sb("x_high", [P, DC, T], F32R)
        xL = sb("x_low", [P, DC, T], F32R)
        xn = (chunks_of(xH), chunks_of(xL))
        acc = [scratch[:, s, :] for s in range(SLOTS)]
        rope_tables(nc, dram, const, cosT[:], sinT[:], scratch)

        def col(name, k=0):
            return vec[:, bass.ds(VEC2[name][0] + k, 1)]

        def cst(name, k=0, n=None):
            a, w = CONST[name]
            return const[:, a + k:a + (k + n if n else w)]

        def act_to(dst, func=None):
            if func is None:
                return ("act", True, lambda f, ps, s: nc.scalar.copy(part(dst, f), ps))
            return ("act", True, lambda f, ps, s: nc.scalar.activation(part(dst, f), ps, func))

        def times(dst, src):
            return ("dve", False, lambda f, ps, s: nc.vector.tensor_tensor(part(dst, f), part(dst, f), part(src, f), ALU.mult))

        def parts_of(src, high, low):
            return [("act", False, lambda f, ps, s: nc.scalar.copy(part(high, f), part(src, f))),
                    ("dve", False, lambda f, ps, s: nc.vector.tensor_tensor(part(low, f), part(src, f), part(high, f).bitcast(F32),
                                                                            ALU.subtract))]

        def norm_to(high, low, x, gain, group=DC, width=D):
            return Norm(nc, x, None, DC, group, tools, width, lambda c: col(gain, c), chunks_of(scratch), banks,
                        pair=(chunks_of(high), chunks_of(low)))

        def gate_and_out(name, n, y, mixT, last=False):
            gate = Linear(f"{name}_gate", dram["w_gate"], layer * 24 + 8 * n, 8, DC, xn, [act_to(scratch, ACT.Sigmoid)])
            if n == 2:
                steps = [("dve", True, lambda f, ps, s: nc.vector.tensor_tensor(part(mixT, f), part(scratch, f), ps, ALU.mult))]
            else:
                steps = [("dve", True, lambda f, ps, s: nc.vector.tensor_tensor(part(scratch, f), part(scratch, f), ps, ALU.mult)),
                         ("dve", False, lambda f, ps, s: nc.vector.tensor_tensor(part(mixT, f), part(mixT, f), part(scratch, f),
                                                                                 ALU.add))]
            return [gate, Linear(f"{name}_out", dram[f"w_{name}_out"], layer * 8, 8, DC, y, steps, behind="gdn_z" if n == 2 else None, fed=(n != 2))]

        with nc.Fori(0, LAYERS) as layer:
            with stage(nc, "vec_loaded") as (block, loaded):
                @block.sync
                def _(sp):
                    sp.dma_start(vec[:], row(dram["vec2"], layer)).then_inc(loaded, 16)
                    sp.wait_ge(loaded, 16)
            yT = hT
            delta_rule(nc, dram, psum, layer, yT, small, cum, smallN, cumN, col, cst, ones, ring, banks, ident, scratch, tools, spare,
                       xn, norm_to(xH, xL, chunks_of(hT), "norm1"), acc, hT)
            with ExitStack() as mix:
                mixT = mix.enter_context(nc.sbuf_tensor("mixed", [P, 8, T], F32))
                with ExitStack() as mla:
                    c8 = mla.enter_context(nc.sbuf_tensor("mla_c", [P, 8, T], F32))
                    with ExitStack() as tail:
                        yH = tail.enter_context(nc.sbuf_tensor("gdn_y_high", [P, 8, T], F32R))
                        yL = tail.enter_context(nc.sbuf_tensor("gdn_y_low", [P, 8, T], F32R))
                        linears(nc, "gdn_tail", [
                            Linear("gdn_z", dram["w_gdn_z"], layer * 8, 8, DC, xn,
                                   [act_to(scratch, ACT.Silu), times(yT, scratch)] + parts_of(yT, yH, yL)),
                            *gate_and_out("gdn", 2, (chunks_of(yH), chunks_of(yL)), mixT),
                            Linear("mla_in", dram["w_mla_in"], layer * 8, 8, DC, xn, [act_to(c8)])], ring, banks)
                    latent_attention(nc, dram, layer, c8, yT, col, cst, ones, ring, banks, ident, scratch, tools, spare, cosT, sinT)
                with ExitStack() as tail:
                    yH = tail.enter_context(nc.sbuf_tensor("mla_y_high", [P, 8, T], F32R))
                    yL = tail.enter_context(nc.sbuf_tensor("mla_y_low", [P, 8, T], F32R))
                    pair = (chunks_of(yH), chunks_of(yL))
                    linears(nc, "mla_tail", gate_and_out("mla", 1, pair, mixT), ring, banks, pre=Split(nc, chunks_of(yT), DC, pair))
                duality(nc, dram, layer, xn, yT, small, cum, smallN, cumN, col, cst, ones, ring, banks, ident, scratch, acc)
                linears(nc, "ssd_gate_z", [Linear("ssd_z", dram["w_ssd_z"], layer * 8, 8, DC, xn,
                                                  [act_to(scratch, ACT.Silu), times(yT, scratch)])], ring, banks)
                with ExitStack() as tail:
                    yH = tail.enter_context(nc.sbuf_tensor("ssd_y_high", [P, 8, T], F32R))
                    yL = tail.enter_context(nc.sbuf_tensor("ssd_y_low", [P, 8, T], F32R))
                    gate, ssd_out = gate_and_out("ssd", 0, (chunks_of(yH), chunks_of(yL)), mixT)
                    ssd_out.steps += parts_of(mixT, xH, xL)
                    linears(nc, "ssd_tail", [gate, ssd_out, Linear("w_mix", dram["w_mix"], layer * 8, 8, DC, xn, add_steps(nc, hT),
                                                                   behind="ssd_out")], ring, banks,
                            pre=norm_to(yH, yL, chunks_of(yT), "ssd_g", 4, 512),
                            fill=(hT[:].rearrange("p c n -> p (c n)"), dram["stream"]))
            with ExitStack() as mlp:
                halves = [[mlp.enter_context(nc.sbuf_tensor(f"up_{n}{k}", [P, 8, T], F32R)) for n in ("high", "low")]
                          for k in range(2)]
                square = ("dve", False, lambda f, ps, s: nc.vector.tensor_tensor(part(scratch, f), part(scratch, f),
                                                                                 part(scratch, f), ALU.mult))

                def up(q):
                    high, low = halves[q % 2]
                    return Linear(f"w_up{q}", dram["w_up"], layer * 32 + 8 * q, 8, DC, xn,
                                  [act_to(scratch, ACT.Relu), square] + parts_of(scratch, high, low), fed=(q == 0))

                def down(q):
                    return Linear(f"w_down{q}", dram["w_down"], layer * 32 + 8 * q, 8, DC, tuple(chunks_of(t) for t in halves[q % 2]),
                                  add_steps(nc, hT), behind=f"w_up{q}")
                quarters = [up(0), up(1), down(0), up(2), down(1), up(3), down(2), down(3)]
                linears(nc, "mlp", quarters, ring, banks, pre=norm_to(xH, xL, chunks_of(hT), "norm2"))


def narrow_rows(nc, small, cum, smallN, cumN, col, ones, banks, ident, scratch):
    x, neg_abs, e, rate = scratch[:, 7, :], scratch[:, 1, :], scratch[:, 2, :], scratch[:, 3, 0:1]
    with stage(nc, "shifted magnitude logs rates beta_ready dve_step rows_ready turned copied") as (
            block, shifted, magnitude, logs, rates, beta, dve_step, rows_ready, turned, copied):
        @block.tensor
        def _(pe):
            pe.wait_ge(rows_ready, 1)
            for n, src in enumerate((small, cum)):
                for t in range(TT):
                    last = nc.tensor.transpose(banks[2 + n][:, t * P:(t + 1) * P], src[:, t * P:(t + 1) * P], ident)
                last.then_inc(turned, 1)

        @block.scalar
        def _(act):
            nc.scalar.activation(small[32:64, :], x[32:64, :], ACT.Sigmoid).then_inc(beta, 1)
            act.wait_ge(shifted, 1)
            nc.scalar.activation(e, neg_abs, ACT.Exp).then_inc(magnitude, 1)
            nc.scalar.activation(rate, col("a_log"), ACT.Exp).then_inc(rates, 1)
            act.wait_ge(magnitude, 1)
            nc.scalar.activation(e, e, ACT.Ln, bias=1.0).then_inc(logs, 1)
            for n, dst in enumerate((smallN, cumN)):
                act.wait_ge(turned, n + 1)
                nc.scalar.copy(dst[:].rearrange("p a b -> p (a b)"), banks[2 + n]).then_inc(copied, 1)

        @block.vector
        def _(dve):
            v = nc.vector
            link = Chain(dve, dve_step)
            link(v.tensor_scalar(neg_abs, x, -1.0, None, ALU.mult))
            v.tensor_tensor(neg_abs, x, neg_abs, ALU.min).then_inc(shifted, 1)
            link(v.memset(cum[:], 0.0))
            dve.wait_ge(rates, 1)
            dve.wait_ge(logs, 1)
            dve.wait_ge(beta, 1)
            link(v.scalar_tensor_tensor(x, x, 0.0, e, ALU.max, ALU.add))
            v.tensor_copy(small[0:32, :], x[0:32, :])
            v.tensor_copy(small[64:128, :], x[64:128, :])
            link(v.tensor_scalar(e, x, rate, -1.0, ALU.mult, ALU.mult))
            for t in range(TT):
                s = slice(t * P, (t + 1) * P)
                v.tensor_tensor_scan(cum[0:32, s], ones[0:32, :], e[0:32, s], 0.0, ALU.mult, ALU.add)
            for t in range(2 * TT):
                s = slice(t * 64, (t + 1) * 64)
                last = v.tensor_tensor_scan(cum[64:96, s], ones[64:96, 0:64], e[64:96, s], 0.0, ALU.mult, ALU.add)
            last.then_inc(rows_ready, 1)


def spread_row(nc, bank, src, base, h, ident):
    rows = slice(base, base + 32)
    return nc.tensor.matmul(bank, ident[rows, base + h:base + h + 1].to_broadcast([32, P]), src[rows, :], start=True, stop=True)


def wide(ap):
    return ap.unsqueeze(1).to_broadcast([ap.shape[0], TT, P])


def tiles4(bank):
    return bank.rearrange("p (t n) -> p t n", n=P)


def duality(nc, dram, layer, xn, yT, small, cum, smallN, cumN, col, cst, ones, ring, banks, ident, scratch, acc):
    with ExitStack() as held:
        def sb(name, shape, dt=F32):
            return held.enter_context(nc.sbuf_tensor(name, shape, dt))
        xp = sb("ssd_xbc", [P, 12, T + 3])
        with stage(nc, "ssd_zeroed") as (block, zeroed):
            @block.vector
            def _(dve):
                nc.vector.memset(xp[:, :, 0:3], 0.0)
        linears(nc, "ssd_in", [Linear("ssd_xbc", dram["w_ssd_xbc"], layer * 12, 12, DC, xn, conv_steps(
            nc, xp, lambda f, k: col("conv_ssd", f * 4 + k), lambda f: col("conv_ssd_b", f), acc), lag=True)], ring, banks)
        xdt = sb("ssd_xdt", [P, TT, D])
        xdd = scratch[:].rearrange("p (t c) n -> p t (c n)", c=2)[:, 0:3]
        Bn = sb("ssd_Bn", [P, 2, TT, P])
        CBT = sb("ssd_CBT", [P, 2, TT, P])
        H = ring
        last_cum = sb("ssd_last", [P, SSD_HEADS, TT])
        state_decay = sb("ssd_state_decay", [P, SSD_HEADS, TT])
        decay_end = sb("ssd_decay_end", [P, TT, SSD_HEADS])
        chunk_ends = tiles4(cum[0:32, :])[:, :, P - 1:P].squeeze(2)
        with stage(nc, "turned scaled b_turned b_copied cb_done cb_copied row_spread last_copied exps dve_step ends_ready") as (
                block, turned, scaled, b_turned, b_copied, cb_done, cb_copied, spread, last_copied, exps, dve_step, ends):
            @block.tensor
            def _(pe):
                for j in range(8):
                    t, half = divmod(j, 2)
                    if j >= 2:
                        pe.wait_ge(scaled, j - 1)
                    for k in range(4):
                        last = nc.tensor.transpose(banks[j % 2][:, k * P:(k + 1) * P], xp[:, 4 * half + k, t * P:(t + 1) * P], ident)
                    last.then_inc(turned, 1)
                for g in range(2):
                    for t in range(TT):
                        last = nc.tensor.transpose(banks[2 + g][:, t * P:(t + 1) * P], xp[:, 8 + g, t * P:(t + 1) * P], ident)
                    last.then_inc(b_turned, 1)
                    for t in range(TT):
                        s = slice(t * P, (t + 1) * P)
                        last = nc.tensor.matmul(banks[4 + g][:, s], xp[:, 8 + g, s], xp[:, 10 + g, s], start=True, stop=True)
                    last.then_inc(cb_done, 1)
                for h in range(SSD_HEADS):
                    last = nc.tensor.matmul(banks[6][:, h * TT:(h + 1) * TT], ident[0:32, h:h + 1].to_broadcast([32, P]),
                                            chunk_ends, start=True, stop=True)
                last.then_inc(spread, 1)

            @block.scalar
            def _(act):
                for g in range(2):
                    act.wait_ge(b_turned, g + 1)
                    nc.scalar.copy(Bn[:, g], tiles4(banks[2 + g])).then_inc(b_copied, 1)
                    act.wait_ge(cb_done, g + 1)
                    nc.scalar.copy(CBT[:, g], tiles4(banks[4 + g])).then_inc(cb_copied, 1)
                act.wait_ge(spread, 1)
                nc.scalar.copy(last_cum[:].rearrange("p h t -> p (h t)"), banks[6][:, 0:SSD_HEADS * TT]).then_inc(last_copied, 1)
                act.wait_ge(last_copied, 1)
                nc.scalar.activation(state_decay[:], last_cum[:], ACT.Exp).then_inc(exps, 1)
                act.wait_ge(ends, 1)
                nc.scalar.activation(decay_end[:], decay_end[:], ACT.Exp).then_inc(exps, 1)

            @block.vector
            def _(dve):
                v = nc.vector
                link = Chain(dve, dve_step)
                for j in range(8):
                    t, half = divmod(j, 2)
                    dve.wait_ge(turned, j + 1)
                    v.tensor_tensor(xdt[:, t, 512 * half:512 * half + 512].rearrange("p (h d) -> p h d", d=64),
                                    banks[j % 2].rearrange("p (h d) -> p h d", d=64),
                                    bc(smallN[:, t, 8 * half:8 * half + 8], 64), ALU.mult).then_inc(scaled, 1)
                dve.wait_ge(last_copied, 1)
                v.tensor_tensor(decay_end[:], last_cum[:].rearrange("p h t -> p t h"), cumN[:, :, 0:SSD_HEADS], ALU.subtract)\
                    .then_inc(ends, 1)
                dve.wait_ge(exps, 2)
                dve.wait_ge(scaled, 8)
                for t in range(3):
                    link(v.tensor_tensor(xdd[:, t, :].rearrange("p (h d) -> p h d", d=64),
                                         xdt[:, t, :].rearrange("p (h d) -> p h d", d=64), bc(decay_end[:, t, :], 64), ALU.mult))
        with stage(nc, "states_done dve_step") as (block, done, dve_step):
            @block.tensor
            def _(pe):
                for t in range(3):
                    for g in range(2):
                        nc.tensor.matmul(banks[2 * t + g], Bn[:, g, t, :], xdd[:, t, 512 * g:512 * g + 512],
                                         start=True, stop=True).then_inc(done, 1)

            @block.vector
            def _(dve):
                v = nc.vector
                link = Chain(dve, dve_step)
                for t in range(3):
                    for g in range(2):
                        dve.wait_ge(done, 2 * t + g + 1)
                        s = slice(512 * g, 512 * g + 512)
                        if t == 0:
                            link(v.tensor_copy(H[:, 0, s], banks[g]))
                        else:
                            link(v.tensor_tensor(H[:, t, s].rearrange("p (h d) -> p h d", d=64),
                                                 H[:, t - 1, s].rearrange("p (h d) -> p h d", d=64),
                                                 bc(state_decay[:, 8 * g:8 * g + 8, t], 64), ALU.mult))
                            link(v.tensor_tensor(H[:, t, s], H[:, t, s], banks[2 * t + g], ALU.add))
        L = sb("ssd_L", [P, 4, T])
        CE = sb("ssd_CE", [P, 4, T])
        row_banks = [banks[b] for b in (0, 1, 4, 5)]
        with stage(nc, "row_spread differences masked exps weighted c_scaled y_done y_stored") as (
                block, spread, differences, masked, exps, weighted, c_scaled, y_done, y_stored):
            @block.tensor
            def _(pe):
                def row_of(h):
                    if h >= 4:
                        pe.wait_ge(exps, 2 * (h - 3))
                    spread_row(nc, row_banks[h % 4], cum, DT_ROWS, h, ident).then_inc(spread, 1)
                for h in range(3):
                    row_of(h)
                for h in range(SSD_HEADS):
                    if h + 3 < SSD_HEADS:
                        row_of(h + 3)
                    out = banks[2 + (h // 2) % 2][64 * (h % 2):64 * (h % 2) + 64, :]
                    pe.wait_ge(weighted, h + 1)
                    pe.wait_ge(c_scaled, h + 1)
                    if h % 2 == 0 and h >= 4:
                        pe.wait_ge(y_stored, h // 2 - 1)
                    for t in range(TT):
                        s = slice(t * P, (t + 1) * P)
                        last = nc.tensor.matmul(out[:, s], xdt[:, t, 64 * h:64 * h + 64], L[:, h % 4, s], start=True, stop=(t == 0))
                        if t:
                            last = nc.tensor.matmul(out[:, s], H[:, t - 1, 64 * h:64 * h + 64], CE[:, h % 4, s], start=False, stop=True)
                    last.then_inc(y_done, 1)

            @block.vector
            def _(dve):
                v = nc.vector

                def finish(c):
                    dve.wait_ge(y_done, 2 * c + 2)
                    v.scalar_tensor_tensor(yT[:, c, :], xp[:, c, 0:T], col("ssd_d", c), banks[2 + c % 2], ALU.mult, ALU.add)\
                        .then_inc(y_stored, 1)

                def differ(h):
                    dve.wait_ge(spread, h + 1)
                    if h >= 4:
                        dve.wait_ge(y_done, h - 3)
                    v.tensor_tensor(tiles4(L[:, h % 4]), tiles4(row_banks[h % 4]), cumN[:, :, h:h + 1].to_broadcast([P, TT, P]),
                                    ALU.subtract).then_inc(differences, 1)
                    dve.wait_ge(differences, h + 1)
                    v.tensor_tensor(tiles4(L[:, h % 4]), tiles4(L[:, h % 4]), wide(cst("neg128")), ALU.add).then_inc(masked, 1)

                differ(0)
                differ(1)
                for h in range(SSD_HEADS):
                    if h + 2 < SSD_HEADS:
                        differ(h + 2)
                    dve.wait_ge(exps, 2 * h + 2)
                    v.tensor_tensor(tiles4(L[:, h % 4]), tiles4(L[:, h % 4]), CBT[:, h // 8], ALU.mult).then_inc(weighted, 1)
                    if h % 2 == 1 and h >= 3:
                        finish(h // 2 - 1)
                finish(7)

            @block.scalar
            def _(act):
                for h in range(SSD_HEADS):
                    act.wait_ge(differences, h + 1)
                    if h >= 4:
                        act.wait_ge(y_done, h - 3)
                    nc.scalar.activation(CE[:, h % 4, :], row_banks[h % 4], ACT.Exp).then_inc(exps, 1)
                    act.wait_ge(masked, h + 1)
                    nc.scalar.activation(L[:, h % 4, :], L[:, h % 4, :], ACT.Exp).then_inc(exps, 1)

            @block.gpsimd
            def _(pool):
                for h in range(SSD_HEADS):
                    pool.wait_ge(exps, 2 * h + 1)
                    nc.gpsimd.tensor_tensor(CE[:, h % 4, :], CE[:, h % 4, :], xp[:, 10 + h // 8, 0:T], ALU.mult).then_inc(c_scaled, 1)


def latent_attention(nc, dram, layer, c8, yT, col, cst, ones, ring, banks, ident, scratch, tools, spare, cosT, sinT):
    def into(dst):
        return lambda nc, f, ps: nc.scalar.copy(part(dst, f), ps)
    with ExitStack() as held:
        def sb(name, shape, dt=F32):
            return held.enter_context(nc.sbuf_tensor(name, shape, dt))
        q = sb("mla_q", [P, 12, T])
        kn = sb("mla_k", [P, 4, T])
        vals = sb("mla_v", [P, TT, D])
        rmsnorm(nc, "mla_norm_q", lambda c: c8[:, c, :], lambda c: c8[:, c, :], 4, 4, tools, 512, lambda c: col("mla_q_g", c),
                lambda c: scratch[:, c, :], banks)
        rmsnorm(nc, "mla_norm_kv", lambda c: c8[:, 4 + c, :], lambda c: c8[:, 4 + c, :], 2, 2, tools, 256, lambda c: col("mla_kv_g", c),
                lambda c: scratch[:, c, :], banks)
        linear(nc, "mla_uq", dram["w_mla_uq"], layer * 12, 12, lambda c: c8[:, c, :], 4, ring, banks, into(q))
        for n, dst in enumerate((c8, kn)):
            linear(nc, f"mla_uk{n}", dram["w_mla_uk"], layer * 8 + 4 * n, 4, lambda c: c8[:, 4 + c, :], 2, ring, banks,
                   into(dst))
        def rotations(block, step, pool_step):
            def rotate(eng, ops, sem, a, b, t0, t1):
                link = Chain(eng, sem)
                for x, y in zip(a, b):
                    link(ops.tensor_tensor(t0, x, sinT[:], ALU.mult))
                    link(ops.tensor_tensor(t1, y, sinT[:], ALU.mult))
                    link(ops.tensor_tensor(x, x, cosT[:], ALU.mult))
                    link(ops.tensor_tensor(x, x, t1, ALU.subtract))
                    link(ops.tensor_tensor(y, y, cosT[:], ALU.mult))
                    link(ops.tensor_tensor(y, y, t0, ALU.add))

            @block.vector
            def _(dve):
                rotate(dve, nc.vector, step, [q[:, 8, :], q[:, 9, :]], [q[:, 10, :], q[:, 11, :]], scratch[:, 0, :], scratch[:, 1, :])

            @block.gpsimd
            def _(pool):
                rotate(pool, nc.gpsimd, pool_step, [c8[:, 6, :]], [c8[:, 7, :]], scratch[:, 2, :], scratch[:, 3, :])

        for n in range(2):
            linear_tokens(nc, f"mla_uv{n}", dram["w_mla_uv"], layer * 2 + n, lambda c: c8[:, 4 + c, :], 2, ring, banks, TT,
                          lambda t, n=n: vals[:, t, n * 512:(n + 1) * 512],
                          aside=None if n else rotations)

        def scores(h, qt):
            r = slice(32 * (h % 4), 32 * (h % 4) + 32)
            qs, ks = slice(qt * P, (qt + 1) * P), slice(0, (qt + 1) * P)
            return [(q[:, h, qs], (c8 if h < 4 else kn)[:, h % 4, ks]), (q[r, 8 + h // 4, qs], c8[r, 6, ks]), (q[r, 10 + h // 4, qs], c8[r, 7, ks])]
        attention(nc, "latent", 8, scores, lambda qt: qt + 1, 192 ** -0.5, lambda h, qt: cst("causal", 384 - P * qt, P * (qt + 1)),
                  lambda h, k: vals[:, k, h * P:(h + 1) * P], P, lambda h: slice(0, P), lambda h: yT[:, h, :],
                  banks, *attention_memory(scratch, ring, spare), ident)


def delta_rule(nc, dram, psum, layer, yT, small, cum, smallN, cumN, col, cst, ones, ring, banks, ident, scratch, tools, spare,
               xn, norm, acc, hT):
    B4 = 4
    with ExitStack() as held:
        def sb(name, shape, dt=F32):
            return held.enter_context(nc.sbuf_tensor(name, shape, dt))
        xp = sb("gdn_qkv", [P, 16, T + 3])
        with stage(nc, "gdn_zeroed") as (block, zeroed):
            @block.vector
            def _(dve):
                nc.vector.memset(xp[:, :, 0:3], 0.0)
        linears(nc, "gdn_in", [
            Linear("narrow", dram["w_narrow"], layer, 1, DC, xn,
                   [("dve", True, lambda f, ps, s: nc.vector.tensor_scalar(scratch[:, 7, :], ps, col("small_b"), None, ALU.add))],
                   fed=True),
            Linear("gdn_qkv", dram["w_gdn_qkv"], layer * 16, 16, DC, xn,
                   conv_steps(nc, xp, lambda f, k: col("conv_gdn", f * 4 + k), None, acc), lag=True)],
            ring, banks, pre=norm, spill=(dram["stream"], hT[:].rearrange("p c n -> p (c n)")))
        narrow_rows(nc, small, cum, smallN, cumN, col, ones, banks, ident, scratch)
        rmsnorm(nc, "gdn_l2", lambda c: xp[:, c, 0:T], lambda c: xp[:, c, 0:T], 8, 1, tools, 1.0, None,
                lambda c: scratch[:, c, :], banks, mean=False)
        acT = sb("gdn_acT", [P, B4, TT, P])
        qg = sb("gdn_qg", [P, B4, T])
        kd = sb("gdn_kd", [P, B4, TT, P])
        uN = yT[:].rearrange("p c (t n) -> p c t n", n=P)[:, 0:4]
        wT = yT[:, 4:8, :]
        AT = scratch[:].rearrange("p c (t n) -> p c t n", n=P)[:, 0:4]
        Tn = scratch[:].rearrange("p c (t n) -> p c t n", n=P)[:, 4:8]
        Tt = sb("gdn_Tt", [P, B4, TT, P])
        vb = sb("gdn_vb", [P, B4, TT, P])
        kb = sb("gdn_kb", [P, B4, TT, P])
        ring4 = ring[:].rearrange("p s (a t n) -> p s a t n", t=TT, n=P)
        Dm = [ring4[:, 0, 0], ring4[:, 0, 1]]
        eg = [ring4[:, 1, 0], ring4[:, 1, 1]]
        am = [ring4[:, 2, 0], ring4[:, 2, 1]]
        Wb = [ring4[:, 3, 0], ring4[:, 3, 1]]
        S = spare[:, 0, :].rearrange("p (x n) -> p x n", n=P)
        Sd = spare[:, 1, :].rearrange("p (x n) -> p x n", n=P)
        vn = sb("gdn_vn", [P, B4, P])
        g_last = sb("gdn_last", [P, B4, 8])
        g_end = sb("gdn_end", [P, B4, TT])
        kbs = sb("gdn_kbs", [P, TT, B4])

        for hb in range(2):
            heads = [4 * hb + x for x in range(B4)]
            g0 = A_ROWS + 4 * hb
            b0 = BETA_ROWS + 4 * hb
            with stage(nc, "products_done differ masked exps ends_done dve_step banks_used ends_exp") as (
                    block, products, differ, masked, exps, ends, dve_step, used, ends_exp):
                @block.tensor
                def _(pe):
                    for x, h in enumerate(heads):
                        b = 4 * (x % 2)
                        if x >= 2:
                            pe.wait_ge(used, x - 1)
                        q_, k_ = xp[:, h // 2, :], xp[:, 4 + h // 2, :]
                        spread_row(nc, banks[b], cum, A_ROWS, h, ident)
                        spread_row(nc, banks[b + 1], small, BETA_ROWS, h, ident)
                        for n, r in ((2, q_), (3, k_)):
                            for t in range(TT):
                                s = slice(t * P, (t + 1) * P)
                                last = nc.tensor.matmul(banks[b + n][:, s], k_[:, s], r[:, s], start=True, stop=True)
                        last.then_inc(products, 1)

                @block.vector
                def _(dve):
                    v = nc.vector
                    link = Chain(dve, dve_step)
                    for x, h in enumerate(heads):
                        b = 4 * (x % 2)
                        dve.wait_ge(products, x + 1)
                        v.tensor_tensor(Dm[x % 2], tiles4(banks[b]), cumN[:, :, A_ROWS + h:A_ROWS + h + 1].to_broadcast([P, TT, P]),
                                        ALU.subtract).then_inc(differ, 1)
                        dve.wait_ge(differ, x + 1)
                        v.tensor_tensor(Dm[x % 2], Dm[x % 2], wide(cst("neg64")), ALU.add).then_inc(masked, 1)
                        v.tensor_copy(g_last[:, x, :], banks[b].rearrange("p (c n) -> p c n", n=64)[:, :, 63:64].squeeze(2))
                        t_ = tiles4(banks[b])
                        v.tensor_copy(g_end[0:64, x, :], t_[0:64, :, 63:64].squeeze(2))
                        link(v.tensor_copy(g_end[64:128, x, :], t_[64:128, :, 127:128].squeeze(2)))
                        v.tensor_tensor(g_end[:, x, :], g_end[:, x, :], cumN[:, :, A_ROWS + h:A_ROWS + h + 1].squeeze(2), ALU.subtract)\
                            .then_inc(ends, 1)
                        dve.wait_ge(exps, 2 * x + 2)
                        v.scalar_tensor_tensor(acT[:, x].rearrange("p t n -> p (t n)"), banks[b + 2], GDN_SCALE,
                                               Dm[x % 2].rearrange("p t n -> p (t n)"), ALU.mult, ALU.mult)
                        link(v.tensor_tensor(AT[:, x], tiles4(banks[b + 3]), Dm[x % 2], ALU.mult))
                        link(v.tensor_tensor(AT[:, x], AT[:, x], tiles4(banks[b + 1]), ALU.mult))
                        link(v.tensor_tensor(AT[:, x], AT[:, x], wide(cst("strict64")), ALU.mult))
                        v.scalar_tensor_tensor(qg[:, x, :], xp[:, h // 2, 0:T], GDN_SCALE, eg[x % 2].rearrange("p t n -> p (t n)"),
                                               ALU.mult, ALU.mult).then_inc(used, 1)
                    dve.wait_ge(ends_exp, 3)
                    v.tensor_tensor(kbs[:], kbs[:], smallN[:, :, b0:b0 + B4], ALU.mult)

                @block.scalar
                def _(act):
                    for x in range(B4):
                        act.wait_ge(ends, x + 1)
                        if x >= 2:
                            act.wait_ge(used, x - 1)
                        nc.scalar.activation(eg[x % 2], tiles4(banks[4 * (x % 2)]), ACT.Exp).then_inc(exps, 1)
                        act.wait_ge(masked, x + 1)
                        nc.scalar.activation(Dm[x % 2], Dm[x % 2], ACT.Exp).then_inc(exps, 1)
                    act.wait_ge(ends, B4)
                    nc.scalar.activation(g_end[:], g_end[:], ACT.Exp).then_inc(ends_exp, 1)
                    nc.scalar.activation(g_last[:], g_last[:], ACT.Exp).then_inc(ends_exp, 1)
                    nc.scalar.activation(kbs[:], cumN[:, :, g0:g0 + B4], ACT.Exp).then_inc(ends_exp, 1)

            with stage(nc, "turned scaled dve_step t_ready t_turned t_copied") as (
                    block, turned, scaled, dve_step, t_ready, t_turned, t_copied):
                @block.tensor
                def _(pe):
                    for x, h in enumerate(heads):
                        b = 2 * (x % 2)
                        if x >= 2:
                            pe.wait_ge(scaled, x - 1)
                        for n, c in enumerate((8 + h, 4 + h // 2)):
                            for t in range(TT):
                                s = slice(t * P, (t + 1) * P)
                                last = nc.tensor.transpose(banks[b + n][:, s], xp[:, c, s], ident)
                        last.then_inc(turned, 1)
                    for x in range(B4):
                        pe.wait_ge(t_ready, x + 1)
                        for t in range(TT):
                            last = nc.tensor.transpose(banks[4 + x][:, t * P:(t + 1) * P], Tt[:, x, t, :], ident)
                        last.then_inc(t_turned, 1)

                @block.vector
                def _(dve):
                    v = nc.vector
                    link = Chain(dve, dve_step)
                    for x, h in enumerate(heads):
                        b = 2 * (x % 2)
                        dve.wait_ge(turned, x + 1)
                        v.tensor_tensor(vb[:, x], tiles4(banks[b]), smallN[:, :, BETA_ROWS + h:BETA_ROWS + h + 1].to_broadcast([P, TT, P]), ALU.mult)
                        v.tensor_tensor(kb[:, x], tiles4(banks[b + 1]), kbs[:, :, x:x + 1].to_broadcast([P, TT, P]), ALU.mult)
                        v.tensor_tensor(kd[:, x], tiles4(banks[b + 1]), bc(g_end[:, x, :], P), ALU.mult).then_inc(scaled, 1)
                    for x in range(B4):
                        link(v.tensor_tensor(Tt[:, x], AT[:, x], wide(cst("level", 0, P)), ALU.mult))
                        v.tensor_tensor(Tt[:, x], wide(ident), Tt[:, x], ALU.subtract).then_inc(t_ready, 1)

                @block.scalar
                def _(act):
                    for x in range(B4):
                        act.wait_ge(t_turned, x + 1)
                        nc.scalar.copy(Tn[:, x], tiles4(banks[4 + x])).then_inc(t_copied, 1)

            jobs = [(k, x) for k in range(1, 6) for x in range(B4)]
            with stage(nc, "level_ready w_done w_copied v_done half_updated updated") as (
                    block, level_ready, w_done, w_copied, v_done, half_updated, updated):
                @block.gpsimd
                def _(pool):
                    for j, (k, x) in enumerate(jobs):
                        if j >= 2:
                            pool.wait_ge(w_done, j - 1)
                        nc.gpsimd.tensor_tensor(am[j % 2], AT[:, x], wide(cst("level", k * P, P)), ALU.mult).then_inc(level_ready, 1)

                @block.tensor
                def _(pe):
                    def w(j):
                        k, x = jobs[j]
                        pe.wait_ge(level_ready, j + 1)
                        if j >= 4:
                            pe.wait_ge(updated, j - 3)
                        if j >= 2:
                            pe.wait_ge(w_copied, j - 1)
                        for t in range(TT):
                            last = nc.tensor.matmul(banks[j % 2][:, t * P:(t + 1) * P], am[j % 2][:, t, :], Tn[:, x, t, :], start=True, stop=True)
                        last.then_inc(w_done, 1)

                    w(0)
                    for j, (k, x) in enumerate(jobs):
                        if j + 1 < len(jobs):
                            w(j + 1)
                        pe.wait_ge(w_copied, j + 1)
                        if j >= 2:
                            pe.wait_ge(updated, j - 1)
                        for t in range(TT):
                            s = slice(t * P, (t + 1) * P)
                            last = nc.tensor.matmul(banks[2 + j % 2][:, s], Wb[j % 2][:, t, :], Tt[:, x, t, :], start=True, stop=True)
                            if k < 5:
                                last = nc.tensor.matmul(banks[4 + j % 2][:, s], Tt[:, x, t, :], Wb[j % 2][:, t, :], start=True, stop=True)
                        last.then_inc(v_done, 1)

                @block.scalar
                def _(act):
                    for j in range(len(jobs)):
                        act.wait_ge(w_done, j + 1)
                        if j >= 2:
                            act.wait_ge(v_done, j - 1)
                        nc.scalar.copy(Wb[j % 2], tiles4(banks[j % 2])).then_inc(w_copied, 1)

                @block.vector
                def _(dve):
                    for j, (k, x) in enumerate(jobs):
                        dve.wait_ge(v_done, j + 1)
                        last = nc.vector.tensor_tensor(Tt[:, x], Tt[:, x], tiles4(banks[2 + j % 2]), ALU.subtract)
                        if k < 5:
                            last = nc.vector.tensor_tensor(Tn[:, x], Tn[:, x], tiles4(banks[4 + j % 2]), ALU.subtract)
                        last.then_inc(updated, 1)

            with stage(nc, "solved u_copied w_copied") as (block, solved, u_copied, w_copied):
                @block.tensor
                def _(pe):
                    for x in range(B4):
                        if x >= 2:
                            pe.wait_ge(u_copied, x - 1)
                            pe.wait_ge(w_copied, x - 1)
                        for t in range(TT):
                            s = slice(t * P, (t + 1) * P)
                            nc.tensor.matmul(banks[x % 2][:, s], Tt[:, x, t, :], vb[:, x, t, :], start=True, stop=True)
                            last = nc.tensor.matmul(banks[2 + x % 2][:, s], kb[:, x, t, :], Tt[:, x, t, :], start=True, stop=True)
                        last.then_inc(solved, 1)

                @block.scalar
                def _(act):
                    for x in range(B4):
                        act.wait_ge(solved, x + 1)
                        nc.scalar.copy(uN[:, x], tiles4(banks[x % 2])).then_inc(u_copied, 1)

                @block.vector
                def _(dve):
                    for x in range(B4):
                        dve.wait_ge(solved, x + 1)
                        nc.vector.tensor_copy(wT[:, x, :], banks[2 + x % 2]).then_inc(w_copied, 1)

            with stage(nc, "state_ready ws_done v_new_ready o_done ds_done o_copied decayed") as (
                    block, state_ready, ws_done, v_new, o_done, ds_done, o_copied, decayed):
                @block.tensor
                def _(pe):
                    for c in range(8):
                        t, half = divmod(c, 2)
                        r = slice(64 * half, 64 * half + 64)
                        s = slice(64 * c, 64 * c + 64)
                        pe.wait_ge(state_ready, c + 1)
                        for x in range(B4):
                            last = nc.tensor.matmul(banks[0][r, x * P:(x + 1) * P], wT[:, x, s], S[:, x, :], start=True, stop=True)
                        last.then_inc(ws_done, 1)
                        if c >= 1:
                            pe.wait_ge(o_copied, c)
                        for x in range(B4):
                            nc.tensor.matmul(banks[4 + x][:, 0:64], S[:, x, :], qg[:, x, s], start=True, stop=False)
                        pe.wait_ge(v_new, c + 1)
                        for x in range(B4):
                            last = nc.tensor.matmul(banks[2][:, x * P:(x + 1) * P], kd[r, x, t, :], vn[r, x, :], start=True, stop=True)
                        last.then_inc(ds_done, 1)
                        for x in range(B4):
                            last = nc.tensor.matmul(banks[4 + x][:, 0:64], vn[r, x, :], acT[r, x, t, 64 * half:64 * half + 64],
                                                    start=False, stop=True)
                        last.then_inc(o_done, 1)

                @block.vector
                def _(dve):
                    v = nc.vector
                    v.memset(S[:], 0.0).then_inc(state_ready, 1)
                    dve.wait_ge(state_ready, 1)
                    for c in range(8):
                        t, half = divmod(c, 2)
                        r = slice(64 * half, 64 * half + 64)
                        dve.wait_ge(ws_done, c + 1)
                        v.tensor_tensor(vn[r], uN[r, :, t, :], banks[0][r, :].rearrange("p (x n) -> p x n", n=P), ALU.subtract)\
                            .then_inc(v_new, 1)
                        v.tensor_tensor(Sd[:], S[:], g_last[:, :, c:c + 1].to_broadcast([P, B4, P]), ALU.mult).then_inc(decayed, 1)
                        dve.wait_ge(decayed, c + 1)
                        dve.wait_ge(ds_done, c + 1)
                        v.tensor_tensor(S[:], Sd[:], banks[2].rearrange("p (x n) -> p x n", n=P), ALU.add).then_inc(state_ready, 1)
                        dve.wait_ge(state_ready, c + 2)

                @block.scalar
                def _(act):
                    for c in range(8):
                        act.wait_ge(o_done, c + 1)
                        nc.scalar.copy(xp[:, 8 + 4 * hb:12 + 4 * hb, 64 * c:64 * c + 64],
                                       psum[:, 4:8, 0:64]).then_inc(o_copied, 1)
        rmsnorm(nc, "gdn_norm", lambda c: xp[:, 8 + c, 0:T], lambda c: yT[:, c, :], 8, 1, tools, P, lambda c: col("gdn_g"),
                lambda c: scratch[:, c, :], banks)


def program(nc, dram, out):
    with ExitStack() as held:
        def sb(name, shape, dt=F32):
            return held.enter_context(nc.sbuf_tensor(name, shape, dt))
        psum = held.enter_context(nc.psum_tensor("banks", [P, 8, 512], F32))
        hT = sb("hT", [P, DC, T])
        scratch = sb("scratch", [P, 8, T])
        ring = sb("ring", [P, SLOTS, 8 * P])
        spare = sb("spare", [P, 2, T])
        ones = sb("ones", [P, P])
        columns = sb("columns", [P, 3])
        eps = sb("eps", [P, 1])
        roots = sb("roots", [P, 64])
        ident = sb("ident", [P, P])
        tools = (roots, eps[:], ident[:], columns)
        with stage(nc, "filled made") as (block, filled, made):
            @block.gpsimd
            def _(pool):
                nc.gpsimd.memset(ident[:], 0.0).then_inc(filled, 1)
                pool.wait_ge(filled, 1)
                nc.gpsimd.affine_select(out=ident[:], in_=ident[:], compare_op=ALU.not_equal, fill=1.0, base=0,
                                        pattern=[[-1, P]], channel_multiplier=1)

            @block.vector
            def _(dve):
                nc.vector.memset(ones[:], 1.0)
                nc.vector.memset(eps[:], EPS)
                nc.vector.memset(columns[:], 0.0).then_inc(made, 1)
                dve.wait_ge(made, 1)
                nc.vector.memset(columns[:, 0:1], 1.0)
                for k in range(2):
                    nc.vector.memset(columns[64 * k:64 * k + 64, 1 + k:2 + k], 1.0)

        first_block(nc, dram, psum, hT, scratch, ring, tools, spare, ident[:])
        second_block(nc, dram, psum, hT, scratch, ring, tools, spare, ones[:], ident[:])
        final_g = sb("final_g", [P, DC])
        banks = [psum[:, b, :] for b in range(8)]
        with stage(nc, "final_g_loaded") as (block, loaded):
            @block.sync
            def _(sp):
                sp.dma_start(final_g[:], dram["final_g"]).then_inc(loaded, 16)
                sp.wait_ge(loaded, 16)
        norm = Norm(nc, chunks_of(hT), chunks_of(hT), DC, DC, tools, D, lambda c: final_g[:, c:c + 1], chunks_of(scratch), banks)
        with stage(nc, "stored " + " ".join(f"final_{n}" for n in norm.NAMES.split())) as (block, stored, *sems):
            norm.take(sems)
            block.scalar(norm.act)
            block.tensor(norm.pe)
            block.vector(norm.dve)

            @block.sync
            def _(sp):
                for c in range(DC):
                    sp.wait_ge(norm.scaled, c + 1)
                    sp.dma_start(out[:, c * T:(c + 1) * T], hT[:, c, :]).then_inc(stored, 16)
                sp.wait_ge(stored, 16 * DC)



def _tiles(w):
    import numpy as np
    k, n = w.shape
    return np.ascontiguousarray(w.reshape(k // P, P, n // P, P).transpose(2, 1, 0, 3)).reshape(n // P, P, k)


def _strips(w, n=512):
    import numpy as np
    k, m = w.shape
    return np.ascontiguousarray(w.reshape(k // P, P, m // n, n).transpose(2, 1, 0, 3)).reshape(m // n, P, k // P * n)


def _cols(v):
    return v.reshape(-1, P).T


def _chunks(x):
    import numpy as np
    k, n = x.shape
    return np.ascontiguousarray(x.reshape(k // P, P, n).transpose(1, 0, 2)).reshape(P, -1)


def _layout_first(a):
    import numpy as np
    d = {}
    d["xT"] = _chunks(a["x"][0].T)
    d["memT"] = _chunks(a["mem"][0].T)
    d["w_in"] = _tiles(a["w_in"][0])
    dist = np.arange(P)[:, None] - (np.arange(512)[None, :] - 384)
    d["bias"] = np.ascontiguousarray(a["rel_bias"][0][:, np.clip(dist, -63, 128) + 63].transpose(1, 0, 2)).reshape(P, -1)
    c = {n: np.zeros((P, 16, 32), np.float32) for n in ("c_re", "c_im")}
    b = {n: np.zeros((P, 4, 128), np.float32) for n in ("b_re", "b_im")}
    for n in ("re", "im"):
        src_c, src_b = a["ssm_c_" + n][0], a["ssm_b_" + n][0]
        for g in range(32):
            i, k = divmod(g, 2)
            c["c_" + n][64 * k:64 * k + 64, i, 16 * k:16 * k + 16] = src_c[g].T
            p = 32 * (i % 4) + 16 * k
            b["b_" + n][p:p + 16, i // 4, 64 * k:64 * k + 64] = src_b[g].T
    for n, v in list(c.items()) + list(b.items()):
        d[n] = v.reshape(P, -1)
    d["w_glu"] = _tiles(a["ssm_w_glu"][0])
    d["w_out"] = _tiles(a["w_out"][0])
    for n in ("w_mem_q", "w_mem_k", "w_mem_v", "w_mem_o"):
        d[n] = _tiles(a[n][0])
    d["w_peer_q"] = _tiles(a["w_peer_q"][0])
    d["peer_keys"] = np.ascontiguousarray(a["peer_keys"][0].reshape(16, P, P).transpose(2, 0, 1)).reshape(P, -1)
    d["peer_u"] = _tiles(a["peer_u"][0].T)
    d["peer_v"] = a["peer_v"][0].reshape(P, P, D)
    state = lambda v: v.reshape(16, P).T
    parts = dict(mix_g=_cols(a["norm_mix_g"][0]), att_q_g=_cols(np.tile(a["att_q_g"][0], 2)),
                 att_k_g=_cols(np.tile(a["att_k_g"][0], 2)), lam_re=state(a["ssm_lam_re"][0]),
                 lam_im=state(a["ssm_lam_im"][0]), log_step=state(np.repeat(a["ssm_log_step"][0], 64)),
                 ssm_d=_cols(a["ssm_d"][0].reshape(-1)), b_glu=_cols(a["ssm_b_glu"][0]),
                 mixed_g=np.concatenate([_cols(a["att_out_g"][0]), _cols(a["ssm_out_g"][0])], axis=1),
                 mem_g=_cols(a["norm_mem_g"][0]), memkv_g=_cols(a["norm_memkv_g"][0]), mem_q_g=_cols(a["mem_q_g"][0]),
                 mem_k_g=_cols(a["mem_k_g"][0]), peer_g=_cols(a["norm_peer_g"][0]))
    assert list(parts) == list(VEC1)
    d["vec1"] = np.concatenate([parts[n] for n in VEC1], axis=1)
    return d


def _layout_second(a):
    import numpy as np
    d = {}
    a = {n[:-2]: v for n, v in a.items() if n.endswith("_2")}
    both = lambda f: np.concatenate([f(l) for l in range(LAYERS)])
    at = np.cumsum([0, 1024, 1536, 16, 512, 256, 64, 2048, 1024, 8, 8, 3072])
    part = lambda l, n: a["w_in"][l][:, at[n]:at[n + 1]]
    d["w_ssd_z"] = both(lambda l: _tiles(part(l, 0)))
    d["w_ssd_xbc"] = both(lambda l: _tiles(part(l, 1)))
    d["w_gdn_qkv"] = both(lambda l: _tiles(part(l, 6)))
    d["w_gdn_z"] = both(lambda l: _tiles(part(l, 7)))
    d["w_gate"] = both(lambda l: _tiles(part(l, 10)))

    def narrow(l):
        w = np.zeros((D, P), np.float32)
        w[:, DT_ROWS:DT_ROWS + 16] = part(l, 2)
        w[:, BETA_ROWS:BETA_ROWS + 8] = part(l, 8)
        w[:, A_ROWS:A_ROWS + 8] = part(l, 9)
        return _tiles(w)
    d["w_narrow"] = both(narrow)

    def mla_in(l):
        kr = part(l, 5)
        return _tiles(np.concatenate([part(l, 3), part(l, 4), np.tile(kr[:, 0:32], (1, 4)), np.tile(kr[:, 32:64], (1, 4))], axis=1))
    d["w_mla_in"] = both(mla_in)

    def uq(l):
        w = a["mla_w_uq"][l].reshape(512, 8, 192)
        return _tiles(np.concatenate([w[:, :, n0:n1].reshape(512, -1) for n0, n1 in ((0, 128), (128, 160), (160, 192))], axis=1))
    d["w_mla_uq"] = both(uq)
    ukv = lambda l: a["mla_w_ukv"][l].reshape(256, 8, 256)
    d["w_mla_uk"] = both(lambda l: _tiles(ukv(l)[:, :, 0:128].reshape(256, -1)))
    d["w_mla_uv"] = both(lambda l: _strips(ukv(l)[:, :, 128:256].reshape(256, -1)))
    for n, src in (("w_ssd_out", "w_ssd_out"), ("w_mla_out", "w_mla_out"), ("w_gdn_out", "w_gdn_out"), ("w_mix", "w_out"),
                   ("w_up", "w_up")):
        d[n] = both(lambda l: _tiles(a[src][l]))
    d["w_down"] = both(lambda l: np.ascontiguousarray(
        _tiles(a["w_down"][l]).reshape(8, P, 4, 1024).transpose(2, 0, 1, 3)).reshape(32, P, 1024))
    d["positions"] = np.tile(a["positions"].reshape(1, T), (P, 1))

    m, l = np.arange(P)[:, None], np.arange(P)[None, :]
    neg = lambda keep: np.where(keep, 0.0, NEG)
    levels = [((m ^ l) >= 1 << k) & ((m ^ l) < 2 << k) & (l > m) for k in range(6)]
    inv = 10000.0 ** (-np.arange(0, 64, 2, dtype=np.float32) / np.float32(64))
    parts = dict(neg128=neg(l >= m), neg64=neg((l >= m) & (l // 64 == m // 64)), strict64=(l > m) & (l // 64 == m // 64),
                 level=np.concatenate(levels, axis=1), causal=np.concatenate([np.zeros((P, 384)), neg(l <= m)], axis=1),
                 inv_freq=np.tile(inv, 4)[:, None])
    assert list(parts) == list(CONST)
    d["consts"] = np.concatenate([np.asarray(v, np.float32) for v in parts.values()], axis=1)

    def vec(l):
        conv = lambda w: w.reshape(4, -1, P).transpose(2, 1, 0).reshape(P, -1)
        small = np.zeros((2, P, 1), np.float32)
        small[0, DT_ROWS:DT_ROWS + 16, 0], small[0, A_ROWS:A_ROWS + 8, 0] = a["ssd_dt_bias"][l], a["gdn_dt_bias"][l]
        small[1, DT_ROWS:DT_ROWS + 16, 0], small[1, A_ROWS:A_ROWS + 8, 0] = a["ssd_a_log"][l], a["gdn_a_log"][l]
        parts = dict(norm1=_cols(a["norm1_g"][l]), conv_ssd=conv(a["ssd_conv_w"][l]), conv_ssd_b=_cols(a["ssd_conv_b"][l]),
                     small_b=small[0], a_log=small[1], ssd_d=_cols(np.repeat(a["ssd_d"][l], 64)), ssd_g=_cols(a["ssd_norm_g"][l]),
                     mla_q_g=_cols(a["mla_q_norm_g"][l]), mla_kv_g=_cols(a["mla_kv_norm_g"][l]), conv_gdn=conv(a["gdn_conv_w"][l]),
                     gdn_g=_cols(a["gdn_norm_g"][l]), norm2=_cols(a["norm2_g"][l]))
        assert list(parts) == list(VEC2)
        return np.concatenate(list(parts.values()), axis=1)
    d["vec2"] = np.stack([vec(l) for l in range(LAYERS)])
    d["final_g"] = _cols(a["final_norm_g"])
    return d


def layout(a):
    import numpy as np
    a = {n: np.asarray(v) for n, v in a.items()}
    d = _layout_first(a)
    d.update(_layout_second(a))
    return {n: np.ascontiguousarray(v) for n, v in d.items()}


def kernel(**inputs):
    import numpy as np
    import concourse.bacc as bacc
    from concourse.bass_utils import run_bass_kernel_spmd

    nc = bacc.Bacc("TRN2", target_bir_lowering=False, num_devices=1)
    arrays = {f"in_{n}": v for n, v in layout(inputs).items()}
    dram = {n[3:]: nc.dram_tensor(n, v.shape, mybir.dt.from_np(v.dtype), kind="ExternalInput").ap()
            for n, v in arrays.items()}
    dram["gates"] = nc.dram_tensor("gates", (PK, PK, T), F32, kind="Internal").ap()
    dram["stream"] = nc.dram_tensor("stream", (P, DC * T), F32, kind="Internal").ap()
    out = nc.dram_tensor("out", (P, DC * T), F32, kind="ExternalOutput").ap()
    program(nc, dram, out)
    result = run_bass_kernel_spmd(nc, [arrays], core_ids=[0]).results[0]["out"]
    return np.ascontiguousarray(np.asarray(result).reshape(P, DC, T).transpose(2, 1, 0)).reshape(1, T, D)
```
